# Optimizing a Trainium2 kernel written in Bass

```python
import jax
import jax.numpy as jnp
from jax import lax
import numpy as np

D_MODEL = 1024
BATCH = 1
SEQ = 512
DEPTH = 2

GRID_W = 64
CTX_LEN = 256
N_EVEN = (DEPTH + 1) // 2
N_ODD = DEPTH // 2
D_FF = 4 * D_MODEL
N_MOD = 6
EPS = 1e-6

ML_DK = 128
ML_DV = 128
ML_HEADS = D_MODEL // (2 * ML_DV)
ML_QK = ML_HEADS * ML_DK
ML_W = ML_HEADS * ML_DV
ML_CHUNK = 128
GATE_CAP = 15.0

AT_DH = 64
AT_HEADS = D_MODEL // (2 * AT_DH)
AT_KV_HEADS = AT_HEADS // 4
AT_GROUP = AT_HEADS // AT_KV_HEADS
AT_W = AT_HEADS * AT_DH
AT_KV_W = AT_KV_HEADS * AT_DH
WINDOW = 128
AT_BLOCK = 128
ROPE_BASE = 10000.0

EV_SIZES = (ML_QK, ML_QK, ML_W, ML_W, 4 * ML_HEADS, AT_W, AT_KV_W, AT_KV_W)
P_EVEN = 2 * ML_QK + 2 * ML_W + 4 * ML_HEADS + AT_W + 2 * AT_KV_W
MIX_W = ML_W + AT_W

RW_HEAD = 64
RW_HEADS = D_MODEL // RW_HEAD
RW_DECAY_LORA = 64
RW_AAA_LORA = 64
RW_GATE_LORA = 160
RW_LN_EPS = 64e-5

kernel_name = 'hybrid_mlstm_swa_rwkv7_dit_trunk'

def split_points():
    pts, acc = [], 0
    for s in EV_SIZES[:-1]:
        acc += s
        pts.append(acc)
    return pts

def rmsnorm(u, g):
    uf = u.astype(jnp.float32)
    y = uf * lax.rsqrt(jnp.mean(uf * uf, axis=-1, keepdims=True) + EPS)
    return (y * g.astype(jnp.float32)).astype(u.dtype)

def softcap(u):
    return GATE_CAP * jnp.tanh(u / GATE_CAP)

def modulate(u, lc, shift_c, scale_c, shift_l, scale_l):
    uc = u[:, :lc] * (1 + scale_c) + shift_c
    ul = u[:, lc:] * (1 + scale_l[:, None]) + shift_l[:, None]
    return jnp.concatenate([uc, ul], axis=1)

def apply_gate(y, lc, gate_c, gate_l):
    return jnp.concatenate([y[:, :lc] * gate_c, y[:, lc:] * gate_l[:, None]], axis=1)

def dir_order(u, lc):
    return jnp.concatenate([jnp.flip(u[:, :lc], axis=1), jnp.flip(u[:, lc:], axis=1)], axis=1)

def seq_order(u, lc, d):
    return u if d == 0 else dir_order(u, lc)

def seg_shift(u, lc, step):
    t = u.shape[1]
    pos = jnp.arange(t)
    if step == 1:
        s = jnp.pad(u, ((0, 0), (1, 0), (0, 0)))[:, :-1]
        border = (pos == 0) | (pos == lc)
    else:
        s = jnp.pad(u, ((0, 0), (0, 1), (0, 0)))[:, 1:]
        border = (pos == lc - 1) | (pos == t - 1)
    return jnp.where(border[None, :, None], jnp.zeros((), u.dtype), s)

def axial_rope(u, rows):
    f32 = jnp.float32
    half = AT_DH // 2
    quarter = half // 2
    inv = ROPE_BASE ** (-jnp.arange(quarter, dtype=f32) / quarter)
    rpos = jnp.repeat(jnp.arange(rows, dtype=f32), GRID_W)
    cpos = jnp.tile(jnp.arange(GRID_W, dtype=f32), rows)

    def rot(xh, pos):
        ang = pos[:, None] * inv[None, :]
        cos = jnp.cos(ang)[None, :, None, :].astype(xh.dtype)
        sin = jnp.sin(ang)[None, :, None, :].astype(xh.dtype)
        x1, x2 = xh[..., :quarter], xh[..., quarter:]
        return jnp.concatenate([x1 * cos - x2 * sin, x1 * sin + x2 * cos], axis=-1)

    return jnp.concatenate([rot(u[..., :half], rpos), rot(u[..., half:], cpos)], axis=-1)

def band_blocks(u):
    b, s = u.shape[0], u.shape[1]
    nb = s // AT_BLOCK
    up = jnp.pad(u, ((0, 0), (AT_BLOCK, AT_BLOCK), (0, 0), (0, 0)))
    up = up.reshape(b, nb + 2, AT_BLOCK, AT_KV_HEADS, AT_DH)
    return jnp.concatenate([up[:, :-2], up[:, 1:-1], up[:, 2:]], axis=2)

def window_attention(q, k, v, lc, rows, q_g, k_g, sink):
    f32 = jnp.float32
    q = rmsnorm(q, q_g)
    k = rmsnorm(k, k_g)
    qc, kc, vc = q[:, :lc], k[:, :lc], v[:, :lc]
    ql = axial_rope(q[:, lc:], rows)
    kl = axial_rope(k[:, lc:], rows)
    vl = v[:, lc:]
    b, s = ql.shape[0], ql.shape[1]
    nb = s // AT_BLOCK
    nk = 3 * AT_BLOCK
    scale = AT_DH ** -0.5
    sink_hg = sink.astype(f32).reshape(1, 1, AT_KV_HEADS, AT_GROUP, 1, 1)
    qlb = ql.reshape(b, nb, AT_BLOCK, AT_KV_HEADS, AT_GROUP, AT_DH)
    kb, vb = band_blocks(kl), band_blocks(vl)
    s_band = jnp.einsum('bnqhgd,bnkhd->bnhgqk', qlb, kb).astype(f32) * scale
    s_ctx = jnp.einsum('bnqhgd,bkhd->bnhgqk', qlb, kc).astype(f32) * scale
    qi = jnp.arange(AT_BLOCK)[:, None]
    ki = jnp.arange(nk)[None, :]
    in_window = jnp.abs(ki - AT_BLOCK - qi) <= WINDOW
    kpos = (jnp.arange(nb)[:, None] - 1) * AT_BLOCK + jnp.arange(nk)[None, :]
    in_range = (kpos >= 0) & (kpos < s)
    valid = in_window[None] & in_range[:, None, :]
    s_band = jnp.where(valid[None, :, None, None], s_band, -jnp.inf)
    sink_l = jnp.broadcast_to(sink_hg, s_band.shape[:-1] + (1,))
    p = jax.nn.softmax(jnp.concatenate([s_band, s_ctx, sink_l], axis=-1), axis=-1)
    ol = (jnp.einsum('bnhgqk,bnkhd->bnqhgd', p[..., :nk].astype(v.dtype), vb)
          + jnp.einsum('bnhgqk,bkhd->bnqhgd', p[..., nk:nk + lc].astype(v.dtype), vc))
    ol = ol.reshape(b, s, AT_W)
    qcg = qc.reshape(b, lc, AT_KV_HEADS, AT_GROUP, AT_DH)
    s_cc = jnp.einsum('bqhgd,bkhd->bhgqk', qcg, kc).astype(f32) * scale
    sink_c = jnp.broadcast_to(sink_hg[0], s_cc.shape[:-1] + (1,))
    pc = jax.nn.softmax(jnp.concatenate([s_cc, sink_c], axis=-1), axis=-1)[..., :lc]
    oc = jnp.einsum('bhgqk,bkhd->bqhgd', pc.astype(v.dtype), vc).reshape(b, lc, AT_W)
    return jnp.concatenate([oc, ol], axis=1)

def mlstm_chunk_scan(q, k, v, ig, lf):
    b, h, t, dk = q.shape
    dv = v.shape[-1]
    L = ML_CHUNK
    nc = t // L

    def chunks(u):
        return jnp.moveaxis(u.reshape(u.shape[:2] + (nc, L) + u.shape[3:]), 2, 0)

    lower = jnp.tril(jnp.ones((L, L), dtype=bool))

    def step(carry, xs):
        C, n, m = carry
        qc, kc, vc, ic, fc = xs
        bcum = jnp.cumsum(fc, axis=-1)
        dlog = bcum[..., :, None] - bcum[..., None, :] + ic[..., None, :]
        dlog = jnp.where(lower, dlog, -jnp.inf)
        inter = bcum + m[..., None]
        mt = jnp.maximum(jnp.max(dlog, axis=-1), inter)
        dw = jnp.exp(dlog - mt[..., None])
        iw = jnp.exp(inter - mt)
        sc = jnp.einsum('bhtk,bhsk->bhts', qc, kc) * dw
        num = (jnp.einsum('bhts,bhsv->bhtv', sc, vc)
               + iw[..., None] * jnp.einsum('bhvk,bhtk->bhtv', C, qc))
        den = jnp.maximum(jnp.abs(jnp.sum(sc, axis=-1) + iw * jnp.einsum('bhk,bhtk->bht', n, qc)),
                          jnp.exp(-mt))
        hout = num / den[..., None]
        bl = bcum[..., -1]
        ws_log = bl[..., None] - bcum + ic
        m_new = jnp.maximum(bl + m, jnp.max(ws_log, axis=-1))
        ws = jnp.exp(ws_log - m_new[..., None])
        carry_decay = jnp.exp(bl + m - m_new)
        C = carry_decay[..., None, None] * C + jnp.einsum('bhsv,bhsk->bhvk', vc * ws[..., None], kc)
        n = carry_decay[..., None] * n + jnp.einsum('bhs,bhsk->bhk', ws, kc)
        return (C, n, m_new), hout

    f32 = jnp.float32
    init = (jnp.zeros((b, h, dv, dk), f32), jnp.zeros((b, h, dk), f32), jnp.zeros((b, h), f32))
    _, hs = lax.scan(step, init, (chunks(q), chunks(k), chunks(v), chunks(ig), chunks(lf)))
    return jnp.moveaxis(hs, 0, 2).reshape(b, h, t, dv)

def mlstm_mixer(q, k, v, o, gates, lc, f_bias, out_g):
    f32 = jnp.float32
    b, t, _ = q.shape
    qh = q.reshape(b, t, ML_HEADS, ML_DK).astype(f32)
    kh = k.reshape(b, t, ML_HEADS, ML_DK).astype(f32) * (ML_DK ** -0.5)
    vh = v.reshape(b, t, ML_HEADS, ML_DV).astype(f32)
    g = gates.reshape(b, t, 2, 2, ML_HEADS).astype(f32)
    ig = softcap(g[:, :, :, 0])
    lf = jax.nn.log_sigmoid(softcap(g[:, :, :, 1] + f_bias.astype(f32)))
    outs = []
    for d in range(2):
        def bhtd(u):
            return jnp.moveaxis(seq_order(u, lc, d), 2, 1)
        hd = mlstm_chunk_scan(bhtd(qh), bhtd(kh), bhtd(vh), bhtd(ig[:, :, d]), bhtd(lf[:, :, d]))
        outs.append(seq_order(jnp.moveaxis(hd, 1, 2), lc, d))
    hsum = rmsnorm(outs[0] + outs[1], out_g.reshape(ML_HEADS, ML_DV))
    return (hsum.reshape(b, t, ML_W) * jax.nn.sigmoid(o.astype(f32))).astype(q.dtype)

def even_mixer(h, lc, rows, w_in, b_in, w_out, f_bias, out_g, q_g, k_g, sink):
    b, t, _ = h.shape
    p = h @ w_in + b_in
    mq, mk, mv, mo, mg, aq, ak, av = jnp.split(p, split_points(), axis=-1)
    ym = mlstm_mixer(mq, mk, mv, mo, mg, lc, f_bias, out_g)
    ya = window_attention(aq.reshape(b, t, AT_HEADS, AT_DH), ak.reshape(b, t, AT_KV_HEADS, AT_DH),
                          av.reshape(b, t, AT_KV_HEADS, AT_DH), lc, rows, q_g, k_g, sink)
    return jnp.concatenate([ym, ya], axis=-1) @ w_out

def rwkv7_scan(r, w, k, v, a, bb):
    b, t, h, n = r.shape

    def step(S, xs):
        rt, wt, kt, vt, at, bt = xs
        S = (S * wt[:, :, None, :]
             + jnp.einsum('bhvk,bhk->bhv', S, at)[..., None] * bt[:, :, None, :]
             + vt[..., None] * kt[:, :, None, :])
        return S, jnp.einsum('bhvk,bhk->bhv', S, rt)

    xs = tuple(jnp.moveaxis(u, 1, 0) for u in (r, w, k, v, a, bb))
    _, y = lax.scan(step, jnp.zeros((b, h, n, n), jnp.float32), xs)
    return jnp.moveaxis(y, 0, 1)

def rwkv7_mixer(u, lc, mu, w_rkv, w0, w1, w2, a0, a1, a2, g1, g2, k_k, k_a, r_k, ln_g, ln_b, w_out):
    f32 = jnp.float32
    b, t, d_model = u.shape
    d_prev = seg_shift(u, lc, 1) - u
    d_next = seg_shift(u, lc, -1) - u
    xr, xw, xk, xv, xa, xg = [u + mu[i, 0] * d_prev + mu[i, 1] * d_next for i in range(6)]
    r = xr @ w_rkv[0]
    k = xk @ w_rkv[1]
    v = xv @ w_rkv[2]
    gate = jax.nn.sigmoid(xg @ g1) @ g2

    def heads(z):
        return z.reshape(b, t, RW_HEADS, RW_HEAD).astype(f32)

    kk = heads(k * k_k)
    kk = kk * lax.rsqrt(jnp.maximum(jnp.sum(kk * kk, axis=-1, keepdims=True), 1e-24))
    rh, vh = heads(r), heads(v)
    outs, bonus = [], []
    for d in range(2):
        w_log = -jax.nn.softplus(-(w0[d] + jnp.tanh(xw @ w1[d]) @ w2[d])) - 0.5
        decay = jnp.exp(-jnp.exp(heads(w_log)))
        a = jax.nn.sigmoid(a0[d] + (xa @ a1[d]) @ a2[d])
        kd = heads(k * (1 + (a - 1) * k_a))
        args = [seq_order(z, lc, d) for z in (rh, decay, kd, vh, -kk, kk * heads(a))]
        outs.append(seq_order(rwkv7_scan(*args), lc, d))
        bonus.append(jnp.sum(rh * kd * r_k.astype(f32), axis=-1, keepdims=True) * vh)
    y = outs[0] + outs[1]
    mean = jnp.mean(y, axis=-1, keepdims=True)
    var = jnp.mean(jnp.square(y - mean), axis=-1, keepdims=True)
    y = ((y - mean) * lax.rsqrt(var + RW_LN_EPS)).reshape(b, t, d_model)
    y = y * ln_g.astype(f32) + ln_b.astype(f32) + (bonus[0] + bonus[1]).reshape(b, t, d_model)
    return (y * gate.astype(f32)).astype(u.dtype) @ w_out

def channel_mixer(h, w1, w2):
    return jnp.square(jax.nn.relu(h @ w1)) @ w2

def setup_inputs(seed: int = 0) -> dict:
    key = jax.random.key(seed)
    ks = iter(jax.random.split(key, 48))
    f32 = jnp.float32
    D = D_MODEL

    def nrm(shape, scale):
        return jax.random.normal(next(ks), shape, f32) * scale

    return {
        'x': nrm((BATCH, SEQ, D), 1.0),
        'c': nrm((BATCH, D), 1.0),
        'ctx': nrm((BATCH, CTX_LEN, D), 1.0),
        'c_ctx': nrm((D,), 1.0),
        'ada_w': nrm((DEPTH, D, N_MOD * D), 0.5 * D ** -0.5),
        'ada_b': nrm((DEPTH, N_MOD * D), 0.02),
        'norm1_g': 1.0 + nrm((DEPTH, D), 0.02),
        'norm2_g': 1.0 + nrm((DEPTH, D), 0.02),
        'mlp_w1': nrm((DEPTH, D, D_FF), D ** -0.5),
        'mlp_w2': nrm((DEPTH, D_FF, D), D_FF ** -0.5),
        'ev_w_in': nrm((N_EVEN, D, P_EVEN), D ** -0.5),
        'ev_b_in': nrm((N_EVEN, P_EVEN), 0.02),
        'ev_w_out': nrm((N_EVEN, MIX_W, D), MIX_W ** -0.5),
        'ml_f_bias': jnp.linspace(3.0, 6.0, ML_HEADS, dtype=f32)[None, None] + nrm((N_EVEN, 2, ML_HEADS), 0.1),
        'ml_out_g': 1.0 + nrm((N_EVEN, ML_W), 0.02),
        'at_q_g': 1.0 + nrm((N_EVEN, AT_DH), 0.02),
        'at_k_g': 1.0 + nrm((N_EVEN, AT_DH), 0.02),
        'at_sink': nrm((N_EVEN, AT_HEADS), 0.5),
        'rw_mu': jax.random.uniform(next(ks), (N_ODD, 6, 2, D), f32, 0.0, 0.5),
        'rw_w_rkv': nrm((N_ODD, 3, D, D), D ** -0.5),
        'rw_w0': jnp.linspace(-6.0, -1.0, D, dtype=f32) + nrm((N_ODD, 2, D), 0.1),
        'rw_w1': nrm((N_ODD, 2, D, RW_DECAY_LORA), D ** -0.5),
        'rw_w2': nrm((N_ODD, 2, RW_DECAY_LORA, D), 0.1 * RW_DECAY_LORA ** -0.5),
        'rw_a0': nrm((N_ODD, 2, D), 0.1),
        'rw_a1': nrm((N_ODD, 2, D, RW_AAA_LORA), D ** -0.5),
        'rw_a2': nrm((N_ODD, 2, RW_AAA_LORA, D), 0.5 * RW_AAA_LORA ** -0.5),
        'rw_g1': nrm((N_ODD, D, RW_GATE_LORA), D ** -0.5),
        'rw_g2': nrm((N_ODD, RW_GATE_LORA, D), RW_GATE_LORA ** -0.5),
        'rw_k_k': 0.85 + nrm((N_ODD, D), 0.02),
        'rw_k_a': 1.0 + nrm((N_ODD, D), 0.02),
        'rw_r_k': nrm((N_ODD, RW_HEADS, RW_HEAD), 0.1),
        'rw_ln_g': 1.0 + nrm((N_ODD, D), 0.02),
        'rw_ln_b': nrm((N_ODD, D), 0.02),
        'rw_w_out': nrm((N_ODD, D, D), D ** -0.5),
    }

def reference(x, c, ctx, c_ctx, ada_w, ada_b, norm1_g, norm2_g, mlp_w1, mlp_w2,
              ev_w_in, ev_b_in, ev_w_out, ml_f_bias, ml_out_g, at_q_g, at_k_g, at_sink,
              rw_mu, rw_w_rkv, rw_w0, rw_w1, rw_w2, rw_a0, rw_a1, rw_a2, rw_g1, rw_g2,
              rw_k_k, rw_k_a, rw_r_k, rw_ln_g, rw_ln_b, rw_w_out):
    b, s, d_model = x.shape
    lc = ctx.shape[1]
    rows = s // GRID_W
    z = jnp.concatenate([ctx, x], axis=1)
    s_lat = jax.nn.silu(c)
    s_ctx = jax.nn.silu(c_ctx)
    for layer in range(DEPTH):
        mod_l = (s_lat @ ada_w[layer] + ada_b[layer]).reshape(b, N_MOD, d_model)
        mod_c = (s_ctx @ ada_w[layer] + ada_b[layer]).reshape(N_MOD, d_model)
        h = modulate(rmsnorm(z, norm1_g[layer]), lc, mod_c[0], mod_c[1], mod_l[:, 0], mod_l[:, 1])
        j = layer // 2
        if layer % 2 == 0:
            y = even_mixer(h, lc, rows, ev_w_in[j], ev_b_in[j], ev_w_out[j], ml_f_bias[j], ml_out_g[j],
                           at_q_g[j], at_k_g[j], at_sink[j])
        else:
            y = rwkv7_mixer(h, lc, rw_mu[j], rw_w_rkv[j], rw_w0[j], rw_w1[j], rw_w2[j], rw_a0[j],
                            rw_a1[j], rw_a2[j], rw_g1[j], rw_g2[j], rw_k_k[j], rw_k_a[j], rw_r_k[j],
                            rw_ln_g[j], rw_ln_b[j], rw_w_out[j])
        z = z + apply_gate(y, lc, mod_c[2], mod_l[:, 2])
        if layer == DEPTH - 1:
            z = z[:, lc:]
            lc = 0
        h = modulate(rmsnorm(z, norm2_g[layer]), lc, mod_c[3], mod_c[4], mod_l[:, 3], mod_l[:, 4])
        z = z + apply_gate(channel_mixer(h, mlp_w1[layer], mlp_w2[layer]), lc, mod_c[5], mod_l[:, 5])
    return z


_drawn_inputs = setup_inputs


def setup_inputs(seed=0):
    import zlib

    import numpy as np

    out = dict(_drawn_inputs(seed))
    spreads = {}
    factors = {'norm1_g': 6.459,
     'norm2_g': 4.418,
     'ev_b_in': 4.345,
     'ml_out_g': 8.0,
     'at_q_g': 8.0,
     'at_k_g': 8.0,
     'at_sink': 8.0,
     'rw_w1': 64.0,
     'rw_w2': 64.0,
     'rw_a0': 8.0,
     'rw_k_k': 40.632,
     'rw_k_a': 6.178,
     'rw_ln_g': 64.0,
     'rw_ln_b': 64.0,
     'rw_w0': 6.366}
    for name, (base, spread) in spreads.items():
        noise = np.random.default_rng([zlib.crc32(name.encode()), seed]).standard_normal(out[name].shape)
        drawn = base * np.exp(spread * noise) if base else spread * noise
        out[name] = jnp.asarray(drawn.astype(out[name].dtype))
    for name, factor in factors.items():
        out[name] = (out[name] * factor).astype(out[name].dtype)
    return out
```

```python
from contextlib import ExitStack

import numpy as np

import concourse.bass as bass
from concourse import mybir

F32 = mybir.dt.float32
F32R = mybir.dt.float32r
U32 = mybir.dt.uint32
ALU = mybir.AluOpType
ACT = mybir.ActivationFunctionType
AX = mybir.AxisListType

P = 128
D = 1024
KT = D // P
LC = 256
LAT = 512
T = LC + LAT
EPS = 1e-6
LN_EPS = 64e-5
CAP = 15.0
NEG = -1e30
KAPPA = float(np.exp(-0.5))
L = 64
SEGS = ((0, LC), (LC, LAT))
CTX, LATS = SEGS

N_IN = 23
T_IN = 0
T_OUT0 = T_IN + N_IN
T_MLP0 = T_OUT0 + 8
T_V = T_MLP0 + 64
T_K = T_V + 8
T_W = T_K + 8
T_A = T_W + 1
T_R = T_A + 1
T_G = T_R + 8
T_OUT1 = T_G + 2
T_MLP1 = T_OUT1 + 8
NT = T_MLP1 + 64


def offsets(table):
    at, n = {}, 0
    for name, width in table:
        at[name] = n
        n += width
    return at, n


VOFF, NV = offsets([("c", 16), ("ada_b", 96), ("g1", 16), ("g2", 16), ("b_in", N_IN), ("fb", 1),
                    ("out_g", 4), ("q_g", 1), ("k_g", 1), ("sink", 8), ("mu", 96), ("w0", 16),
                    ("a0", 16), ("k_k", 8), ("k_a", 8), ("r_k", 8), ("ln_g", 8), ("ln_b", 8)])
COFF, NC = offsets([("ident", 128), ("ones", 128), ("bd", 128)])
C0OFF, NC0 = offsets([("perm", 128), ("neg", 256), ("cos", 512), ("sin", 512), ("sel", 1024),
                      ("reset", 768)])
C1OFF, NC1 = offsets([("mstrict", 128), ("mincl", 128), ("lvl", 768), ("eye", 64),
                      ("reset", 512), ("hsel", 128), ("hbc", 1024)])


def trunk(nc, zin, wall, ada, pv, cm, cm0, cm1, lora2, g2w, out, z_dram, vt_dram, vk_dram,
          y_dram):
    ctx = ExitStack()
    with ctx:
        BASE = 16512

        def at(name, kb, shape, dt=F32):
            return nc.alloc_sbuf_tensor_at(name, shape, dt, offset=BASE + int(kb * 1024))

        def sem(name):
            return ctx.enter_context(nc.semaphore(name))

        z = at("z", 0, [P, KT, T])
        WR = at("WR", 24, [P, 2, KT, P])
        WH = at("WH", 32, [P, 2, KT, P], F32R)
        WL = at("WL", 40, [P, 2, KT, P], F32R)
        PV = at("PV", 48, [P, NV])
        MOD = at("MOD", 50, [P, 2, 48, 2])
        CO = at("CO", 50.75, [P, 80])
        CM = at("CM", 51.125, [P, NC])
        CM1 = at("CM1", 53, [P, NC1 - D])
        RA = 62
        RB = RA + 48
        XH = at("XH", RA, [P, KT, T], F32R)
        XL = at("XL", RA + 24, [P, KT, T], F32R)
        ps = ctx.enter_context(nc.psum_tensor("ps", [P, 8, 512], F32))
        ADA = at("ADA", RA, [P, 8, KT, P])
        SC = at("SC", RA + 40, [P, 64])
        NS = [{k: at(f"{k}{i}", o + b, s) for k, b, s in (
            ("SQ", 0, [P, 2, T]), ("ACC", 6, [P, T]), ("STD", 9, [P, T]), ("RS", 12, [P, T]),
            ("TM", 15, [P, 2, T]), ("HF", 21, [P, 2, T]))}
            for i, o in enumerate((RB, RB + 60, RB + 25))]
        Q = at("Q", RB, [P, N_IN, T])
        H = at("H", RB + 69, [P, 4, T])
        CM0 = at("CM0", RB + 81, [P, NC0])
        N5 = at("N5", RA, [64, 5, T])
        R5 = at("R5", RA + 15, [64, 5, T])
        BC = at("BC", RA + 30, [64, T])
        GM = at("GM", RA + 33, [64, T])
        IG = at("IG", RA + 36, [64, T])
        LF = at("LF", RA + 39, [64, T])
        GX = at("GX", RA + 42, [P, T])
        GF = at("GF", RA + 45, [64, T])
        MM = at("MM", 52.75, [64, 8])
        KVT = at("KVT", RA + 15, [P, 8, P])
        KVK = at("KVK", RA + 19, [P, 8, P])
        EE = at("EE", RA + 23, [P, 4, P])
        IW = at("IW", RA + 25, [P, 4, P])
        FL = at("FL", RA + 27, [P, 4, P])
        WM = at("WM", RA + 29, [P, 4, P])
        QT = at("QT", RA + 31, [P, 4, P])
        VW = at("VW", RA + 33, [P, 4, P + 1])
        YM = at("YM", RA + 35.25, [P, 4, P])
        CT = at("CT", RA + 37.25, [P, 2, 4, P + 1])
        NR = at("NR", RA + 41.5, [P, 4, P])
        CS = at("CS", RA + 43.5, [P, 6, 64])
        CW = at("CW", RA + 45, [P, 6, 64])

        def vec(name, j=0, n=1):
            return PV[:, VOFF[name] + j:VOFF[name] + j + n]

        def vecd(name, j):
            return PV[:, bass.ds(j + VOFF[name], 1)]

        def cmat(name, n=128):
            return CM[:, COFF[name]:COFF[name] + n]

        def c0(name, a, n):
            return CM0[:, C0OFF[name] + a:C0OFF[name] + a + n]

        def c1(name, a, n):
            return CM1[:, C1OFF[name] + a:C1OFF[name] + a + n]

        ident, ones, bd = cmat("ident"), cmat("ones"), cmat("bd")

        consts_in = sem("consts_in")
        cm0_in = sem("cm0_in")
        ada_in = [sem(f"ada_in{j}") for j in range(8)]
        silu = sem("silu")
        ada_done = sem("ada_done")
        mod_ready = sem("mod_ready")
        w_in = [sem("w_in0"), sem("w_in1")]
        w_hi, w_lo, tile_done = sem("w_hi"), sem("w_lo"), sem("tile_done")
        acc_lat, acc_ctx = sem("acc_lat"), sem("acc_ctx")
        n_sq, n_acc, n_stat, n_std = sem("n_sq"), sem("n_acc"), sem("n_stat"), sem("n_std")
        n_tm, n_h = sem("n_tm"), sem("n_h")
        x_hi, x_lo = sem("x_hi"), sem("x_lo")
        hid_sq, hid_hi, hid_lo = sem("hid_sq"), sem("hid_hi"), sem("hid_lo")
        out_done = sem("out_done")
        X_COUNT = {"norm0": 0}

        def seg(x, s):
            return x[s[0]:s[0] + s[1]]

        def tile_loop(eng, t0, n, body, peel=0):
            for m in range(min(peel, n)):
                body(t0 + m, (t0 + m) // 2, m, (t0 + m) % 2)
            pairs = (n - peel) // 2
            if pairs > 1:
                with eng.Fori(0, pairs) as i:
                    for j in range(2):
                        b = t0 + peel + j
                        body(i * 2 + b, i + b // 2, i * 2 + (peel + j), b % 2)
            else:
                pairs = 0
            for m in range(peel + 2 * pairs, n):
                body(t0 + m, (t0 + m) // 2, m, (t0 + m) % 2)

        def load_weights(sp):
            for t in range(2):
                sp.dma_start(WR[:, t], wall[t]).then_inc(w_in[t % 2], 16)

            def body(t, half, m, s):
                sp.wait_ge(w_hi, t - 1)
                sp.wait_ge(w_lo, t - 1)
                sp.dma_start(WR[:, s], wall[bass.ds(t, 1)].rearrange("a p k m -> (a p) k m")
                             ).then_inc(w_in[s], 16)
            tile_loop(sp, 2, NT - 2, body)

        def split_hi(t, half, s, first=False):
            nc.scalar.wait_ge(w_in[s], (half + 1) * 16)
            nc.scalar.activation(WH[:, s], WR[:, s], ACT.Copy).then_inc(w_hi, 1)

        def split_lo(t, half, s):
            nc.vector.wait_ge(w_in[s], (half + 1) * 16)
            nc.vector.wait_ge(w_hi, t + 1)
            nc.vector.tensor_tensor(WL[:, s], WR[:, s], WH[:, s].bitcast(F32),
                                    ALU.subtract).then_inc(w_lo, 1)

        def gemm_pe(pe, t0, n, segs, c_before, xh, xl, x_wait=None, last_wait=None):
            def body(t, half, m, s):
                if x_wait is not None:
                    pe.wait_ge(*x_wait)
                pe.wait_ge(w_hi, t + 1)
                pe.wait_ge(w_lo, t + 1)
                if not isinstance(t, int) or t >= 2:
                    pe.wait_ge(acc_lat, t - 1)
                if CTX in segs:
                    cc = c_before + m - 1
                    if not isinstance(cc, int) or cc >= 1:
                        pe.wait_ge(acc_ctx, cc)
                for k in range(KT):
                    if k == KT - 1 and last_wait is not None:
                        pe.wait_ge(*last_wait)
                    for a, b, first in ((WH, xh, True), (WH, xl, False), (WL, xh, False)):
                        for sg in segs:
                            bank = 2 * s + (0 if sg is LATS else 1)
                            mm = nc.tensor.matmul(
                                ps[:, bank, 0:sg[1]], a[:, s, k], b[:, k, sg[0]:sg[0] + sg[1]],
                                start=(k == 0 and first), stop=(k == KT - 1 and a is WL))
                mm.then_inc(tile_done, 1)
            tile_loop(pe, t0, n, body, peel=2 if t0 == 0 else 0)

        def acc(s, sg):
            return ps[:, 2 * s + (0 if sg is LATS else 1), 0:sg[1]]

        def step_act(act, t0, n, evict, peel=0):
            def body(t, half, m, s):
                act.wait_ge(tile_done, t + 1)
                if evict is not None:
                    evict(t, m, s)
                if not isinstance(t, int) or t + 2 < NT:
                    split_hi(t + 2, half + 1, s)
            lim = max(0, min(n, NT - 2 - t0))
            tile_loop(act, t0, lim, body, peel)
            for m in range(lim, n):
                body(t0 + m, (t0 + m) // 2, m, (t0 + m) % 2)

        def step_dve(dve, t0, n, evict, peel=0):
            def body(t, half, m, s):
                dve.wait_ge(tile_done, t + 1)
                if evict is not None:
                    evict(t, m, s)
                if not isinstance(t, int) or t + 2 < NT:
                    split_lo(t + 2, half + 1, s)
            lim = max(0, min(n, NT - 2 - t0))
            tile_loop(dve, t0, lim, body, peel)
            for m in range(lim, n):
                body(t0 + m, (t0 + m) // 2, m, (t0 + m) % 2)


        def ada_sync(sp):
            for turn in range(1):
                for j in range(8):
                    sp.dma_start(ADA[:, j], ada[j]).then_inc(ada_in[j], 16)
            with sp.Fori(1, 12) as i:
                for j in range(8):
                    sp.wait_ge(ada_done, i * 8 + (j - 7))
                    sp.dma_start(ADA[:, j], ada[bass.ds(i * 8 + j, 1)].rearrange(
                        "a p k m -> (a p) k m")).then_inc(ada_in[j], 16)

        def ada_pe(pe):
            pe.wait_ge(silu, 3)
            with pe.Fori(0, 12) as i:
                for j in range(8):
                    pe.wait_ge(ada_in[j], i * 16 + 16)
                    for k in range(KT):
                        mm = nc.tensor.matmul(ps[:, 7, bass.ds(i * 16 + 2 * j, 2)], ADA[:, j, k],
                                              SC[:, 16 + 2 * k:18 + 2 * k], start=(k == 0),
                                              stop=(k == KT - 1))
                    mm.then_inc(ada_done, 1)

        def ada_act(act):
            act.wait_ge(consts_in, 32)
            nc.scalar.activation(SC[:, 0:16], vec("c", 0, 16), ACT.Tanh, scale=0.5
                                 ).then_inc(silu, 1)

        def ada_dve(dve):
            dve.wait_ge(consts_in, 32)
            dve.wait_ge(silu, 1)
            nc.vector.tensor_scalar(SC[:, 32:48], SC[:, 0:16], 0.5, 0.5, ALU.mult, ALU.add
                                    ).then_inc(silu, 1)
            dve.wait_ge(silu, 2)
            nc.vector.tensor_tensor(SC[:, 16:32], SC[:, 32:48], vec("c", 0, 16), ALU.mult
                                    ).then_inc(silu, 1)
            dve.wait_ge(ada_done, 96)
            nc.vector.tensor_tensor(
                MOD[:], ps[:, 7, 0:192].rearrange("p (l m c) -> p l m c", l=2, c=2),
                vec("ada_b", 0, 96).rearrange("p (l m) -> p l m", l=2)[:, :, :, None
                                                                        ].broadcast_to([P, 2, 48, 2]),
                ALU.add).then_inc(mod_ready, 1)
            dve.wait_ge(mod_ready, 1)
            for n in range(4):
                sc = MOD[:, n // 2, 8 + 24 * (n % 2):16 + 24 * (n % 2), :]
                g = vec("g1" if n % 2 == 0 else "g2", 8 * (n // 2), 8)
                nc.vector.scalar_tensor_tensor(
                    out=CO[:, 16 * n:16 * n + 16].rearrange("p (k c) -> p k c", c=2), in0=sc,
                    scalar=1.0, in1=g[:, :, None].broadcast_to([P, 8, 2]), op0=ALU.add,
                    op1=ALU.mult).then_inc(mod_ready, 1)
            nc.vector.memset(CO[:, 64:65], EPS).then_inc(mod_ready, 1)
            nc.vector.memset(CO[:, 65:66], LN_EPS).then_inc(mod_ready, 1)
            nc.vector.memset(CO[:, 66:67], 1.0).then_inc(mod_ready, 1)

        def norm_pe(pe, n, segs):
            pe.wait_ge(n_acc, 8 * n + 8)
            for sg in segs:
                mm = nc.tensor.matmul(ps[:, 6 if sg is LATS else 7, 0:sg[1]], ones,
                                      NS[NSI[n]]["ACC"][:, sg[0]:sg[0] + sg[1]], start=True,
                                      stop=True)
            mm.then_inc(n_stat, 1)

        NSI = {0: 0, 1: 1, 2: 2, 3: 1}
        ZA = {0: 0, 1: 0, 2: 0, 3: LC}

        def norm_act(act, n, segs, z_wait, split):
            B = NS[NSI[n]]
            a = ZA[n]
            for w in z_wait:
                act.wait_ge(*w)
            for k in range(KT):
                if k >= 2:
                    act.wait_ge(n_acc, 8 * n + k - 1)
                nc.scalar.activation(B["SQ"][:, k % 2, a:T], z[:, k, a:T], ACT.Square
                                     ).then_inc(n_sq, 1)
            act.wait_ge(n_stat, n + 1)
            act.wait_ge(mod_ready, 8)
            for sg in segs:
                nc.scalar.activation(B["STD"][:, sg[0]:sg[0] + sg[1]],
                                     ps[:, 6 if sg is LATS else 7, 0:sg[1]], ACT.Sqrt,
                                     bias=CO[:, 64:65], scale=1.0 / D).then_inc(n_std, 1)
            if split:
                for k in range(KT):
                    act.wait_ge(n_h, 8 * n + k + 1)
                    nc.scalar.activation(XH[:, k, a:T], B["HF"][:, k % 2, a:T], ACT.Copy
                                         ).then_inc(x_hi, 1)

        def norm_dve(dve, n, segs, z_wait, x0, split):
            B = NS[NSI[n]]
            a = ZA[n]
            for w in z_wait:
                dve.wait_ge(*w)
            if not split:
                for c in (1, 258, 259, T + 4):
                    nc.vector.memset(U[:, :, c:c + 1], 0.0)
            for k in range(KT):
                dve.wait_ge(n_sq, 8 * n + k + 1)
                if k == 0:
                    nc.vector.tensor_copy(B["ACC"][:, a:T], B["SQ"][:, 0, a:T]).then_inc(n_acc, 1)
                else:
                    dve.wait_ge(n_acc, 8 * n + k)
                    nc.vector.tensor_tensor(B["ACC"][:, a:T], B["ACC"][:, a:T],
                                            B["SQ"][:, k % 2, a:T], ALU.add).then_inc(n_acc, 1)
            dve.wait_ge(n_std, NSTD[n] + len(segs))
            nc.vector.reciprocal(B["RS"][:, a:T], B["STD"][:, a:T]).then_inc(n_tm, 1)
            dve.wait_ge(n_tm, 9 * n + 1)
            sh = 24 * (n % 2)
            for k in range(KT):
                if k >= 2:
                    dve.wait_ge(n_h, 8 * n + k - 1)
                nc.vector.tensor_tensor(B["TM"][:, k % 2, a:T], z[:, k, a:T], B["RS"][:, a:T],
                                        ALU.mult).then_inc(n_tm, 1)
                dve.wait_ge(n_tm, 9 * n + k + 2)
                if split and k >= 2:
                    dve.wait_ge(x_hi, x0 + k - 1)
                    dve.wait_ge(x_lo, x0 + k - 1)
                for i, sg in enumerate(segs):
                    v = SEGS.index(sg)
                    if split:
                        o = B["HF"][:, k % 2, sg[0]:sg[0] + sg[1]]
                    else:
                        o = U[:, k, 2 + 2 * v + sg[0]:2 + 2 * v + sg[0] + sg[1]]
                    ins = nc.vector.tensor_scalar(
                        o, B["TM"][:, k % 2, sg[0]:sg[0] + sg[1]],
                        CO[:, 16 * n + 2 * k + v:16 * n + 2 * k + v + 1],
                        MOD[:, n // 2, sh + k, v:v + 1], ALU.mult, ALU.add)
                ins.then_inc(n_h, 1)
                if split:
                    dve.wait_ge(n_h, 8 * n + k + 1)
                    dve.wait_ge(x_hi, x0 + k + 1)
                    nc.vector.tensor_tensor(XL[:, k, a:T], B["HF"][:, k % 2, a:T],
                                            XH[:, k, a:T].bitcast(F32), ALU.subtract
                                            ).then_inc(x_lo, 1)

        NSTD = {0: 0, 1: 2, 2: 4, 3: 6}
        U = at("U", RB, [P, KT, T + 6])

        def in_act(t, m, s):
            nc.scalar.activation(q_lat(m), acc(s, LATS), ACT.Identity,
                                 bias=vecd("b_in", m)).then_inc(acc_lat, 1)

        def in_dve(t, m, s):
            nc.vector.tensor_scalar(q_ctx(m), acc(s, CTX), vecd("b_in", m), None, ALU.add
                                    ).then_inc(acc_ctx, 1)

        def q_lat(m):
            return Q[:, bass.ds(m, 1), LC:T]

        def q_ctx(m):
            return Q[:, bass.ds(m, 1), 0:LC]

        def res_dve(layer, gate, segs):
            def evict(t, m, s):
                nc.vector.wait_ge(acc_lat, t)
                for sg in segs:
                    v = SEGS.index(sg)
                    zz = z[:, bass.ds(m, 1), sg[0]:sg[0] + sg[1]].rearrange("p a t -> p (a t)")
                    nc.vector.scalar_tensor_tensor(
                        out=zz, in0=acc(s, sg),
                        scalar=MOD[:, layer, bass.ds(m + 8 * gate, 1), v:v + 1].rearrange(
                            "p a b -> p (a b)"), in1=zz, op0=ALU.mult, op1=ALU.add
                        ).then_inc(acc_lat if sg is LATS else acc_ctx, 1)
            return evict

        HH = at("HH", RB, [P, KT, T], F32R)
        HL = at("HL", RB + 24, [P, KT, T], F32R)
        HR = at("HR", RB + 48, [P, 2, T])
        HS_ = at("HS_", RB + 54, [P, 2, T])

        def mlp(eng, which, layer, t0, segs, c0_, x_ready):
            a = 0 if CTX in segs else LC

            def up_act(hb):
                def evict(t, m, s):
                    n = m + hb
                    if not isinstance(n, int) or n >= 2:
                        nc.scalar.wait_ge(hid_sq, n - 1)
                    if CTX in segs:
                        nc.scalar.activation(HR[:, s, 0:LC], acc(s, CTX), ACT.Relu
                                             ).then_inc(acc_ctx, 1)
                    nc.scalar.activation(HR[:, s, LC:T], acc(s, LATS), ACT.Relu
                                         ).then_inc(acc_lat, 1)
                    nc.scalar.wait_ge(hid_sq, n + 1)
                    nc.scalar.activation(hh(HH, m), HS_[:, s, a:T], ACT.Copy
                                         ).then_inc(hid_hi, 1)
                return evict

            def up_dve(hb):
                def evict(t, m, s):
                    n = m + hb
                    nc.vector.wait_ge(acc_lat, t + 1)
                    if not isinstance(n, int) or n >= 2:
                        nc.vector.wait_ge(hid_hi, n - 1)
                        nc.vector.wait_ge(hid_lo, n - 1)
                    nc.vector.tensor_tensor(HS_[:, s, a:T], HR[:, s, a:T], HR[:, s, a:T],
                                            ALU.mult).then_inc(hid_sq, 1)
                    nc.vector.wait_ge(hid_hi, n + 1)
                    nc.vector.tensor_tensor(hh(HL, m), HS_[:, s, a:T], hh(HH, m).bitcast(F32),
                                            ALU.subtract).then_inc(hid_lo, 1)
                return evict

            def hh(x, m):
                return x[:, bass.ds(m, 1), a:T].rearrange("p a t -> p (a t)")

            for g in range(4):
                hb = 32 * layer + 8 * g + 2 * 0
                tu, td = t0 + 16 * g, t0 + 16 * g + 8
                cu = c0_ + 16 * g
                if which == "pe":
                    gemm_pe(eng, tu, 8, segs, cu, XH, XL, x_wait=x_ready)
                    gemm_pe(eng, td, 8, segs, cu + 8, HH, HL, x_wait=(hid_lo, hb + 7),
                            last_wait=(hid_lo, hb + 8))
                elif which == "act":
                    step_act(eng, tu, 8, up_act(hb), peel=2 if hb == 0 else 0)
                    step_act(eng, td, 8, None)
                else:
                    step_dve(eng, tu, 8, up_dve(hb), peel=2 if hb == 0 else 0)
                    step_dve(eng, td, 8, res_dve(layer, 5, segs))

        ml_gx, ml_gf, ml_sc, ml_g, ml_nat = (sem("ml_gx"), sem("ml_gf"), sem("ml_sc"),
                                             sem("ml_g"), sem("ml_nat"))
        ml_colp, ml_col = sem("ml_colp"), sem("ml_col")
        ml_kvt, ml_tr, ml_kvk = sem("ml_kvt"), sem("ml_tr"), sem("ml_kvk")
        ml_bc, ml_exp, ml_w, ml_vw = sem("ml_bc"), sem("ml_exp"), sem("ml_w"), sem("ml_vw")
        ml_num, ml_cn, ml_y, ml_ct, ml_nr = (sem("ml_num"), sem("ml_cn"), sem("ml_y"),
                                             sem("ml_ct"), sem("ml_nr"))
        ml_init = sem("ml_init")
        fin_sq, fin_st, fin_sd, fin_o, fin_y, fin_hi = (sem("fin_sq"), sem("fin_st"),
                                                        sem("fin_sd"), sem("fin_o"),
                                                        sem("fin_y"), sem("fin_hi"))
        fin_lo = sem("fin_lo")
        ORDER = [(0, 2, 1), (2, 6, 7)]

        def ml_gates_act(act):
            act.wait_ge(acc_lat, N_IN)
            act.wait_ge(acc_ctx, N_IN)
            act.wait_ge(ml_sc, 1)
            nc.scalar.activation(GX[:], Q[:, 16], ACT.Tanh, bias=CO[:, 67:68], scale=1.0 / CAP
                                 ).then_inc(ml_gx, 1)
            act.wait_ge(ml_gx, 1)
            act.wait_ge(cm0_in, 16)
            act.dma_start(GF[:], GX[64:128]).then_inc(ml_gf, 16)
            act.wait_ge(ml_gf, 16)
            nc.scalar.activation(GM[:], GF[:], ACT.Exp, scale=-CAP).then_inc(ml_gx, 1)
            act.wait_ge(ml_gx, 2)
            nc.scalar.activation(BC[:], GM[:], ACT.Ln, bias=CO[0:64, 66:67]).then_inc(ml_gx, 1)
            act.wait_ge(ml_colp, 12)
            pcol = ps[:, 6:8].rearrange("p a b -> p (a b)")
            nc.scalar.activation(CW[:], pcol[:, 384:768].rearrange("p (c r) -> p c r", c=6),
                                 ACT.Exp).then_inc(ml_col, 1)
            nc.scalar.activation(CS[:], pcol[:, 0:384].rearrange("p (c r) -> p c r", c=6),
                                 ACT.Copy).then_inc(ml_col, 1)

        def ml_gates_dve(dve):
            nc.vector.tensor_scalar(CO[:, 67:68], vec("fb"), 1.0 / CAP, None, ALU.mult
                                    ).then_inc(ml_sc, 1)
            dve.wait_ge(ml_gx, 3)
            nc.vector.tensor_scalar(IG[0:32], GX[0:32], CAP, None, ALU.mult).then_inc(ml_sc, 1)
            nc.vector.tensor_scalar(LF[0:32], BC[0:32], -1.0, None, ALU.mult).then_inc(ml_sc, 1)
            for sg in SEGS:
                a, b = sg[0], sg[0] + sg[1]
                nc.vector.tensor_scalar(IG[32:64, a:b], GX[32:64, a:b][:, ::-1], CAP, None,
                                        ALU.mult).then_inc(ml_sc, 1)
                nc.vector.tensor_scalar(LF[32:64, a:b], BC[32:64, a:b][:, ::-1], -1.0, None,
                                        ALU.mult).then_inc(ml_sc, 1)
            dve.wait_ge(ml_sc, 7)
            dve.wait_ge(cm0_in, 16)
            nc.vector.tensor_tensor_scan(BC[:], c0("reset", 0, T)[0:64], LF[:], 0.0, ALU.mult,
                                         ALU.add).then_inc(ml_g, 1)
            nc.vector.memset(MM[:, 0:1], 0.0).then_inc(ml_g, 1)
            dve.wait_ge(ml_g, 2)
            nc.vector.tensor_tensor(R5[:, 3], IG[:], BC[:], ALU.subtract).then_inc(ml_g, 1)
            dve.wait_ge(ml_g, 3)
            for c in range(6):
                a, b = 128 * c, 128 * c + 128
                nc.vector.tensor_tensor_scan(GM[:, a:b], R5[:, 3, a:b], R5[:, 3, a:b],
                                             MM[:, c:c + 1], ALU.max, ALU.max).then_inc(ml_g, 1)
                dve.wait_ge(ml_g, 4 + 2 * c)
                nc.vector.tensor_tensor(MM[:, c + 1:c + 2], BC[:, b - 1:b], GM[:, b - 1:b],
                                        ALU.add).then_inc(ml_g, 1)
                dve.wait_ge(ml_g, 5 + 2 * c)
            nc.vector.tensor_scalar(R5[:, 0], GM[:], -1.0, None, ALU.mult).then_inc(ml_g, 1)
            nc.vector.scalar_tensor_tensor(out=R5[:, 2], in0=BC[:], scalar=-1.0, in1=GM[:],
                                           op0=ALU.mult, op1=ALU.subtract).then_inc(ml_g, 1)
            for c in range(6):
                a, b = 128 * c, 128 * c + 128
                nc.vector.tensor_scalar(R5[:, 1, a:b], GM[:, a:b], -1.0, MM[:, c:c + 1],
                                        ALU.mult, ALU.add).then_inc(ml_g, 1)
                nc.vector.tensor_scalar(R5[:, 4, a:b], R5[:, 3, a:b], GM[:, b - 1:b], None,
                                        ALU.subtract).then_inc(ml_g, 1)
            dve.wait_ge(ml_g, 29)
            nc.vector.tensor_copy(N5[0:32], R5[0:32]).then_inc(ml_nat, 1)
            for sg in SEGS:
                a, b = sg[0], sg[0] + sg[1]
                nc.vector.tensor_copy(N5[32:64, :, a:b], R5[32:64, :, a:b][:, :, ::-1]
                                      ).then_inc(ml_nat, 1)
            nc.vector.tensor_scalar(Q[:, 0:4], Q[:, 0:4], float(P) ** -0.5, None, ALU.mult
                                    ).then_inc(ml_init, 1)
            nc.vector.memset(H[:], 0.0).then_inc(ml_init, 1)
            dve.wait_ge(ml_nat, 3)
            nc.vector.memset(CT[:], 0.0).then_inc(ml_init, 1)

        def ml_gates_pe(pe):
            pe.wait_ge(ml_nat, 3)
            pcol = ps[:, 6:8].rearrange("p a b -> p (a b)")
            for r in range(2):
                for c in range(6):
                    o = 384 * r + 64 * c
                    nc.tensor.transpose(pcol[:, o:o + 64], N5[:, 3 + r, 128 * c:128 * c + 128],
                                        ident[0:64, 0:64]).then_inc(ml_colp, 1)

        def chunks(eng, body):
            for lo, hi, flip in ORDER:
                with eng.Fori(0, hi - lo) as i:
                    for d in range(2):
                        c = eng.snap(i + lo if d == 0 else i * -1 + (flip - lo))
                        body(i * 2 + (2 * lo + d), d, c, eng.snap(c * P))

        def ml_pe(pe):
            pe.wait_ge(ml_col, 2)
            pe.wait_ge(ml_init, 4)

            def body(u, d, c, off):
                tok = bass.ds(off, P)
                pe.wait_ge(ml_kvt, u + 1)
                pe.wait_ge(ml_ct, u * 4)
                for j in range(8):
                    mm = nc.tensor.transpose(ps[:, j // 4, P * (j % 4):P * (j % 4) + P],
                                             KVT[:, j], ident)
                mm.then_inc(ml_tr, 1)
                pe.wait_ge(ml_w, u)
                pe.wait_ge(ml_exp, u * 6)
                for h in range(4):
                    nc.tensor.matmul(ps[:, 5, P * h:P * h + P], KVT[:, h], Q[:, h, tok],
                                     start=True, stop=True)
                for r, bank in ((0, 2), (1, 3), (2, 4)):
                    for h in range(4):
                        o = ps[:, bank, P * h:P * h + P]
                        mm = nc.tensor.matmul(
                            o, c0("sel", P * (4 * d + h), P)[0:64], N5[:, r, tok], start=True,
                            stop=(r != 0))
                        if r == 0:
                            nc.tensor.matmul(o, ident, c0("neg", P * d, P), start=False,
                                             stop=True)
                mm.then_inc(ml_bc, 1)
                pe.wait_ge(ml_kvk, u + 1)
                pe.wait_ge(ml_vw, u + 1)
                pe.wait_ge(ml_y, u)
                for h in range(4):
                    o = ps[:, 6, P * h:P * h + P]
                    nc.tensor.matmul(o, KVK[:, 4 + h], WM[:, h], start=True, stop=False)
                    nc.tensor.matmul(o, CT[:, d, h, 0:P], QT[:, h], start=False, stop=True)
                nc.tensor.matmul(ps[:, 7, :], ones, WM[:].rearrange("p h t -> p (h t)"),
                                 start=True, stop=False)
                pe.wait_ge(ml_nr, u + 1)
                for h in range(4):
                    mm = nc.tensor.matmul(ps[:, 7, P * h:P * h + P], NR[:, h], QT[:, h],
                                          start=False, stop=(h == 3))
                mm.then_inc(ml_num, 1)
                for h in range(4):
                    mm = nc.tensor.matmul(ps[:, h // 2, (P + 1) * (h % 2):(P + 1) * (h % 2) + P + 1],
                                          KVK[:, h], VW[:, h], start=True, stop=True)
                mm.then_inc(ml_cn, 1)
            chunks(pe, body)

        def ml_act(act):
            act.wait_ge(ml_init, 4)

            def body(u, d, c, off):
                act.wait_ge(ml_num, u)
                nc.scalar.activation(KVT[:], Q[:, 4:12, bass.ds(off, P)], ACT.Copy
                                     ).then_inc(ml_kvt, 1)
                act.wait_ge(ml_tr, u + 1)
                act.wait_ge(ml_cn, u)
                nc.scalar.activation(KVK[:].rearrange("p j t -> p (j t)"),
                                     ps[:, 0:2].rearrange("p a b -> p (a b)"), ACT.Copy
                                     ).then_inc(ml_kvk, 1)
                act.wait_ge(ml_ct, u * 4)
                nc.scalar.activation(NR[:], CT[:, d, :, P:P + 1].broadcast_to([P, 4, P]),
                                     ACT.Copy).then_inc(ml_nr, 1)
                act.wait_ge(ml_bc, u + 1)
                act.wait_ge(ml_w, u)
                for h in range(4):
                    nc.scalar.activation(
                        EE[:, h], ps[:, 2, P * h:P * h + P], ACT.Exp,
                        bias=CS[:, bass.ds(c, 1), 32 * d + h:32 * d + h + 1].rearrange(
                            "p a b -> p (a b)")).then_inc(ml_exp, 1)
                nc.scalar.activation(IW[:].rearrange("p h t -> p (h t)"), ps[:, 3], ACT.Exp
                                     ).then_inc(ml_exp, 1)
                act.wait_ge(ml_y, u)
                nc.scalar.activation(FL[:].rearrange("p h t -> p (h t)"), ps[:, 4], ACT.Exp
                                     ).then_inc(ml_exp, 1)
            chunks(act, body)

        def ml_dve(dve):
            dve.wait_ge(ml_init, 3)
            nc.vector.memset(VW[:], 0.0).then_inc(ml_init, 1)
            dve.wait_ge(ml_col, 2)

            def body(u, d, c, off):
                tok = bass.ds(off, P)
                dve.wait_ge(ml_exp, u * 6 + 4)
                dve.wait_ge(ml_num, u)
                dve.wait_ge(ml_cn, u)
                nc.vector.tensor_tensor(WM[:].rearrange("p h t -> p (h t)"),
                                        EE[:].rearrange("p h t -> p (h t)"), ps[:, 5],
                                        ALU.mult).then_inc(ml_w, 1)
                dve.wait_ge(ml_kvk, u + 1)
                ws = CW[:, bass.ds(c, 1), 32 * d:32 * d + 4].rearrange("p a (h b) -> p (a h) b",
                                                                      b=1)
                nc.vector.tensor_tensor(VW[:, :, 0:P], KVK[:, 4:8], ws.broadcast_to([P, 4, P]),
                                        ALU.mult)
                nc.vector.tensor_copy(VW[:, :, P:P + 1], ws)
                dve.wait_ge(ml_exp, u * 6 + 6)
                nc.vector.tensor_tensor(QT[:], Q[:, 0:4, tok], IW[:], ALU.mult
                                        ).then_inc(ml_vw, 1)
                dve.wait_ge(ml_cn, u + 1)
                dve.wait_ge(ml_nr, u + 1)
                last = P - 1 if d == 0 else 0
                for h in range(4):
                    o = (P + 1) * (h % 2)
                    nc.vector.scalar_tensor_tensor(
                        out=CT[:, d, h], in0=CT[:, d, h], scalar=IW[:, h, last:last + 1],
                        in1=ps[:, h // 2, o:o + P + 1], op0=ALU.mult, op1=ALU.add
                        ).then_inc(ml_ct, 1)
                fl = FL[:].rearrange("p h t -> p (h t)")
                nc.vector.tensor_tensor(fl, fl, ps[:, 7], ALU.max).then_inc(ml_g, 1)
                dve.wait_ge(ml_g, u * 4 + 30)
                nc.vector.scalar_tensor_tensor(out=fl, in0=ps[:, 7], scalar=-1.0, in1=fl,
                                               op0=ALU.mult, op1=ALU.max).then_inc(ml_g, 1)
                dve.wait_ge(ml_g, u * 4 + 31)
                nc.vector.reciprocal(YM[:], FL[:]).then_inc(ml_g, 1)
                dve.wait_ge(ml_g, u * 4 + 32)
                nc.vector.tensor_tensor(YM[:].rearrange("p h t -> p (h t)"), ps[:, 6],
                                        YM[:].rearrange("p h t -> p (h t)"), ALU.mult
                                        ).then_inc(ml_g, 1)
                dve.wait_ge(ml_g, u * 4 + 33)
                nc.vector.tensor_tensor(H[:, :, tok], H[:, :, tok], YM[:], ALU.add
                                        ).then_inc(ml_y, 1)
            chunks(dve, body)

        FB = dict(SQ=at("FSQ", RB, [P, T]), SD=at("FSD", RB + 3, [P, T]),
                  RS=at("FRS", RB + 6, [P, T]), SG=at("FSG", RB + 9, [P, T]),
                  Y=at("FY", RB + 12, [P, T]))

        def fin_pe(pe):
            for h in range(4):
                pe.wait_ge(fin_sq, h + 1)
                if h:
                    pe.wait_ge(fin_sd, 2 * h)
                nc.tensor.matmul(ps[:, 2], ones, FB["SQ"][:, LC:T], start=True, stop=True)
                nc.tensor.matmul(ps[:, 3, 0:LC], ones, FB["SQ"][:, 0:LC], start=True, stop=True
                                 ).then_inc(fin_st, 1)

        def fin_act(act):
            for h in range(4):
                if h:
                    act.wait_ge(fin_y, 2 * h)
                else:
                    act.wait_ge(ml_y, 12)
                nc.scalar.activation(FB["SG"][:], Q[:, 12 + h], ACT.Tanh, scale=0.5
                                     ).then_inc(fin_o, 1)
                act.wait_ge(fin_st, h + 1)
                nc.scalar.activation(FB["SD"][:, LC:T], ps[:, 2], ACT.Sqrt, bias=CO[:, 64:65],
                                     scale=1.0 / P).then_inc(fin_sd, 1)
                nc.scalar.activation(FB["SD"][:, 0:LC], ps[:, 3, 0:LC], ACT.Sqrt,
                                     bias=CO[:, 64:65], scale=1.0 / P).then_inc(fin_sd, 1)
                act.wait_ge(fin_y, 2 * h + 2)
                nc.scalar.activation(XH[:, h], FB["Y"][:], ACT.Copy).then_inc(fin_hi, 1)

        def fin_dve(dve):
            dve.wait_ge(ml_y, 12)
            for h in range(4):
                nc.vector.tensor_tensor(FB["SQ"][:], H[:, h], H[:, h], ALU.mult
                                        ).then_inc(fin_sq, 1)
                dve.wait_ge(fin_sd, 2 * h + 2)
                nc.vector.reciprocal(FB["RS"][:], FB["SD"][:]).then_inc(ml_g, 1)
                dve.wait_ge(fin_o, h + 1)
                nc.vector.tensor_scalar(FB["SG"][:], FB["SG"][:], 0.5, 0.5, ALU.mult, ALU.add
                                        ).then_inc(ml_g, 1)
                dve.wait_ge(ml_g, 78 + 2 * h + 1)
                if h:
                    dve.wait_ge(fin_hi, h)
                    dve.wait_ge(fin_lo, h)
                nc.vector.scalar_tensor_tensor(out=FB["Y"][:], in0=H[:, h],
                                               scalar=vec("out_g", h), in1=FB["RS"][:],
                                               op0=ALU.mult, op1=ALU.mult).then_inc(fin_y, 1)
                dve.wait_ge(fin_y, 2 * h + 1)
                nc.vector.tensor_tensor(FB["Y"][:], FB["Y"][:], FB["SG"][:], ALU.mult
                                        ).then_inc(fin_y, 1)
                dve.wait_ge(fin_hi, h + 1)
                nc.vector.tensor_tensor(XL[:, h], FB["Y"][:], XH[:, h].bitcast(F32),
                                        ALU.subtract).then_inc(fin_lo, 1)

        KD = at("KD", RB, [P, 2, T])
        VA = at("VA", RB + 6, [P, 6, P])
        ASQ = at("ASQ", RB + 9, [P, T])
        ASD = at("ASD", RB + 12, [P, T])
        ARS = at("ARS", RB + 15, [P, T])
        QZ = at("QZ", RB + 18, [P, 8, P])
        PP = at("PP", RB + 22, [P, 2, 640])
        PT = at("PT", RB + 27, [P, 2, 640])
        ON = at("ON", RB + 32, [P, 8, 64])
        SM = at("SM", RB + 34, [P, 6, 8])
        at_sq, at_st, at_sd, at_rs, at_n = (sem("at_sq"), sem("at_st"), sem("at_sd"),
                                            sem("at_rs"), sem("at_n"))
        at_perm, at_x, at_kd, at_va = sem("at_perm"), sem("at_x"), sem("at_kd"), sem("at_va")
        at_vt, at_z = sem("at_vt"), sem("at_z")
        at_qz, at_s, at_mx, at_nb, at_p = (sem("at_qz"), sem("at_s"), sem("at_mx"),
                                           sem("at_nb"), sem("at_p"))
        at_t, at_pt, at_o, at_es, at_r = (sem("at_t"), sem("at_pt"), sem("at_o"), sem("at_es"),
                                          sem("at_r"))
        at_on, at_ot, at_hi, at_lo = sem("at_on"), sem("at_ot"), sem("at_hi"), sem("at_lo")
        QS0, KS0, VS0 = 17, 21, 22
        SCALE = 64 ** -0.5
        KINDS = {"ctx": (0, 0, ()), "first": (2, 0, ((384, 1),)),
                 "mid": (3, -1, ((128, 0), (384, 1))), "last": (2, -1, ((256, 0),))}

        def blocks(eng, body):
            with eng.Fori(0, 2) as i:
                body(i, eng.snap(i * P), i, "ctx")
            body(2, LC, 2, "first")
            with eng.Fori(3, 5) as i:
                body(i, eng.snap(i * P), i, "mid")
            body(5, 5 * P, 5, "last")

        def attn_pe(pe):
            for i in range(5):
                pe.wait_ge(at_sq, i + 1)
                pe.wait_ge(at_sd, 2 * i)
                nc.tensor.matmul(ps[:, 0], bd, ASQ[:, LC:T], start=True, stop=True)
                nc.tensor.matmul(ps[:, 1, 0:LC], bd, ASQ[:, 0:LC], start=True, stop=True
                                 ).then_inc(at_st, 1)
                pe.wait_ge(at_n, i + 1)
                pe.wait_ge(at_x, i)
                nc.tensor.matmul(ps[:, 2], c0("perm", 0, P), Q[:, QS0 + i, LC:T], start=True,
                                 stop=True).then_inc(at_perm, 1)
            pv = ps[:, 3:5].rearrange("p a b -> p (a b)")
            for c in range(6):
                mm = nc.tensor.transpose(pv[:, P * c:P * c + P], Q[:, VS0, P * c:P * c + P], ident)
            mm.then_inc(at_vt, 1)
            pe.wait_ge(at_kd, 64)
            pe.wait_ge(at_va, 1)

            def body(b, tok, blk, kind):
                nb, rel, masks = KINDS[kind]
                ntr = nb + 2

                def scores(h):
                    s = h % 2
                    pe.wait_ge(at_qz, b * 2 + 2)
                    if h >= 2:
                        pe.wait_ge(at_p, b * 8 + (h - 1))
                    else:
                        pe.wait_ge(at_r, b * 2)
                    if nb:
                        o = ps[:, 2 * s, 512 - P * nb:512]
                        nc.tensor.matmul(o, QZ[:, h],
                                         KD[:, h // 4, bass.ds(tok + P * rel, P * nb)],
                                         start=True, stop=not masks)
                        for i, (col, m) in enumerate(masks):
                            nc.tensor.matmul(ps[:, 2 * s, col:col + P], ident,
                                             c0("neg", P * m, P), start=False,
                                             stop=i == len(masks) - 1)
                    nc.tensor.matmul(ps[:, 2 * s + 1, 0:LC], QZ[:, h], KD[:, h // 4, 0:LC],
                                     start=True, stop=True).then_inc(at_s, 1)

                def turn(h):
                    pe.wait_ge(at_p, b * 8 + (h + 1))
                    pe.wait_ge(at_pt, b * 8 + h)
                    pt = ps[:, 4:6].rearrange("p a b -> p (a b)")
                    for k in range(ntr):
                        mm = nc.tensor.transpose(pt[:, P * k:P * k + P],
                                                 PP[:, h % 2, P * k:P * k + P], ident)
                    mm.then_inc(at_t, 1)

                def values(h):
                    pe.wait_ge(at_pt, b * 8 + (h + 1))
                    if h == 0:
                        pe.wait_ge(at_on, b)
                    for k in range(ntr):
                        if k < nb:
                            v = VA[:, bass.ds(blk + (rel + k), 1), 64 * (h // 4):64 * (h // 4) + 64]
                            v = v.rearrange("p a c -> p (a c)")
                        else:
                            v = VA[:, k - nb, 64 * (h // 4):64 * (h // 4) + 64]
                        mm = nc.tensor.matmul(ps[:, 6, 64 * h:64 * h + 64],
                                              PT[:, h % 2, P * k:P * k + P], v, start=k == 0,
                                              stop=k == ntr - 1)
                    mm.then_inc(at_o, 1)
                for h in range(10):
                    if h < 8:
                        scores(h)
                    if 1 <= h <= 8:
                        turn(h - 1)
                    if h >= 2:
                        values(h - 2)
                pe.wait_ge(at_on, b + 1)
                pe.wait_ge(at_lo, b)
                for j in range(4):
                    mm = nc.tensor.transpose(ps[:, 7, P * j:P * j + P],
                                             ON[:, 2 * j:2 * j + 2].rearrange("p a c -> p (a c)"),
                                             ident)
                mm.then_inc(at_ot, 1)
            blocks(pe, body)

        def attn_act(act):
            for i in range(5):
                act.wait_ge(at_st, i + 1)
                act.wait_ge(at_rs, i)
                nc.scalar.activation(ASD[:, LC:T], ps[:, 0], ACT.Sqrt, bias=CO[:, 64:65],
                                     scale=1.0 / 64).then_inc(at_sd, 1)
                nc.scalar.activation(ASD[:, 0:LC], ps[:, 1, 0:LC], ACT.Sqrt, bias=CO[:, 64:65],
                                     scale=1.0 / 64).then_inc(at_sd, 1)
            act.wait_ge(at_vt, 1)
            nc.scalar.activation(VA[:].rearrange("p c t -> p (c t)"),
                                 ps[:, 3:5].rearrange("p a b -> p (a b)")[:, 0:T], ACT.Copy
                                 ).then_inc(at_va, 1)
            act.wait_ge(at_x, 5)
            act.wait_ge(at_z, 12)

            def body(b, tok, blk, kind):
                nb, rel, masks = KINDS[kind]
                n = P * (nb + 2)
                act.wait_ge(at_s, b * 8)
                for e in range(2):
                    nc.scalar.activation(
                        QZ[64 * e:64 * e + 64].rearrange("p (j e) t -> p j e t", e=2)[:, :, e],
                        Q[64 * e:64 * e + 64, QS0:QS0 + 4, bass.ds(tok, P)], ACT.Copy
                        ).then_inc(at_qz, 1)
                for h in range(9):
                    if h < 8:
                        s = h % 2
                        act.wait_ge(at_nb, b * 8 + (h + 1))
                        if h >= 2:
                            act.wait_ge(at_t, b * 8 + (h - 1))
                        else:
                            act.wait_ge(at_t, b * 8)
                        src = ps[:, 2 * s:2 * s + 2].rearrange("p a b -> p (a b)")[
                            :, 512 - P * nb:512 + LC]
                        nc.scalar.activation(PP[:, s, 0:n], src, ACT.Exp,
                                             bias=SM[:, 1, h:h + 1], scale=SCALE,
                                             accum_out=SM[:, 2, h:h + 1]).then_inc(at_p, 1)
                    if h >= 1:
                        g = h - 1
                        act.wait_ge(at_t, b * 8 + (g + 1))
                        act.wait_ge(at_o, b * 8 + max(g - 1, 0))
                        nc.scalar.activation(PT[:, g % 2, 0:n],
                                             ps[:, 4:6].rearrange("p a b -> p (a b)")[:, 0:n],
                                             ACT.Copy).then_inc(at_pt, 1)
                act.wait_ge(at_r, b * 2 + 1)
                nc.scalar.activation(SM[:, 4], SM[:, 3], ACT.Exp).then_inc(at_es, 1)
                act.wait_ge(at_ot, b + 1)
                nc.scalar.activation(XH[:, 4:8, bass.ds(tok, P)],
                                     ps[:, 7].rearrange("p (j t) -> p j t", j=4), ACT.Copy
                                     ).then_inc(at_hi, 1)
            blocks(act, body)

        def attn_dve(dve):
            dve.wait_ge(fin_lo, 4)
            dve.wait_ge(fin_hi, 4)
            for i in range(5):
                x = Q[:, QS0 + i]
                dve.wait_ge(at_st, i)
                nc.vector.tensor_tensor(ASQ[:], x, x, ALU.mult).then_inc(at_sq, 1)
                dve.wait_ge(at_sd, 2 * i + 2)
                nc.vector.reciprocal(ARS[:], ASD[:]).then_inc(at_rs, 1)
                dve.wait_ge(at_rs, i + 1)
                nc.vector.scalar_tensor_tensor(out=x, in0=x, scalar=vec("q_g" if i < 4 else "k_g"),
                                               in1=ARS[:], op0=ALU.mult, op1=ALU.mult
                                               ).then_inc(at_n, 1)
                dve.wait_ge(at_perm, i + 1)
                nc.vector.tensor_tensor(ASQ[:, 0:512], ps[:, 2], c0("sin", 0, LAT), ALU.mult
                                        ).then_inc(at_z, 1)
                nc.vector.tensor_tensor(x[:, LC:T], x[:, LC:T], c0("cos", 0, LAT), ALU.mult
                                        ).then_inc(at_z, 1)
                dve.wait_ge(at_z, 2 * i + 2)
                nc.vector.tensor_tensor(x[:, LC:T], x[:, LC:T], ASQ[:, 0:512], ALU.add
                                        ).then_inc(at_x, 1)
                dve.wait_ge(at_x, i + 1)
            nc.vector.memset(QZ[:], 0.0).then_inc(at_z, 1)
            nc.vector.tensor_scalar(SM[:, 5], vec("sink", 0, 8), -1.0, None, ALU.mult
                                    ).then_inc(at_z, 1)
            dve.wait_ge(at_z, 12)

            def body(b, tok, blk, kind):
                nb, rel, masks = KINDS[kind]
                for h in range(8):
                    s = h % 2
                    dve.wait_ge(at_s, b * 8 + (h + 1))
                    src = ps[:, 2 * s:2 * s + 2].rearrange("p a b -> p (a b)")[
                        :, 512 - P * nb:512 + LC]
                    nc.vector.tensor_reduce(SM[:, 0, h:h + 1], src, AX.X, ALU.max
                                            ).then_inc(at_mx, 1)
                    dve.wait_ge(at_mx, b * 8 + (h + 1))
                    nc.vector.tensor_scalar(SM[:, 1, h:h + 1], SM[:, 0, h:h + 1], -SCALE,
                                            SM[:, 5, h:h + 1], ALU.mult, ALU.min
                                            ).then_inc(at_nb, 1)
                dve.wait_ge(at_nb, b * 8 + 8)
                dve.wait_ge(at_es, b)
                nc.vector.tensor_tensor(SM[:, 3], SM[:, 1], vec("sink", 0, 8), ALU.add
                                        ).then_inc(at_r, 1)
                dve.wait_ge(at_es, b + 1)
                dve.wait_ge(at_p, b * 8 + 8)
                nc.vector.tensor_tensor(SM[:, 4], SM[:, 4], SM[:, 2], ALU.add).then_inc(at_r, 1)
                dve.wait_ge(at_r, b * 2 + 2)
                nc.vector.reciprocal(SM[:, 0], SM[:, 4]).then_inc(at_rs, 1)
                dve.wait_ge(at_rs, b + 6)
                dve.wait_ge(at_o, b * 8 + 8)
                dve.wait_ge(at_ot, b)
                nc.vector.tensor_tensor(ON[:], ps[:, 6].rearrange("p (h c) -> p h c", h=8),
                                        SM[:, 0][:, :, None].broadcast_to([P, 8, 64]), ALU.mult
                                        ).then_inc(at_on, 1)
                dve.wait_ge(at_ot, b + 1)
                dve.wait_ge(at_hi, b + 1)
                xs = bass.ds(tok, P)
                nc.vector.tensor_tensor(XL[:, 4:8, xs],
                                        ps[:, 7].rearrange("p (j t) -> p j t", j=4),
                                        XH[:, 4:8, xs].bitcast(F32), ALU.subtract
                                        ).then_inc(at_lo, 1)
            blocks(dve, body)

        def attn_pool(pool):
            pool.wait_ge(at_x, 5)
            for g in range(2):
                for e in range(2):
                    pool.dma_start(KD[64 * e:64 * e + 64, g], Q[64 * g:64 * g + 64, KS0]
                                   ).then_inc(at_kd, 16)

        RR = at("RR", RB + 24.5, [P, KT, LAT])
        KK_ = at("KK_", RB + 40.5, [P, KT, T])
        VKB = at("VKB", RB + 64.5, [P, 2, 6, P])
        H1 = at("H1", RB + 76.5, [P, 2, T])
        G1 = at("G1", RB + 82.5, [P, 2, LAT])
        MX = at("MX", RB + 86.5, [P, 2, T])
        MC = at("MC", RB + 92.5, [P, 6, 8])
        mc_ready, mx_a, mx_b, mx_c = sem("mc_ready"), sem("mx_a"), sem("mx_b"), sem("mx_c")
        vk_t, vk_c, vk_out, vt_out = sem("vk_t"), sem("vk_c"), [sem("vk_out0"), sem("vk_out1")], sem("vt_out")
        g1_ready, cm1_in, z_out = sem("g1_ready"), sem("cm1_in"), sem("z_out")
        MIXES = [(3, T_V, 8, SEGS), (2, T_K, 8, SEGS), (1, T_W, 1, SEGS), (4, T_A, 1, SEGS),
                 (0, T_R, 8, (LATS,)), (5, T_G, 2, (LATS,))]

        def ushift(k, sg, by):
            a = 2 + 2 * SEGS.index(sg) + sg[0] + by
            return U[:, k, a:a + sg[1]]

        def mix_act(act, q):
            i, t0, n, segs = MIXES[q]
            a = segs[0][0]

            def scale(k):
                if k >= 2:
                    act.wait_ge(x_lo, 16 + 8 * q + k - 1)
                for sg in segs:
                    ins = nc.scalar.activation(MX[:, k % 2, sg[0]:sg[0] + sg[1]], ushift(k, sg, 0),
                                               ACT.Copy, scale=MC[:, i, k:k + 1])
                ins.then_inc(mx_a, 1)
            if q == 0:
                act.wait_ge(mc_ready, 2)
                act.wait_ge(n_h, 24)
            act.wait_ge(x_lo, 16 + 8 * q)
            for k in range(KT):
                if k == 0:
                    scale(0)
                if k + 1 < KT:
                    scale(k + 1)
                act.wait_ge(mx_c, 8 * q + k + 1)
                nc.scalar.activation(XH[:, k, a:T], MX[:, k % 2, a:T], ACT.Copy).then_inc(x_hi, 1)

        def mix_dve(dve, q):
            i, t0, n, segs = MIXES[q]
            a = segs[0][0]
            for k in range(KT):
                dve.wait_ge(mx_a, 8 * q + k + 1)
                for by, sm in ((-1, mx_b), (1, mx_c)):
                    for sg in segs:
                        m = MX[:, k % 2, sg[0]:sg[0] + sg[1]]
                        ins = nc.vector.scalar_tensor_tensor(
                            out=m, in0=ushift(k, sg, by),
                            scalar=vec("mu", 16 * i + (0 if by < 0 else 8) + k), in1=m,
                            op0=ALU.mult, op1=ALU.add)
                    ins.then_inc(sm, 1)
                    dve.wait_ge(sm, 8 * q + k + 1)
                dve.wait_ge(x_hi, 16 + 8 * q + k + 1)
                nc.vector.tensor_tensor(XL[:, k, a:T], MX[:, k % 2, a:T],
                                        XH[:, k, a:T].bitcast(F32), ALU.subtract
                                        ).then_inc(x_lo, 1)

        def at_tile(x, m, lo, hi):
            return x[:, bass.ds(m, 1), lo:hi].rearrange("p a t -> p (a t)")

        def mix_evict(q, eng):
            def act_side(t, m, s):
                if q <= 1:
                    nc.scalar.activation(at_tile(KK_, m, LC, T), acc(s, LATS), ACT.Copy
                                         ).then_inc(acc_lat, 1)
                elif q <= 3:
                    f = ACT.Tanh if q == 2 else ACT.Copy
                    nc.scalar.activation(H1[:, q - 2, 0:LC], acc(s, CTX), f).then_inc(acc_ctx, 1)
                    nc.scalar.activation(H1[:, q - 2, LC:T], acc(s, LATS), f).then_inc(acc_lat, 1)
                elif q == 4:
                    nc.scalar.activation(at_tile(RR, m, 0, LAT), acc(s, LATS), ACT.Copy
                                         ).then_inc(acc_lat, 1)
                else:
                    nc.scalar.activation(G1[:, m], acc(s, LATS), ACT.Tanh, scale=0.5
                                         ).then_inc(acc_lat, 1)

            def dve_side(t, m, s):
                if q <= 1:
                    nc.vector.tensor_copy(at_tile(KK_, m, 0, LC), acc(s, CTX)).then_inc(acc_ctx, 1)
            return act_side if eng == "act" else dve_side

        def vk_pe(pe):
            pe.wait_ge(acc_lat, T_V + 8)
            pe.wait_ge(acc_ctx, T_V + 8)
            for m in range(8):
                if m >= 2:
                    pe.wait_ge(vk_c, m - 1)
                b = 4 + 2 * (m % 2)
                o = ps[:, b:b + 2].rearrange("p a b -> p (a b)")
                for c in range(6):
                    mm = nc.tensor.transpose(o[:, P * c:P * c + P], KK_[:, m, P * c:P * c + P],
                                             ident)
                mm.then_inc(vk_t, 1)

        def vk_act(act):
            for m in range(8):
                act.wait_ge(vk_t, m + 1)
                if m >= 2:
                    act.wait_ge(vk_out[m % 2], 16 * (m // 2))
                b = 4 + 2 * (m % 2)
                nc.scalar.activation(VKB[:, m % 2].rearrange("p c t -> p (c t)"),
                                     ps[:, b:b + 2].rearrange("p a b -> p (a b)")[:, 0:T],
                                     ACT.Copy).then_inc(vk_c, 1)

        def vk_pool(pool):
            pool.wait_ge(n_h, 24)
            pool.dma_start(z_dram, z[:, :, LC:T]).then_inc(z_out, 16)
            pool.wait_ge(acc_lat, T_V + 8)
            pool.dma_start(vt_dram, KK_[:, :, LC:T]).then_inc(vt_out, 16)
            for m in range(8):
                pool.wait_ge(vk_c, m + 1)
                pool.dma_start(vk_dram[:, P * m:P * m + P].rearrange("(c p) n -> p c n", p=P),
                               VKB[:, m % 2]).then_inc(vk_out[m % 2], 16)

        KN = at("KN", RB, [P, KT, T])
        KQ = at("KQ", RB + 64.5, [P, T])
        KSQ = at("KSQ", RB + 67.5, [P, T])
        KSD = at("KSD", RB + 70.5, [P, T])
        KRS = at("KRS", RB + 73.5, [P, T])
        kk_sq, kk_st, kk_mx, kk_sd, kk_n = (sem("kk_sq"), sem("kk_st"), sem("kk_mx"),
                                            sem("kk_sd"), sem("kk_n"))

        def kk_pe(pe):
            for m in range(8):
                pe.wait_ge(kk_sq, 2 * m + 2)
                nc.tensor.matmul(ps[:, 4], bd, KSQ[:, LC:T], start=True, stop=True)
                nc.tensor.matmul(ps[:, 5, 0:LC], bd, KSQ[:, 0:LC], start=True, stop=True
                                 ).then_inc(kk_st, 1)

        def kk_act(act):
            for m in range(8):
                act.wait_ge(kk_mx, m + 1)
                nc.scalar.activation(KSD[:], KSD[:], ACT.Sqrt).then_inc(kk_sd, 1)

        def kk_dve(dve):
            dve.wait_ge(vk_out[0], 64)
            dve.wait_ge(vk_out[1], 64)
            dve.wait_ge(acc_lat, T_G + 2)
            nc.vector.tensor_scalar(G1[:], G1[:], 0.5, 0.5, ALU.mult, ALU.add
                                    ).then_inc(g1_ready, 1)
            for m in range(8):
                nc.vector.tensor_scalar(KQ[:], KK_[:, m], vec("k_k", m), None, ALU.mult
                                        ).then_inc(kk_sq, 1)
                dve.wait_ge(kk_sq, 2 * m + 1)
                nc.vector.tensor_tensor(KSQ[:], KQ[:], KQ[:], ALU.mult).then_inc(kk_sq, 1)
                dve.wait_ge(kk_st, m + 1)
                nc.vector.tensor_scalar(KSD[:, LC:T], ps[:, 4], 1e-24, None, ALU.max)
                nc.vector.tensor_scalar(KSD[:, 0:LC], ps[:, 5, 0:LC], 1e-24, None, ALU.max
                                        ).then_inc(kk_mx, 1)
                dve.wait_ge(kk_sd, m + 1)
                nc.vector.reciprocal(KRS[:], KSD[:]).then_inc(kk_n, 1)
                dve.wait_ge(kk_n, 2 * m + 1)
                nc.vector.tensor_tensor(KN[:, m], KQ[:], KRS[:], ALU.mult).then_inc(kk_n, 1)
                dve.wait_ge(kk_n, 2 * m + 2)

        L2 = at("L2", 0, [P, 2, D])
        TA = at("TA", 8, [P, 8, L])
        TB = at("TB", 10, [P, 8, L])
        TC = at("TC", 12, [P, 8, L])
        TE = at("TE", 14, [P, 8, L])
        TQ = at("TQ", 16, [P, 8, L])
        TK = at("TK", 18, [P, 8, L])
        DOT = at("DOT", 20, [16, LAT])
        units = [RA + 4 * i for i in range(12)] + [RB + 64.5 + 4 * i for i in range(3)] + [
            RB + 86.5, RB + 90.5]

        def two(name, first, shape):
            return [at(f"{name}{d}", units[first + 8 * d], shape) for d in range(2)]
        BK = two("BK", 0, [P, 8, 2, L])
        AR = two("AR", 1, [P, 8, 2, L])
        NBD = two("NBD", 2, [P, 8, 2, L])
        MTB = two("MTB", 3, [P, 8, 2, L])
        RBK = two("RBK", 4, [P, 8, 2, L])
        PBD = two("PBD", 5, [P, 8, 2, L])
        SBD = two("SBD", 6, [P, 8, 2, L])
        UV = two("UV", 7, [P, 8, 2, L])
        ZZ = [at("ZZ0", units[16], [P, 8, L]), at("ZZ1", RB + 94.5, [P, 8, L])]
        XX = [at("XX0", units[16] + 2, [P, 8, L]), at("XX1", 22, [P, 8, L])]
        HS = at("HS", RB + 96.5, [P, 2, L])
        RK = at("RK", RB + 97, [P, 8, 16])
        PL = at("PL", 52.75, [P, 2, 8])
        OK = at("OK", 52.8125, [P, 8])
        l2_in, sc_init = sem("l2_in"), sem("sc_init")
        pr_hs, pr_lo, pr_x, pr_t, pr_g, pr_e = (sem("pr_hs"), sem("pr_lo"), sem("pr_x"),
                                                sem("pr_t"), sem("pr_g"), sem("pr_e"))
        pr_q, pr_rr, pr_o, pr_dp, pr_dt = (sem("pr_q"), sem("pr_rr"), sem("pr_o"),
                                           sem("pr_dp"), sem("pr_dt"))

        def each(name):
            return [sem(f"{name}{d}") for d in range(2)]
        gA, gR, gT, eA, eR, eT = sem("gA"), sem("gR"), sem("gT"), sem("eA"), sem("eR"), sem("eT")
        zi, z0, iX, iP, iC, iZ, iM, zB = (sem("zi"), sem("z0"), sem("iX"), sem("iP"), sem("iC"),
                                          sem("iZ"), sem("iM"), sem("zB"))
        cH, rH, cU, uU, cY, yS, cS, sA, sU = (sem("cH"), sem("rH"), sem("cU"), sem("uU"),
                                              sem("cY"), sem("yS"), sem("cS"), sem("sA"),
                                              sem("sU"))
        waits_seen = sem("waits_seen")
        yO, vI = each("yO"), each("vI")
        ROWS = (slice(0, 64), slice(64, 128))

        def scan_loop(eng, body):
            for lo, n, base, last in ((0, 4, 0, LC), (4, 8, LC, T)):
                with eng.Fori(0, n) as i:
                    off = [eng.snap(i * L + base), eng.snap(i * -L + (last - L))]
                    body(i + lo, i if lo else None, off)

        def toks(x, off):
            return x[:, :, bass.ds(off, L)]

        def scan_pe(pe):
            pe.wait_ge(l2_in, 16)
            pe.wait_ge(sc_init, 10)
            pe.wait_ge(cm1_in, 16)

            def body(it, il, off):
                bank = [4 * d for d in range(2)]
                for d in range(2):
                    u = it * 2 + d
                    r = ROWS[d]
                    pe.wait_ge(pr_hs, u + 1)
                    pe.wait_ge(iM, it * 10)
                    pe.wait_ge(zB, it * 2)
                    for j in range(2):
                        for p in range(8):
                            mm = nc.tensor.matmul(ps[:, bank[d] + j, L * p:L * p + L],
                                                  L2[r, j, P * p:P * p + P], HS[r, j],
                                                  start=True, stop=True)
                    mm.then_inc(pr_lo, 1)
                    if il is not None:
                        pe.wait_ge(pr_rr, il * 2 + d + 1)
                        pe.wait_ge(rH, it * 2)
                        pe.wait_ge(yS, il * 2)
                        for p in range(8):
                            mm = nc.tensor.matmul(ps[0:16, bank[d] + 2, 0:L], RK[:, p], TB[:, p],
                                                  start=p == 0, stop=p == 7)
                        mm.then_inc(pr_dp, 1)
                for d in range(2):
                    pe.wait_ge(pr_o, it * 2 + d + 1)
                    for e in range(2):
                        for p in range(8):
                            mm = nc.tensor.matmul(
                                ps[:, bank[d] + e, L * p:L * p + L],
                                BK[d][ROWS[e], p].rearrange("p a t -> p (a t)"),
                                AR[d][ROWS[e], p, 0], start=True, stop=True)
                    mm.then_inc(gA, 1)
                if il is not None:
                    for d in range(2):
                        pe.wait_ge(pr_dt, il * 2 + 2)
                        pe.wait_ge(sU, it * 2)
                        for e in range(2):
                            for p in range(8):
                                mm = nc.tensor.matmul(
                                    ps[:, bank[d] + 2 + e, L * p:L * p + L],
                                    BK[d][ROWS[e], p].rearrange("p a t -> p (a t)"),
                                    AR[d][ROWS[e], p, 1], start=True, stop=True)
                        mm.then_inc(gR, 1)
                for d in range(2):
                    pe.wait_ge(consts_in, 32)
                    pe.wait_ge(eA, it * 2 + (d + 1))
                    for e in range(2):
                        for p in range(8):
                            mm = nc.tensor.transpose(
                                ps[:, bank[d] + e, L * p:L * p + L],
                                BK[d][ROWS[e], p].rearrange("p a t -> p (a t)"),
                                ident[ROWS[e], ROWS[e]])
                    mm.then_inc(gT, 1)
                for l in range(5):
                    for d in range(2):
                        pe.wait_ge(iX, it * 10 + (2 * l + d + 1))
                        if l == 0:
                            pe.wait_ge(eT, it * 2 + (d + 1))
                        for p in range(8):
                            mm = nc.tensor.matmul(ps[:, bank[d], L * p:L * p + L],
                                                  NBD[d][:, p].rearrange("p a t -> p (a t)"),
                                                  XX[d][:, p], start=True, stop=True)
                        mm.then_inc(iP, 1)
                    for d in range(2):
                        pe.wait_ge(iC, it * 10 + (2 * l + d + 1))
                        for p in range(8):
                            mm = nc.tensor.matmul(ps[:, bank[d] + 1, L * p:L * p + L],
                                                  PBD[d][:, p].rearrange("p a t -> p (a t)"),
                                                  ZZ[d][:, p], start=True, stop=True)
                        mm.then_inc(iZ, 1)
                for d in range(2):
                    pe.wait_ge(vI[d], it * 32 + 32)
                    pe.wait_ge(sU, it * 2)
                    if il is not None:
                        pe.wait_ge(eR, il * 2 + (d + 1))
                    for p in range(8):
                        for e in range(2):
                            o = ps[ROWS[e], bank[d] + 2, L * p:L * p + L]
                            nc.tensor.matmul(o, MTB[d][:, p, e], UV[d][:, p, e], start=True,
                                             stop=False)
                            mm = nc.tensor.matmul(o, AR[d][:, p, 0], SBD[d][:, p, e],
                                                  start=False, stop=True)
                    mm.then_inc(cH, 1)
                for d in range(2):
                    pe.wait_ge(rH, it * 2 + (d + 1))
                    pe.wait_ge(zB, it * 2 + (d + 1))
                    for p in range(8):
                        mm = nc.tensor.matmul(ps[:, bank[d] + 3, L * p:L * p + L],
                                              PBD[d][:, p].rearrange("p a t -> p (a t)"),
                                              XX[d][:, p], start=True, stop=True)
                    mm.then_inc(cU, 1)
                for d in range(2):
                    pe.wait_ge(uU, it * 2 + (d + 1))
                    if il is not None:
                        for p in range(8):
                            o = ps[:, bank[d] + 2, L * p:L * p + L]
                            nc.tensor.matmul(o, SBD[d][:, p].rearrange("p a t -> p (a t)"),
                                             AR[d][:, p, 1], start=True, stop=False)
                            for e in range(2):
                                mm = nc.tensor.matmul(ps[ROWS[e], bank[d] + 2, L * p:L * p + L],
                                                      UV[d][:, p, e], RBK[d][:, p, e],
                                                      start=False, stop=True)
                        mm.then_inc(cY, 1)
                    for p in range(8):
                        for e in range(2):
                            mm = nc.tensor.matmul(ps[ROWS[e], bank[d] + 3, L * p:L * p + L],
                                                  BK[d][:, p, e], UV[d][:, p, e], start=True,
                                                  stop=True)
                    mm.then_inc(cS, 1)
            scan_loop(pe, body)

        def scan_act(act):
            act.wait_ge(sc_init, 10)

            def body(it, il, off):
                for d in range(2):
                    u = it * 2 + d
                    r = ROWS[d]
                    act.wait_ge(pr_lo, u)
                    src = H1[r, :, bass.ds(off[d], L)]
                    nc.scalar.activation(HS[r], src, ACT.Copy
                                         ).then_inc(pr_hs, 1)
                    for j, x in enumerate((TA, TB)):
                        act.wait_ge(pr_x, u * 2 + j + 1)
                        nc.scalar.activation(x[:], x[:], ACT.Tanh, scale=0.5).then_inc(pr_t, 1)
                    act.wait_ge(pr_g, u * 4 + 4)
                    nc.scalar.activation(TE[:], TC[:], ACT.Exp, scale=-KAPPA).then_inc(pr_e, 1)
                    nc.scalar.activation(TA[:], TA[:], ACT.Exp, scale=-KAPPA).then_inc(pr_e, 1)
                    act.wait_ge(pr_e, u * 3 + 1)
                    nc.scalar.activation(TC[:], TC[:], ACT.Exp, scale=KAPPA).then_inc(pr_e, 1)
                for d in range(2):
                    act.wait_ge(zB, it * 2)
                    if il is not None:
                        act.wait_ge(yO[d], il * 16)
                    nc.scalar.activation(ZZ[d][:], c1("eye", 0, L)[:, None, :].broadcast_to(
                        [P, 8, L]), ACT.Copy).then_inc(zi, 1)
                for d in range(2):
                    act.wait_ge(gT, it * 2 + (d + 1))
                    for e in range(2):
                        ins = nc.scalar.activation(
                            BK[d][:, :, e], ps[:, 4 * d + e].rearrange("p (a t) -> p a t", t=L),
                            ACT.Copy)
                    ins.then_inc(eT, 1)
                for l in range(5):
                    for d in range(2):
                        act.wait_ge(iP, it * 10 + (2 * l + d + 1))
                        for e in range(2):
                            ins = nc.scalar.activation(
                                PBD[d][ROWS[e], :, e],
                                ps[ROWS[e], 4 * d].rearrange("p (a t) -> p a t", t=L), ACT.Copy)
                        ins.then_inc(iC, 1)
                for d in range(2):
                    act.wait_ge(iM, it * 10 + (9 + d))
                    for e in range(2):
                        ins = nc.scalar.activation(PBD[d][ROWS[e], :, e], ZZ[d][ROWS[e]],
                                                   ACT.Copy)
                    ins.then_inc(zB, 1)
                for d in range(2):
                    act.wait_ge(cH, it * 2 + (d + 1))
                    nc.scalar.activation(XX[d][:].rearrange("p a t -> p (a t)"),
                                         ps[:, 4 * d + 2], ACT.Copy).then_inc(rH, 1)
                for d in range(2):
                    act.wait_ge(cU, it * 2 + (d + 1))
                    for e in range(2):
                        ins = nc.scalar.activation(
                            UV[d][ROWS[e], :, e],
                            ps[ROWS[e], 4 * d + 3].rearrange("p (a t) -> p a t", t=L), ACT.Copy)
                    ins.then_inc(uU, 1)
                if il is not None:
                    for d in range(2):
                        act.wait_ge(cY, il * 2 + (d + 1))
                        nc.scalar.activation(ZZ[d][:], ps[:, 4 * d + 2].rearrange("p (a t) -> p a t",
                                                                           t=L), ACT.Copy
                                             ).then_inc(yS, 1)
            scan_loop(act, body)

        def scan_dve(dve):
            dve.wait_ge(z_out, 16)
            dve.wait_ge(tile_done, T_G + 2)
            dve.wait_ge(cm1_in, 16)
            nc.vector.memset(DOT[:], 0.0).then_inc(sc_init, 1)
            for d in range(2):
                for x in (NBD, MTB, PBD, SBD):
                    nc.vector.memset(x[d][:], 0.0)
                nc.vector.memset(UV[d][:], 0.0).then_inc(sc_init, 4)
            nc.vector.tensor_tensor(
                RK[:], c1("hsel", 0, P).rearrange("p (m h) -> p m h", m=8),
                vec("r_k", 0, 8)[:, :, None].broadcast_to([P, 8, 16]), ALU.mult
                ).then_inc(sc_init, 1)
            nc.vector.tensor_scalar(OK[:], vec("k_a", 0, 8), -1.0, 1.0, ALU.mult, ALU.add
                                    ).then_inc(sc_init, 1)
            dve.wait_ge(kk_n, 16)

            def fl(x):
                return x.rearrange("p a t -> p (a t)")

            def body(it, il, off):
                for d in range(2):
                    u = it * 2 + d
                    dve.wait_ge(pr_lo, u + 1)
                    dve.wait_ge(pr_q, u * 4)
                    dve.wait_ge(pr_o, u)
                    if il is not None:
                        dve.wait_ge(pr_dp, il * 2 + d)
                    for j, (x, w) in enumerate(((TA, "w0"), (TB, "a0"))):
                        nc.vector.tensor_tensor(
                            x[:], ps[:, 4 * d + j].rearrange("p (a t) -> p a t", t=L),
                            vec(w, 8 * d, 8)[:, :, None].broadcast_to([P, 8, L]), ALU.add
                            ).then_inc(pr_x, 1)
                    dve.wait_ge(pr_t, u * 2 + 1)
                    nc.vector.tensor_scalar(TA[:], TA[:], 0.5, 0.5, ALU.mult, ALU.add
                                            ).then_inc(pr_g, 1)
                    dve.wait_ge(pr_t, u * 2 + 2)
                    nc.vector.tensor_scalar(TB[:], TB[:], 0.5, 0.5, ALU.mult, ALU.add
                                            ).then_inc(pr_g, 1)
                    dve.wait_ge(pr_g, u * 4 + 1)
                    step = 1 if d == 0 else -1
                    nc.vector.tensor_tensor_scan(fl(TC[:])[:, ::step], c1("reset", 0, 512),
                                                 fl(TA[:])[:, ::step], 0.0, ALU.mult, ALU.add
                                                 ).then_inc(pr_g, 1)
                    dve.wait_ge(pr_g, u * 4 + 3)
                    nc.vector.tensor_tensor(TA[:], TC[:], TA[:], ALU.subtract).then_inc(pr_g, 1)
                    dve.wait_ge(pr_e, u * 3 + 3)
                    dve.wait_ge(cS, it * 2)
                    nc.vector.scalar_tensor_tensor(out=AR[d][:, :, 0], in0=toks(KN, off[d]),
                                                   scalar=-1.0, in1=TA[:], op0=ALU.mult,
                                                   op1=ALU.mult)
                    nc.vector.tensor_copy(PL[:, d], TE[:, :, L - 1 if d == 0 else 0])
                    if il is not None:
                        roff = il * L if d == 0 else il * -L + (LAT - L)
                        nc.vector.tensor_tensor(AR[d][:, :, 1], toks(RR, roff), TE[:],
                                                ALU.mult)
                    dve.wait_ge(pr_q, u * 4 + 4)
                    for e in range(2):
                        nc.vector.tensor_tensor(BK[d][ROWS[e], :, e], TK[ROWS[e]], TC[ROWS[e]],
                                                ALU.mult)
                        ins = nc.vector.tensor_tensor(BK[d][ROWS[e], :, 1 - e], TQ[ROWS[e]],
                                                      TC[ROWS[e]], ALU.mult)
                    ins.then_inc(pr_o, 1)
                    if il is not None:
                        dve.wait_ge(pr_dp, il * 2 + d + 1)
                        dv = DOT[:, bass.ds(roff, L)]
                        dve.wait_ge(pr_dt, il * 2 + d)
                        nc.vector.tensor_tensor(dv, dv, ps[0:16, 4 * d + 2, 0:L], ALU.add
                                                ).then_inc(pr_dt, 1)
                for d in range(2):
                    dve.wait_ge(gA, it * 2 + (d + 1))
                    for e in range(2):
                        for x, r in ((NBD, ROWS[e]), (MTB, ROWS[1 - e])):
                            ins = nc.vector.tensor_tensor(
                                x[d][r, :, e],
                                ps[r, 4 * d + e].rearrange("p (a t) -> p a t", t=L),
                                c1("mstrict", L * d, L)[r][:, None, :].broadcast_to([64, 8, L]),
                                ALU.mult)
                    ins.then_inc(eA, 1)
                if il is not None:
                    for d in range(2):
                        dve.wait_ge(gR, il * 2 + (d + 1))
                        for e in range(2):
                            ins = nc.vector.tensor_tensor(
                                RBK[d][:, :, e],
                                ps[:, 4 * d + 2 + e].rearrange("p (a t) -> p a t", t=L),
                                c1("mincl", L * d, L)[:, None, :].broadcast_to([P, 8, L]), ALU.mult)
                        ins.then_inc(eR, 1)

                def lvl(d, l, r=slice(0, P)):
                    m = c1("lvl", L * (6 * d + l), L)[r].bitcast(U32)
                    return m[:, None, :].broadcast_to([m.shape[0], 8, L])

                def turn(d, l):
                    nc.vector.transpose(fl(XX[d][:]), fl(ZZ[d][:])).then_inc(iX, 1)
                for d in range(2):
                    dve.wait_ge(zi, it * 2 + (d + 1))
                    dve.wait_ge(eA, it * 2 + (d + 1))
                    dve.sem_inc(waits_seen)
                    for e in range(2):
                        ins = nc.vector.copy_predicated(ZZ[d][ROWS[e]], lvl(d, 0, ROWS[e]),
                                                        NBD[d][ROWS[e], :, e])
                    ins.then_inc(z0, 1)
                    dve.wait_ge(z0, it * 2 + (d + 1))
                    dve.wait_ge(cU, it * 2)
                    turn(d, 0)
                for l in range(5):
                    for d in range(2):
                        dve.wait_ge(iZ, it * 10 + (2 * l + d + 1))
                        dve.sem_inc(waits_seen)
                        nc.vector.copy_predicated(
                            ZZ[d][:], lvl(d, l + 1),
                            ps[:, 4 * d + 1].rearrange("p (a t) -> p a t", t=L)
                            ).then_inc(iM, 1)
                        if l < 4:
                            dve.wait_ge(iM, it * 10 + (2 * l + d + 1))
                            turn(d, l + 1)
                for d in range(2):
                    dve.wait_ge(cS, it * 2 + (d + 1))
                    for e in range(2):
                        s_ = SBD[d][ROWS[e], :, e]
                        ins = nc.vector.tensor_tensor(
                            s_, s_, ps[ROWS[e], 4 * d + 3].rearrange("p (a t) -> p a t", t=L),
                            ALU.add)
                    ins.then_inc(sA, 1)
                    dve.wait_ge(sA, it * 2 + (d + 1))
                    for e in range(2):
                        s_ = SBD[d][ROWS[e], :, e]
                        ins = nc.vector.tensor_tensor(
                            s_, s_, PL[ROWS[e], d][:, :, None].broadcast_to([64, 8, L]),
                            ALU.mult)
                    ins.then_inc(sU, 1)
            scan_loop(dve, body)

        def scan_pool(pool):
            pool.dma_start(CM1[:], cm1[:, 0:NC1 - D]).then_inc(cm1_in, 16)
            pool.wait_ge(z_out, 16)
            pool.dma_start(L2[:], lora2).then_inc(l2_in, 16)
            pool.wait_ge(sc_init, 11)
            pool.wait_ge(kk_n, 16)
            for b in range(2):
                pool.wait_ge(vk_out[b], 64)
            vk = vk_dram.rearrange("t (m e n) -> t m e n", e=2, n=L)

            def body(it, il, off):
                for d in range(2):
                    pool.wait_ge(cS, it * 2)
                    pool.sem_inc(waits_seen)
                    for e in range(2):
                        src = vk[bass.ds(off[d], L)]
                        pool.dma_start(UV[d][ROWS[1 - e], :, e], src[:, :, e]
                                       ).then_inc(vI[d], 16)
                for d in range(2):
                    u = it * 2 + d
                    pool.wait_ge(pr_g, u * 4 + 2)
                    pool.wait_ge(pr_o, u)
                    nc.gpsimd.tensor_tensor(TK[:], toks(KN, off[d]), TB[:], ALU.mult
                                            ).then_inc(pr_q, 1)
                    nc.gpsimd.tensor_tensor(TQ[:], TB[:], vec("k_a", 0, 8)[:, :, None
                                            ].broadcast_to([P, 8, L]), ALU.mult
                                            ).then_inc(pr_q, 1)
                    pool.wait_ge(pr_q, u * 4 + 2)
                    nc.gpsimd.tensor_tensor(TQ[:], TQ[:], OK[:][:, :, None].broadcast_to(
                        [P, 8, L]), ALU.add).then_inc(pr_q, 1)
                    pool.wait_ge(pr_q, u * 4 + 3)
                    nc.gpsimd.tensor_tensor(TQ[:], TQ[:], toks(KK_, off[d]), ALU.mult
                                            ).then_inc(pr_q, 1)
                    if il is not None:
                        pool.wait_ge(pr_q, u * 4 + 4)
                        roff = il * L if d == 0 else il * -L + (LAT - L)
                        nc.gpsimd.tensor_tensor(TB[:], TQ[:], toks(RR, roff), ALU.mult
                                                ).then_inc(pr_rr, 1)
                if il is not None:
                    for d in range(2):
                        roff = il * L if d == 0 else il * -L + (LAT - L)
                        pool.wait_ge(yS, il * 2 + (d + 1))
                        pool.sem_inc(waits_seen)
                        pool.dma_start(y_dram[d][:, :, bass.ds(roff, L)], ZZ[d][:]
                                       ).then_inc(yO[d], 16)
            scan_loop(pool, body)

        G2 = at("G2", RB + 40.5, [P, 2, D])
        HB = at("HB", RB + 16, [16, D])
        YA = at("YA", RB + 48.5, [P, 2, 3, LAT])
        YC = at("YC", RB, [P, 2, LAT])
        YQ = at("YQ", RB + 4, [P, LAT])
        YD = at("YD", RB + 6, [P, LAT])
        YR = at("YR", RB + 8, [P, LAT])
        YB = at("YB", RB + 10, [P, LAT])
        YT = at("YT", RB + 12, [P, 2, LAT])
        g2_in, y_in, z_in = sem("g2_in"), [sem("y_in0"), sem("y_in1")], sem("z_in")
        po_s, po_m, po_c, po_q, po_v, po_d = (sem("po_s"), sem("po_m"), sem("po_c"),
                                              sem("po_q"), sem("po_v"), sem("po_d"))
        po_t, po_y, po_hi, po_lo = sem("po_t"), sem("po_y"), sem("po_hi"), sem("po_lo")

        def post_pool(pool):
            for d in range(2):
                pool.wait_ge(yO[d], 128)
            pool.wait_ge(sU, 24)
            pool.wait_ge(pr_dt, 16)
            pool.dma_start(G2[:], g2w).then_inc(g2_in, 16)
            pool.dma_start(HB[:], cm1[0:16, C1OFF["hbc"]:C1OFF["hbc"] + D]).then_inc(g2_in, 16)
            pool.wait_ge(vt_out, 16)
            for m in range(8):
                if m >= 2:
                    pool.wait_ge(po_y, m - 1)
                for i, src in enumerate((y_dram[0], y_dram[1], vt_dram)):
                    pool.dma_start(YA[:, m % 2, i], src[:, m]).then_inc(y_in[m % 2], 16)

        def post_zin(pool):
            pool.wait_ge(po_lo, 8)
            pool.dma_start(z[:, :, LC:T], z_dram).then_inc(z_in, 16)

        def post_pe(pe):
            pe.wait_ge(g2_in, 32)
            pe.wait_ge(g1_ready, 1)
            for m in range(8):
                pe.wait_ge(po_s, m + 1)
                nc.tensor.matmul(ps[:, 4], bd, YC[:, m % 2], start=True, stop=True
                                 ).then_inc(po_m, 1)
                pe.wait_ge(po_y, m)
                nc.tensor.matmul(ps[:, 5], HB[:, P * m:P * m + P], DOT[:], start=True,
                                 stop=True)
                nc.tensor.matmul(ps[:, 6], G2[:, 0, P * m:P * m + P], G1[:, 0], start=True,
                                 stop=False)
                nc.tensor.matmul(ps[:, 6], G2[:, 1, P * m:P * m + P], G1[:, 1], start=False,
                                 stop=True)
                pe.wait_ge(po_q, m + 1)
                nc.tensor.matmul(ps[:, 7], bd, YQ[:], start=True, stop=True).then_inc(po_v, 1)

        def post_act(act):
            for m in range(8):
                act.wait_ge(po_c, m + 1)
                nc.scalar.activation(YQ[:], YC[:, m % 2], ACT.Square).then_inc(po_q, 1)
                act.wait_ge(po_v, m + 1)
                act.wait_ge(po_t, 4 * m)
                nc.scalar.activation(YD[:], ps[:, 7], ACT.Sqrt, bias=CO[:, 65:66], scale=1.0 / L
                                     ).then_inc(po_d, 1)
                act.wait_ge(po_y, m + 1)
                nc.scalar.activation(XH[:, m, LC:T], YT[:, m % 2], ACT.Copy).then_inc(po_hi, 1)

        def post_dve(dve):
            dve.wait_ge(pr_dt, 16)
            for m in range(8):
                dve.wait_ge(y_in[m % 2], 48 * (m // 2 + 1))
                yc = YC[:, m % 2]
                nc.vector.tensor_tensor(yc, YA[:, m % 2, 0], YA[:, m % 2, 1], ALU.add
                                        ).then_inc(po_s, 1)
                dve.wait_ge(po_m, m + 1)
                nc.vector.scalar_tensor_tensor(out=yc, in0=ps[:, 4], scalar=-1.0 / L, in1=yc,
                                               op0=ALU.mult, op1=ALU.add).then_inc(po_c, 1)
                dve.wait_ge(po_d, m + 1)
                nc.vector.reciprocal(YR[:], YD[:]).then_inc(po_t, 1)
                dve.wait_ge(po_t, 4 * m + 1)
                yt = YT[:, m % 2]
                if m >= 2:
                    dve.wait_ge(po_hi, m - 1)
                    dve.wait_ge(po_lo, m - 1)
                nc.vector.tensor_tensor(yt, yc, YR[:], ALU.mult).then_inc(po_t, 1)
                nc.vector.tensor_tensor(YB[:], ps[:, 5], YA[:, m % 2, 2], ALU.mult)
                dve.wait_ge(po_t, 4 * m + 2)
                nc.vector.tensor_scalar(yt, yt, vec("ln_g", m), vec("ln_b", m), ALU.mult, ALU.add
                                        ).then_inc(po_t, 1)
                dve.wait_ge(po_t, 4 * m + 3)
                nc.vector.tensor_tensor(yt, yt, YB[:], ALU.add).then_inc(po_t, 1)
                dve.wait_ge(po_t, 4 * m + 4)
                nc.vector.tensor_tensor(yt, ps[:, 6], yt, ALU.mult).then_inc(po_y, 1)
                dve.wait_ge(po_hi, m + 1)
                nc.vector.tensor_tensor(XL[:, m, LC:T], yt, XH[:, m, LC:T].bitcast(F32),
                                        ALU.subtract).then_inc(po_lo, 1)

        block = ctx.enter_context(nc.Block())

        @block.sync
        def _(sp):
            sp.dma_start(PV[:], pv).then_inc(consts_in, 16)
            sp.dma_start(CM[:], cm).then_inc(consts_in, 16)
            ada_sync(sp)
            sp.dma_start(z[:], zin).then_inc(consts_in, 16)
            load_weights(sp)
            sp.wait_ge(acc_lat, NT)
            sp.dma_start(out, z[:, :, LC:T]).then_inc(out_done, 16)
            sp.wait_ge(out_done, 16)

        @block.gpsimd
        def _(pool):
            pool.dma_start(CM0[:], cm0).then_inc(cm0_in, 16)
            attn_pool(pool)
            vk_pool(pool)
            scan_pool(pool)
            post_pool(pool)
            post_zin(pool)

        @block.tensor
        def _(pe):
            pe.wait_ge(consts_in, 32)
            ada_pe(pe)
            norm_pe(pe, 0, SEGS)
            gemm_pe(pe, T_IN, N_IN, SEGS, 0, XH, XL, x_wait=(x_lo, 8))
            ml_gates_pe(pe)
            ml_pe(pe)
            fin_pe(pe)
            attn_pe(pe)
            gemm_pe(pe, T_OUT0, 8, SEGS, T_OUT0, XH, XL, x_wait=(at_lo, 6))
            norm_pe(pe, 1, SEGS)
            mlp(pe, "pe", 0, T_MLP0, SEGS, T_MLP0, (x_lo, 16))
            norm_pe(pe, 2, SEGS)
            for q, (i, t0, n, segs) in enumerate(MIXES):
                gemm_pe(pe, t0, n, segs, t0, XH, XL, x_wait=(x_lo, 24 + 8 * q))
                if q == 0:
                    vk_pe(pe)
            kk_pe(pe)
            scan_pe(pe)
            post_pe(pe)
            gemm_pe(pe, T_OUT1, 8, (LATS,), 0, XH, XL, x_wait=(po_lo, 8))
            norm_pe(pe, 3, (LATS,))
            mlp(pe, "pe", 1, T_MLP1, (LATS,), 0, (x_lo, 72))

        @block.scalar
        def _(act):
            ada_act(act)
            split_hi(0, 0, 0)
            split_hi(1, 0, 1)
            norm_act(act, 0, SEGS, [(consts_in, 48)], True)
            step_act(act, T_IN, N_IN, in_act)
            ml_gates_act(act)
            ml_act(act)
            fin_act(act)
            attn_act(act)
            step_act(act, T_OUT0, 8, None)
            norm_act(act, 1, SEGS, [(acc_lat, T_MLP0), (acc_ctx, T_MLP0)], True)
            mlp(act, "act", 0, T_MLP0, SEGS, T_MLP0, None)
            norm_act(act, 2, SEGS, [(acc_lat, T_V), (acc_ctx, T_V)], False)
            for q, (i, t0, n, segs) in enumerate(MIXES):
                if q == 1:
                    vk_act(act)
                mix_act(act, q)
                if q == 1:
                    act.wait_ge(vt_out, 16)
                    act.wait_ge(vk_t, 8)
                step_act(act, t0, n, mix_evict(q, "act"))
            kk_act(act)
            scan_act(act)
            post_act(act)
            step_act(act, T_OUT1, 8, None)
            norm_act(act, 3, (LATS,), [(acc_lat, T_MLP1)], True)
            mlp(act, "act", 1, T_MLP1, (LATS,), 0, None)

        @block.vector
        def _(dve):
            ada_dve(dve)
            split_lo(0, 0, 0)
            split_lo(1, 0, 1)
            norm_dve(dve, 0, SEGS, [(consts_in, 48)], 0, True)
            step_dve(dve, T_IN, N_IN, in_dve)
            ml_gates_dve(dve)
            ml_dve(dve)
            fin_dve(dve)
            attn_dve(dve)
            step_dve(dve, T_OUT0, 8, res_dve(0, 2, SEGS))
            norm_dve(dve, 1, SEGS, [(acc_lat, T_MLP0), (acc_ctx, T_MLP0)], 8, True)
            mlp(dve, "dve", 0, T_MLP0, SEGS, T_MLP0, None)
            norm_dve(dve, 2, SEGS, [(acc_lat, T_V), (acc_ctx, T_V)], 16, False)
            mu = vec("mu", 0, 96).rearrange("p (i s k) -> p i s k", i=6, s=2)
            nc.vector.scalar_tensor_tensor(out=MC[:], in0=mu[:, :, 0], scalar=-1.0,
                                           in1=mu[:, :, 1], op0=ALU.mult, op1=ALU.subtract
                                           ).then_inc(mc_ready, 1)
            dve.wait_ge(mc_ready, 1)
            nc.vector.tensor_scalar(MC[:], MC[:], 1.0, None, ALU.add).then_inc(mc_ready, 1)
            for q, (i, t0, n, segs) in enumerate(MIXES):
                mix_dve(dve, q)
                if q == 1:
                    dve.wait_ge(vt_out, 16)
                    dve.wait_ge(vk_t, 8)
                step_dve(dve, t0, n, mix_evict(q, "dve"))
            kk_dve(dve)
            scan_dve(dve)
            post_dve(dve)
            dve.wait_ge(z_in, 16)
            step_dve(dve, T_OUT1, 8, res_dve(1, 2, (LATS,)))
            norm_dve(dve, 3, (LATS,), [(acc_lat, T_MLP1)], 64, True)
            mlp(dve, "dve", 1, T_MLP1, (LATS,), 0, None)


def _tiles(w):
    return w.reshape(KT, P, -1, P).transpose(2, 1, 0, 3)


def _cols(v):
    v = v.reshape(-1, P)
    return v.T


GATE_ROWS = np.concatenate([np.arange(4) + r for r in (0, 32, 64, 96)])
GATE_COLS = np.concatenate([np.arange(4) + g for g in (0, 8, 4, 12)])


def pack(a):
    f = np.float32
    a = {k: np.ascontiguousarray(v) for k, v in a.items()}
    zz = np.concatenate([a["ctx"][0], a["x"][0]], 0)
    zin = zz.T.reshape(KT, P, T).transpose(1, 0, 2)
    wi = a["ev_w_in"][0]
    bi = a["ev_b_in"][0]
    gw = np.zeros((D, P), f)
    gb = np.zeros((P,), f)
    gw[:, GATE_ROWS] = wi[:, 2048 + GATE_COLS]
    gb[GATE_ROWS] = bi[2048 + GATE_COLS]
    fb = np.zeros((P,), f)
    fb[[64, 65, 66, 67]] = a["ml_f_bias"][0, 0]
    fb[[96, 97, 98, 99]] = a["ml_f_bias"][0, 1]
    w_in = np.concatenate([wi[:, :2048], gw, wi[:, 2064:]], 1)
    b_in = np.concatenate([bi[:2048], gb, bi[2064:]])

    def mlp(layer):
        w1, w2 = _tiles(a["mlp_w1"][layer]), a["mlp_w2"][layer]
        return [x for g in range(4) for x in (w1[8 * g:8 * g + 8], _tiles(w2[D * g:D * g + D]))]
    g1 = np.concatenate([a["rw_g1"][0], np.zeros((D, 256 - 160), f)], 1)
    rkv = a["rw_w_rkv"][0]
    wall = np.concatenate(
        [_tiles(w_in), _tiles(a["ev_w_out"][0]), *mlp(0), _tiles(rkv[2]), _tiles(rkv[1]),
         _tiles(np.concatenate([a["rw_w1"][0, 0], a["rw_w1"][0, 1]], 1)),
         _tiles(np.concatenate([a["rw_a1"][0, 0], a["rw_a1"][0, 1]], 1)), _tiles(rkv[0]),
         _tiles(g1), _tiles(a["rw_w_out"][0]), *mlp(1)], 0)
    ada = np.concatenate([_tiles(a["ada_w"][0]), _tiles(a["ada_w"][1])], 0)
    cc = np.stack([a["c_ctx"], a["c"][0]], 0).reshape(2, KT, P).transpose(2, 1, 0).reshape(P, 16)
    pv = np.concatenate(
        [cc, _cols(a["ada_b"]), _cols(a["norm1_g"]), _cols(a["norm2_g"]), _cols(b_in),
         fb[:, None], _cols(a["ml_out_g"][0]), np.tile(a["at_q_g"][0], 2)[:, None],
         np.tile(a["at_k_g"][0], 2)[:, None], np.broadcast_to(a["at_sink"][0], (P, 8)),
         _cols(a["rw_mu"][0]), _cols(a["rw_w0"][0]), _cols(a["rw_a0"][0]), _cols(a["rw_k_k"][0]),
         _cols(a["rw_k_a"][0]), _cols(a["rw_r_k"][0]), _cols(a["rw_ln_g"][0]),
         _cols(a["rw_ln_b"][0])], 1)
    lora2 = np.stack([a["rw_w2"][0].reshape(P, D), a["rw_a2"][0].reshape(P, D)], 1)
    g2 = np.zeros((P, 2, D), f)
    g2[:, 0] = a["rw_g2"][0, :P]
    g2[:160 - P, 1] = a["rw_g2"][0, P:]
    return dict(zin=zin, wall=wall, ada=ada, pv=pv, lora2=lora2, g2w=g2, **tables())


def tables():
    f = np.float32
    i = np.arange(P)
    cm = np.concatenate([np.eye(P), np.ones((P, P)), (i[:, None] // 64 == i[None] // 64)], 1)
    perm = np.zeros((P, P))
    for m in range(P):
        if m % 32 < 16:
            perm[m + 16, m] = -1.0
        else:
            perm[m - 16, m] = 1.0
    neg = np.concatenate([np.where(i[:, None] <= i[None], 0, NEG),
                          np.where(i[:, None] >= i[None], 0, NEG)], 1)
    inv = (10000.0 ** (-np.arange(16, dtype=f) / f(16))).astype(f)
    t = np.arange(LAT)
    pos = np.where((i[:, None] % 64) < 32, (t // 64)[None], (t % 64)[None]).astype(f)
    ang = (pos * inv[i % 16][:, None]).astype(f)
    sel = np.zeros((P, 8, P))
    for d in range(2):
        for h in range(4):
            sel[32 * d + h, 4 * d + h] = 1
    reset = np.broadcast_to(np.arange(T) % P != 0, (P, T))
    cm0 = np.concatenate([perm, neg, np.cos(ang), np.sin(ang), sel.reshape(P, -1), reset], 1)
    j, r = np.arange(64), (i % 64)[:, None]
    lvl = [[], []]
    for s in (1, 2, 4, 8, 16, 32):
        pair = r // (2 * s) == j[None] // (2 * s)
        low, high = r % (2 * s) < s, j[None] % (2 * s) >= s
        lvl[0].append(pair & low & high)
        lvl[1].append(pair & ~low & ~high)
    hsel = np.zeros((P, 8, 16))
    hbc = np.zeros((P, 8, P))
    for p in range(8):
        for e in range(2):
            hsel[64 * e:64 * e + 64, p, 2 * p + e] = 1
            hbc[2 * p + e, p, 64 * e:64 * e + 64] = 1
    j = j[None]
    cm1 = np.concatenate([r < j, r > j, r <= j, r >= j, *lvl[0], *lvl[1], r == j,
                          np.broadcast_to(np.arange(512) % 64 != 0, (P, 512)),
                          hsel.reshape(P, -1), hbc.reshape(P, -1)], 1)
    return {"cm": cm.astype(f), "cm0": cm0.astype(f), "cm1": cm1.astype(f)}


SCRATCH = [("z_dram", (P, KT, LAT)), ("vt_dram", (P, KT, LAT)), ("vk_dram", (T, D)),
           ("y_dram", (2, P, KT, LAT))]


def kernel(**inputs):
    import concourse.bacc as _bacc
    from concourse.bass_utils import run_bass_kernel_spmd as _run

    packed = {k: np.ascontiguousarray(v, dtype=np.float32)
              for k, v in pack({k: np.asarray(v) for k, v in inputs.items()}).items()}
    nc = _bacc.Bacc("TRN2", target_bir_lowering=False, num_devices=1)
    dram = {k: nc.dram_tensor(f"{k}_dram", v.shape, F32, kind="ExternalInput").ap()
            for k, v in packed.items()}
    scratch = {k: nc.dram_tensor(k, shape, F32, kind="Internal").ap() for k, shape in SCRATCH}
    out = nc.dram_tensor("out_dram", (P, KT, LAT), F32, kind="ExternalOutput").ap()
    trunk(nc, out=out, **dram, **scratch)
    r = _run(nc, [{f"{k}_dram": v for k, v in packed.items()}], core_ids=[0])
    y = r.results[0]["out_dram"]
    return np.ascontiguousarray(y.transpose(2, 1, 0)).reshape(1, LAT, D)
```

```python
from contextlib import ExitStack

import numpy as np

import concourse.bass as bass
from concourse import mybir

F32 = mybir.dt.float32
F32R = mybir.dt.float32r
U32 = mybir.dt.uint32
ALU = mybir.AluOpType
ACT = mybir.ActivationFunctionType
AX = mybir.AxisListType

P = 128
D = 1024
KT = D // P
LC = 256
LAT = 512
T = LC + LAT
EPS = 1e-6
LN_EPS = 64e-5
CAP = 15.0
NEG = -1e30
KAPPA = float(np.exp(-0.5))
L = 64
SEGS = ((0, LC), (LC, LAT))
CTX, LATS = SEGS

N_IN = 23
T_IN = 0
T_OUT0 = T_IN + N_IN
T_MLP0 = T_OUT0 + 8
T_V = T_MLP0 + 64
T_K = T_V + 8
T_W = T_K + 8
T_A = T_W + 1
T_R = T_A + 1
T_G = T_R + 8
T_OUT1 = T_G + 2
T_MLP1 = T_OUT1 + 8
NT = T_MLP1 + 64


def offsets(table):
    at, n = {}, 0
    for name, width in table:
        at[name] = n
        n += width
    return at, n


VOFF, NV = offsets([("c", 16), ("ada_b", 96), ("g1", 16), ("g2", 16), ("b_in", N_IN), ("fb", 1),
                    ("out_g", 4), ("q_g", 1), ("k_g", 1), ("sink", 8), ("mu", 96), ("w0", 16),
                    ("a0", 16), ("k_k", 8), ("k_a", 8), ("r_k", 8), ("ln_g", 8), ("ln_b", 8)])
COFF, NC = offsets([("ident", 128), ("ones", 128), ("bd", 128)])
C0OFF, NC0 = offsets([("perm", 128), ("neg", 256), ("cos", 512), ("sin", 512), ("sel", 1024),
                      ("reset", 768)])
C1OFF, NC1 = offsets([("tri", 256), ("lvl", 768), ("eye", 64),
                      ("reset", 512), ("hsel", 128), ("hbc", 1024)])


def trunk(nc, zin, wall, ada, pv, cm, cm0, cm1, lora2, g2w, out, z_dram, vt_dram, vk_dram,
          y_dram, mod_dram):
    ctx = ExitStack()
    with ctx:
        BASE = 16512

        def at(name, kb, shape, dt=F32):
            return nc.alloc_sbuf_tensor_at(name, shape, dt, offset=BASE + int(kb * 1024))

        def sem(name):
            return ctx.enter_context(nc.semaphore(name))

        z = at("z", 0, [P, KT, T])
        WR = at("WR", 24, [P, 2, KT, P])
        WH = at("WH", 32, [P, 2, KT, P], F32R)
        WL = at("WL", 40, [P, 2, KT, P], F32R)
        PV = at("PV", 48, [P, NV])
        MOD = at("MOD", 50, [P, 2, 48, 2])
        CO = at("CO", 50.75, [P, 80])
        CM = at("CM", 51.125, [P, NC])
        CM1 = at("CM1", 53, [P, NC1 - D])
        RA = 62
        RB = RA + 48
        XH = at("XH", RA, [P, KT, T], F32R)
        XL = at("XL", RA + 24, [P, KT, T], F32R)
        ps = ctx.enter_context(nc.psum_tensor("ps", [P, 8, 512], F32))
        SILU = at("SILU", 51.0625, [P, 16])
        SG = at("SG", 52.625, [P, 32])
        ADA = at("ADA", RA, [P, 3, 4, KT, P])
        ROW = at("ROW", RB + 40, [2, 6 * D])
        ROWT = at("ROWT", 60, [96, P])
        ADB = at("ADB", RB + 69, [P, 2, KT, P])
        ROWB = at("ROWB", RB + 77, [2, D])
        NS = [{k: at(f"{k}{i}", o + b, s) for k, b, s in (
            ("SQ", 0, [P, 2, T]), ("ACC", 6, [P, T]), ("STD", 9, [P, T]), ("RS", 12, [P, T]),
            ("TM", 15, [P, 2, T]), ("HF", 21, [P, 2, T]))}
            for i, o in enumerate((RB, RB + 60, RB + 25))]
        Q = at("Q", RB, [P, N_IN, T])
        H = at("H", RB + 69, [P, 4, T])
        CM0 = at("CM0", RB + 81, [P, NC0])
        N5 = at("N5", RA, [64, 5, T])
        R5 = at("R5", RA + 15, [64, 5, T])
        BC = at("BC", RA + 30, [64, T])
        GM = at("GM", RA + 33, [64, T])
        IG = at("IG", RA + 36, [64, T])
        LF = at("LF", RA + 39, [64, T])
        GX = at("GX", RA + 42, [P, T])
        GF = at("GF", RA + 45, [64, T])
        MM = at("MM", 52.75, [64, 8])
        KVT = at("KVT", RA + 15, [P, 8, P])
        KVK = at("KVK", RA + 19, [P, 8, P])
        EE = at("EE", RA + 23, [P, 4, P])
        IW = at("IW", RA + 25, [P, 4, P])
        FL = at("FL", RA + 27, [P, 4, P])
        WM = at("WM", RA + 29, [P, 4, P])
        QT = at("QT", RA + 31, [P, 4, P])
        VW = at("VW", RA + 33, [P, 4, P + 1])
        YM = at("YM", RA + 35.25, [P, 4, P])
        CT = at("CT", RA + 37.25, [P, 2, 4, P + 1])
        NR = at("NR", RA + 41.5, [P, 4, P])
        CS = at("CS", RA + 43.5, [P, 6, 64])
        CW = at("CW", RA + 45, [P, 6, 64])

        def vec(name, j=0, n=1):
            return PV[:, VOFF[name] + j:VOFF[name] + j + n]

        def vecd(name, j):
            return PV[:, bass.ds(j + VOFF[name], 1)]

        def cmat(name, n=128):
            return CM[:, COFF[name]:COFF[name] + n]

        def c0(name, a, n):
            return CM0[:, C0OFF[name] + a:C0OFF[name] + a + n]

        def c1(name, a, n):
            return CM1[:, C1OFF[name] + a:C1OFF[name] + a + n]

        ident, ones, bd = cmat("ident"), cmat("ones"), cmat("bd")

        consts_in = sem("consts_in")
        cm0_in = sem("cm0_in")
        ada_in = [sem(f"ada_in{j}") for j in range(3)]
        adb_in = [sem(f"adb_in{j}") for j in range(2)]
        silu = sem("silu")
        ada_done, ada_row, rowt_in, mod_t = (sem("ada_done"), sem("ada_row"), sem("rowt_in"),
                                             sem("mod_t"))
        adb_done, adb_row, mod_out = sem("adb_done"), sem("adb_row"), sem("mod_out")
        mod_ready = sem("mod_ready")
        w_in = [sem("w_in0"), sem("w_in1")]
        w_hi, w_lo, tile_done = sem("w_hi"), sem("w_lo"), sem("tile_done")
        acc_lat, acc_ctx = sem("acc_lat"), sem("acc_ctx")
        n_sq, n_acc, n_stat, n_std = sem("n_sq"), sem("n_acc"), sem("n_stat"), sem("n_std")
        n_tm, n_h = sem("n_tm"), sem("n_h")
        x_hi, x_lo = sem("x_hi"), sem("x_lo")
        hid_sq, hid_hi, hid_lo = sem("hid_sq"), sem("hid_hi"), sem("hid_lo")
        out_done = sem("out_done")
        waits_seen = sem("waits_seen")
        X_COUNT = {"norm0": 0}

        def seg(x, s):
            return x[s[0]:s[0] + s[1]]

        def tile_loop(eng, t0, n, body, peel=0):
            for m in range(min(peel, n)):
                body(t0 + m, (t0 + m) // 2, m, (t0 + m) % 2)
            pairs = (n - peel) // 2
            if pairs > 1:
                with eng.Fori(0, pairs) as i:
                    for j in range(2):
                        b = t0 + peel + j
                        body(i * 2 + b, i + b // 2, i * 2 + (peel + j), b % 2)
            else:
                pairs = 0
            for m in range(peel + 2 * pairs, n):
                body(t0 + m, (t0 + m) // 2, m, (t0 + m) % 2)

        def load_weights(sp):
            for t in range(2):
                sp.dma_start(WR[:, t], wall[t]).then_inc(w_in[t % 2], 16)

            def body(t, half, m, s):
                sp.wait_ge(w_hi, t - 1)
                sp.wait_ge(w_lo, t - 1)
                sp.dma_start(WR[:, s], wall[bass.ds(t, 1)].rearrange("a p k m -> (a p) k m")
                             ).then_inc(w_in[s], 16)

            def until(a, b):
                tile_loop(sp, a, b - a, body)
            until(2, T_OUT0 + 4)
            adb_sync(sp)
            until(T_OUT0 + 4, T_OUT1 + 4)
            scan_sync(sp)
            until(T_OUT1 + 4, NT)

        def split_hi(t, half, s, first=False):
            nc.scalar.wait_ge(w_in[s], (half + 1) * 16)
            nc.scalar.activation(WH[:, s], WR[:, s], ACT.Copy).then_inc(w_hi, 1)

        def split_lo(t, half, s):
            nc.vector.wait_ge(w_in[s], (half + 1) * 16)
            nc.vector.wait_ge(w_hi, t + 1)
            nc.vector.tensor_tensor(WL[:, s], WR[:, s], WH[:, s].bitcast(F32),
                                    ALU.subtract).then_inc(w_lo, 1)

        def gemm_pe(pe, t0, n, segs, c_before, xh, xl, x_wait=None, last_wait=None):
            def body(t, half, m, s):
                if x_wait is not None:
                    pe.wait_ge(*x_wait)
                pe.wait_ge(w_hi, t + 1)
                pe.wait_ge(w_lo, t + 1)
                if not isinstance(t, int) or t >= 2:
                    pe.wait_ge(acc_lat, t - 1)
                if CTX in segs:
                    cc = c_before + m - 1
                    if not isinstance(cc, int) or cc >= 1:
                        pe.wait_ge(acc_ctx, cc)
                for k in range(KT):
                    if k == KT - 1 and last_wait is not None:
                        pe.wait_ge(*last_wait)
                    for a, b, first in ((WH, xh, True), (WH, xl, False), (WL, xh, False)):
                        for sg in segs:
                            bank = 2 * s + (0 if sg is LATS else 1)
                            mm = nc.tensor.matmul(
                                ps[:, bank, 0:sg[1]], a[:, s, k], b[:, k, sg[0]:sg[0] + sg[1]],
                                start=(k == 0 and first), stop=(k == KT - 1 and a is WL))
                mm.then_inc(tile_done, 1)
            tile_loop(pe, t0, n, body, peel=2 if t0 == 0 else 0)

        def acc(s, sg):
            return ps[:, 2 * s + (0 if sg is LATS else 1), 0:sg[1]]

        def step_act(act, t0, n, evict, peel=0):
            def body(t, half, m, s):
                act.wait_ge(tile_done, t + 1)
                if evict is not None:
                    evict(t, m, s)
                if not isinstance(t, int) or t + 2 < NT:
                    split_hi(t + 2, half + 1, s)
            lim = max(0, min(n, NT - 2 - t0))
            tile_loop(act, t0, lim, body, peel)
            for m in range(lim, n):
                body(t0 + m, (t0 + m) // 2, m, (t0 + m) % 2)

        def step_dve(dve, t0, n, evict, peel=0):
            def body(t, half, m, s):
                dve.wait_ge(tile_done, t + 1)
                if evict is not None:
                    evict(t, m, s)
                if not isinstance(t, int) or t + 2 < NT:
                    split_lo(t + 2, half + 1, s)
            lim = max(0, min(n, NT - 2 - t0))
            tile_loop(dve, t0, lim, body, peel)
            for m in range(lim, n):
                body(t0 + m, (t0 + m) // 2, m, (t0 + m) % 2)


        def ada_sync(sp):
            def group(g, slot):
                sp.dma_start(ADA[:, slot], ada[bass.ds(g * 4, 4)].rearrange(
                    "a p k m -> p a k m")).then_inc(ada_in[slot], 16)
            for j in range(3):
                group(j, j)
            with sp.Fori(1, 4) as i:
                for j in range(3):
                    sp.wait_ge(ada_done, i * 3 + (j - 2))
                    group(i * 3 + j, j)

        def ada_pe(pe):
            pe.wait_ge(silu, 3)
            with pe.Fori(0, 2) as i:
                for g in range(6):
                    pe.wait_ge(ada_in[g % 3], i * 32 + (16 + 16 * (g // 3)))
                    if g >= 2:
                        pe.wait_ge(ada_row, i * 6 + (g - 1))
                    else:
                        pe.wait_ge(ada_row, i * (5 + g))
                    for k in range(KT):
                        mm = nc.tensor.matmul(ps[0:2, 4 + g % 2], SILU[:, 2 * k:2 * k + 2],
                                              ADA[:, g % 3, :, k], start=k == 0,
                                              stop=k == KT - 1)
                    mm.then_inc(ada_done, 1)

        def ada_pool(pool):
            pool.wait_ge(ada_row, 12)
            pool.dma_start(mod_dram[0], ROW[:]).then_inc(mod_out, 16)
            pool.wait_ge(mod_out, 16)
            pool.dma_start(ROWT[:], mod_dram[0].rearrange("c (m n) -> (c m) n", n=P)
                           ).then_inc(rowt_in, 16)

        def mod_pe(pe, layer):
            pe.wait_ge(rowt_in, 16 * layer + 16)
            nc.tensor.transpose(ps[:, 4, 0:96], ROWT[:], ident[0:96, 0:96]).then_inc(mod_t, 1)

        def ada_act(act):
            act.wait_ge(consts_in, 32)
            nc.scalar.activation(SG[:, 0:16], vec("c", 0, 16), ACT.Tanh, scale=0.5
                                 ).then_inc(silu, 1)
            with act.Fori(0, 6) as i:
                for s in range(2):
                    act.wait_ge(ada_done, i * 2 + (s + 1))
                    nc.scalar.activation(ROW[:, bass.ds(i * 1024 + 512 * s, 512)],
                                         ps[0:2, 4 + s], ACT.Copy).then_inc(ada_row, 1)

        def ada_dve(dve):
            dve.wait_ge(consts_in, 32)
            dve.wait_ge(silu, 1)
            nc.vector.tensor_scalar(SG[:, 16:32], SG[:, 0:16], 0.5, 0.5, ALU.mult, ALU.add
                                    ).then_inc(silu, 1)
            dve.wait_ge(silu, 2)
            nc.vector.tensor_tensor(SILU[:], SG[:, 16:32], vec("c", 0, 16), ALU.mult
                                    ).then_inc(silu, 1)
            nc.vector.memset(CO[:, 64:65], EPS).then_inc(mod_ready, 1)
            nc.vector.memset(CO[:, 65:66], LN_EPS).then_inc(mod_ready, 1)
            nc.vector.memset(CO[:, 66:67], 1.0).then_inc(mod_ready, 1)

        def mod_dve(dve, layer):
            dve.wait_ge(mod_t, layer + 1)
            nc.vector.tensor_tensor(
                MOD[:, layer], ps[:, 4, 0:96].rearrange("p (c m) -> p m c", c=2),
                vec("ada_b", 48 * layer, 48)[:, :, None].broadcast_to([P, 48, 2]), ALU.add
                ).then_inc(mod_ready, 1)
            dve.wait_ge(mod_ready, 4 + 3 * layer)
            for n in (2 * layer, 2 * layer + 1):
                sc = MOD[:, layer, 8 + 24 * (n % 2):16 + 24 * (n % 2), :]
                g = vec("g1" if n % 2 == 0 else "g2", 8 * layer, 8)
                nc.vector.scalar_tensor_tensor(
                    out=CO[:, 16 * n:16 * n + 16].rearrange("p (k c) -> p k c", c=2), in0=sc,
                    scalar=1.0, in1=g[:, :, None].broadcast_to([P, 8, 2]), op0=ALU.add,
                    op1=ALU.mult).then_inc(mod_ready, 1)

        def adb_sync(sp):
            sp.wait_ge(fin_lo, 4)
            for j in range(2):
                sp.dma_start(ADB[:, j], ada[48 + j]).then_inc(adb_in[j], 16)
            with sp.Fori(1, 24) as i:
                for j in range(2):
                    sp.wait_ge(adb_done, i * 2 + (j - 1))
                    sp.dma_start(ADB[:, j], ada[bass.ds(i * 2 + (48 + j), 1)].rearrange(
                        "a p k m -> (a p) k m")).then_inc(adb_in[j], 16)

        def adb_pe(pe, b, h):
            pe.wait_ge(adb_in[h % 2], b * 64 + (16 * (h // 2) + 16))
            if h == 4:
                pe.wait_ge(adb_row, b * 2 + 1)
            for k in range(KT):
                mm = nc.tensor.matmul(ps[0:2, 7, P * (h % 4):P * (h % 4) + P],
                                      SILU[:, 2 * k:2 * k + 2], ADB[:, h % 2, k],
                                      start=k == 0, stop=k == KT - 1)
            mm.then_inc(adb_done, 1)

        def adb_dve(dve, b, half):
            dve.wait_ge(adb_done, b * 8 + (4 * half + 4))
            nc.vector.tensor_copy(ROWB[:, 512 * half:512 * half + 512], ps[0:2, 7]
                                  ).then_inc(adb_row, 1)

        def norm_pe(pe, n, segs):
            pe.wait_ge(n_acc, 8 * n + 8)
            for sg in segs:
                mm = nc.tensor.matmul(ps[:, 6 if sg is LATS else 7, 0:sg[1]], ones,
                                      NS[NSI[n]]["ACC"][:, sg[0]:sg[0] + sg[1]], start=True,
                                      stop=True)
            mm.then_inc(n_stat, 1)

        NSI = {0: 0, 1: 1, 2: 2, 3: 1}
        ZA = {0: 0, 1: 0, 2: 0, 3: LC}

        def norm_act(act, n, segs, z_wait, split):
            B = NS[NSI[n]]
            a = ZA[n]
            for w in z_wait:
                act.wait_ge(*w)
            for k in range(KT):
                if k >= 2:
                    act.wait_ge(n_acc, 8 * n + k - 1)
                nc.scalar.activation(B["SQ"][:, k % 2, a:T], z[:, k, a:T], ACT.Square
                                     ).then_inc(n_sq, 1)
            act.wait_ge(n_stat, n + 1)
            act.wait_ge(mod_ready, 6 if n < 2 else 9)
            for sg in segs:
                nc.scalar.activation(B["STD"][:, sg[0]:sg[0] + sg[1]],
                                     ps[:, 6 if sg is LATS else 7, 0:sg[1]], ACT.Sqrt,
                                     bias=CO[:, 64:65], scale=1.0 / D).then_inc(n_std, 1)
            if split:
                for k in range(KT):
                    act.wait_ge(n_h, 8 * n + k + 1)
                    nc.scalar.activation(XH[:, k, a:T], B["HF"][:, k % 2, a:T], ACT.Copy
                                         ).then_inc(x_hi, 1)

        def norm_dve(dve, n, segs, z_wait, x0, split):
            B = NS[NSI[n]]
            a = ZA[n]
            for w in z_wait:
                dve.wait_ge(*w)
            if not split:
                for c in (1, 258, 259, T + 4):
                    nc.vector.memset(U[:, :, c:c + 1], 0.0)
            for k in range(KT):
                dve.wait_ge(n_sq, 8 * n + k + 1)
                if k == 0:
                    nc.vector.tensor_copy(B["ACC"][:, a:T], B["SQ"][:, 0, a:T]).then_inc(n_acc, 1)
                else:
                    dve.wait_ge(n_acc, 8 * n + k)
                    nc.vector.tensor_tensor(B["ACC"][:, a:T], B["ACC"][:, a:T],
                                            B["SQ"][:, k % 2, a:T], ALU.add).then_inc(n_acc, 1)
            dve.wait_ge(n_std, NSTD[n] + len(segs))
            nc.vector.reciprocal(B["RS"][:, a:T], B["STD"][:, a:T]).then_inc(n_tm, 1)
            dve.wait_ge(n_tm, 9 * n + 1)
            sh = 24 * (n % 2)
            for k in range(KT):
                if k >= 2:
                    dve.wait_ge(n_h, 8 * n + k - 1)
                nc.vector.tensor_tensor(B["TM"][:, k % 2, a:T], z[:, k, a:T], B["RS"][:, a:T],
                                        ALU.mult).then_inc(n_tm, 1)
                dve.wait_ge(n_tm, 9 * n + k + 2)
                if split and k >= 2:
                    dve.wait_ge(x_hi, x0 + k - 1)
                    dve.wait_ge(x_lo, x0 + k - 1)
                for i, sg in enumerate(segs):
                    v = SEGS.index(sg)
                    if split:
                        o = B["HF"][:, k % 2, sg[0]:sg[0] + sg[1]]
                    else:
                        o = U[:, k, 2 + 2 * v + sg[0]:2 + 2 * v + sg[0] + sg[1]]
                    ins = nc.vector.tensor_scalar(
                        o, B["TM"][:, k % 2, sg[0]:sg[0] + sg[1]],
                        CO[:, 16 * n + 2 * k + v:16 * n + 2 * k + v + 1],
                        MOD[:, n // 2, sh + k, v:v + 1], ALU.mult, ALU.add)
                ins.then_inc(n_h, 1)
                if split:
                    dve.wait_ge(n_h, 8 * n + k + 1)
                    dve.wait_ge(x_hi, x0 + k + 1)
                    nc.vector.tensor_tensor(XL[:, k, a:T], B["HF"][:, k % 2, a:T],
                                            XH[:, k, a:T].bitcast(F32), ALU.subtract
                                            ).then_inc(x_lo, 1)

        NSTD = {0: 0, 1: 2, 2: 4, 3: 6}
        U = at("U", RB, [P, KT, T + 6])

        def in_act(t, m, s):
            nc.scalar.activation(q_lat(m), acc(s, LATS), ACT.Identity,
                                 bias=vecd("b_in", m)).then_inc(acc_lat, 1)

        def in_dve(t, m, s):
            nc.vector.tensor_scalar(q_ctx(m), acc(s, CTX), vecd("b_in", m), None, ALU.add
                                    ).then_inc(acc_ctx, 1)

        def q_lat(m):
            return Q[:, bass.ds(m, 1), LC:T]

        def q_ctx(m):
            return Q[:, bass.ds(m, 1), 0:LC]

        def res_dve(layer, gate, segs):
            def evict(t, m, s):
                nc.vector.wait_ge(acc_lat, t)
                for sg in segs:
                    v = SEGS.index(sg)
                    zz = z[:, bass.ds(m, 1), sg[0]:sg[0] + sg[1]].rearrange("p a t -> p (a t)")
                    nc.vector.scalar_tensor_tensor(
                        out=zz, in0=acc(s, sg),
                        scalar=MOD[:, layer, bass.ds(m + 8 * gate, 1), v:v + 1].rearrange(
                            "p a b -> p (a b)"), in1=zz, op0=ALU.mult, op1=ALU.add
                        ).then_inc(acc_lat if sg is LATS else acc_ctx, 1)
            return evict

        HH = at("HH", RB, [P, KT, T], F32R)
        HL = at("HL", RB + 24, [P, KT, T], F32R)
        HR = at("HR", RB + 48, [P, 2, T])
        HS_ = at("HS_", RB + 54, [P, 2, T])

        def mlp(eng, which, layer, t0, segs, c0_, x_ready):
            a = 0 if CTX in segs else LC

            def up_act(hb):
                def evict(t, m, s):
                    n = m + hb
                    if not isinstance(n, int) or n >= 2:
                        nc.scalar.wait_ge(hid_sq, n - 1)
                    if CTX in segs:
                        nc.scalar.activation(HR[:, s, 0:LC], acc(s, CTX), ACT.Relu
                                             ).then_inc(acc_ctx, 1)
                    nc.scalar.activation(HR[:, s, LC:T], acc(s, LATS), ACT.Relu
                                         ).then_inc(acc_lat, 1)
                    nc.scalar.wait_ge(hid_sq, n + 1)
                    nc.scalar.activation(hh(HH, m), HS_[:, s, a:T], ACT.Copy
                                         ).then_inc(hid_hi, 1)
                return evict

            def up_dve(hb):
                def evict(t, m, s):
                    n = m + hb
                    nc.vector.wait_ge(acc_lat, t + 1)
                    if not isinstance(n, int) or n >= 2:
                        nc.vector.wait_ge(hid_hi, n - 1)
                        nc.vector.wait_ge(hid_lo, n - 1)
                    nc.vector.tensor_tensor(HS_[:, s, a:T], HR[:, s, a:T], HR[:, s, a:T],
                                            ALU.mult).then_inc(hid_sq, 1)
                    nc.vector.wait_ge(hid_hi, n + 1)
                    nc.vector.tensor_tensor(hh(HL, m), HS_[:, s, a:T], hh(HH, m).bitcast(F32),
                                            ALU.subtract).then_inc(hid_lo, 1)
                return evict

            def hh(x, m):
                return x[:, bass.ds(m, 1), a:T].rearrange("p a t -> p (a t)")

            for g in range(4):
                hb = 32 * layer + 8 * g + 2 * 0
                tu, td = t0 + 16 * g, t0 + 16 * g + 8
                cu = c0_ + 16 * g
                if which == "pe":
                    gemm_pe(eng, tu, 8, segs, cu, XH, XL, x_wait=x_ready)
                    gemm_pe(eng, td, 8, segs, cu + 8, HH, HL, x_wait=(hid_lo, hb + 7),
                            last_wait=(hid_lo, hb + 8))
                elif which == "act":
                    step_act(eng, tu, 8, up_act(hb), peel=2 if hb == 0 else 0)
                    step_act(eng, td, 8, None)
                else:
                    step_dve(eng, tu, 8, up_dve(hb), peel=2 if hb == 0 else 0)
                    step_dve(eng, td, 8, res_dve(layer, 5, segs))

        ml_gx, ml_gf, ml_sc, ml_g, ml_nat = (sem("ml_gx"), sem("ml_gf"), sem("ml_sc"),
                                             sem("ml_g"), sem("ml_nat"))
        ml_colp, ml_col = sem("ml_colp"), sem("ml_col")
        ml_kvt, ml_tr, ml_kvk = sem("ml_kvt"), sem("ml_tr"), sem("ml_kvk")
        ml_bc, ml_exp, ml_w, ml_vw = sem("ml_bc"), sem("ml_exp"), sem("ml_w"), sem("ml_vw")
        ml_num, ml_cn, ml_y, ml_ct, ml_nr = (sem("ml_num"), sem("ml_cn"), sem("ml_y"),
                                             sem("ml_ct"), sem("ml_nr"))
        ml_init = sem("ml_init")
        fin_sq, fin_st, fin_sd, fin_o, fin_y, fin_hi = (sem("fin_sq"), sem("fin_st"),
                                                        sem("fin_sd"), sem("fin_o"),
                                                        sem("fin_y"), sem("fin_hi"))
        fin_lo = sem("fin_lo")
        ORDER = [(0, 2, 1), (2, 6, 7)]

        def ml_gates_act(act):
            act.wait_ge(acc_lat, N_IN)
            act.wait_ge(acc_ctx, N_IN)
            act.wait_ge(ml_sc, 1)
            nc.scalar.activation(GX[:], Q[:, 16], ACT.Tanh, bias=CO[:, 67:68], scale=1.0 / CAP
                                 ).then_inc(ml_gx, 1)
            act.wait_ge(ml_gx, 1)
            act.wait_ge(cm0_in, 16)
            act.dma_start(GF[:], GX[64:128]).then_inc(ml_gf, 16)
            act.wait_ge(ml_gf, 16)
            nc.scalar.activation(GM[:], GF[:], ACT.Exp, scale=-CAP).then_inc(ml_gx, 1)
            act.wait_ge(ml_gx, 2)
            nc.scalar.activation(BC[:], GM[:], ACT.Ln, bias=CO[0:64, 66:67]).then_inc(ml_gx, 1)
            act.wait_ge(ml_colp, 12)
            pcol = ps[:, 6:8].rearrange("p a b -> p (a b)")
            nc.scalar.activation(CW[:], pcol[:, 384:768].rearrange("p (c r) -> p c r", c=6),
                                 ACT.Exp).then_inc(ml_col, 1)
            nc.scalar.activation(CS[:], pcol[:, 0:384].rearrange("p (c r) -> p c r", c=6),
                                 ACT.Copy).then_inc(ml_col, 1)

        def ml_gates_dve(dve):
            nc.vector.tensor_scalar(CO[:, 67:68], vec("fb"), 1.0 / CAP, None, ALU.mult
                                    ).then_inc(ml_sc, 1)
            dve.wait_ge(ml_gx, 3)
            nc.vector.tensor_scalar(IG[0:32], GX[0:32], CAP, None, ALU.mult).then_inc(ml_sc, 1)
            nc.vector.tensor_scalar(LF[0:32], BC[0:32], -1.0, None, ALU.mult).then_inc(ml_sc, 1)
            for sg in SEGS:
                a, b = sg[0], sg[0] + sg[1]
                nc.vector.tensor_scalar(IG[32:64, a:b], GX[32:64, a:b][:, ::-1], CAP, None,
                                        ALU.mult).then_inc(ml_sc, 1)
                nc.vector.tensor_scalar(LF[32:64, a:b], BC[32:64, a:b][:, ::-1], -1.0, None,
                                        ALU.mult).then_inc(ml_sc, 1)
            dve.wait_ge(ml_sc, 7)
            dve.wait_ge(cm0_in, 16)
            nc.vector.tensor_tensor_scan(BC[:], c0("reset", 0, T)[0:64], LF[:], 0.0, ALU.mult,
                                         ALU.add).then_inc(ml_g, 1)
            nc.vector.memset(MM[:, 0:1], 0.0).then_inc(ml_g, 1)
            dve.wait_ge(ml_g, 2)
            nc.vector.tensor_tensor(R5[:, 3], IG[:], BC[:], ALU.subtract).then_inc(ml_g, 1)
            dve.wait_ge(ml_g, 3)
            for c in range(6):
                a, b = 128 * c, 128 * c + 128
                nc.vector.tensor_tensor_scan(GM[:, a:b], R5[:, 3, a:b], R5[:, 3, a:b],
                                             MM[:, c:c + 1], ALU.max, ALU.max).then_inc(ml_g, 1)
                dve.wait_ge(ml_g, 4 + 2 * c)
                nc.vector.tensor_tensor(MM[:, c + 1:c + 2], BC[:, b - 1:b], GM[:, b - 1:b],
                                        ALU.add).then_inc(ml_g, 1)
                dve.wait_ge(ml_g, 5 + 2 * c)
            nc.vector.tensor_scalar(R5[:, 0], GM[:], -1.0, None, ALU.mult).then_inc(ml_g, 1)
            nc.vector.scalar_tensor_tensor(out=R5[:, 2], in0=BC[:], scalar=-1.0, in1=GM[:],
                                           op0=ALU.mult, op1=ALU.subtract).then_inc(ml_g, 1)
            for c in range(6):
                a, b = 128 * c, 128 * c + 128
                nc.vector.tensor_scalar(R5[:, 1, a:b], GM[:, a:b], -1.0, MM[:, c:c + 1],
                                        ALU.mult, ALU.add).then_inc(ml_g, 1)
                nc.vector.tensor_scalar(R5[:, 4, a:b], R5[:, 3, a:b], GM[:, b - 1:b], None,
                                        ALU.subtract).then_inc(ml_g, 1)
            dve.wait_ge(ml_g, 29)
            nc.vector.tensor_copy(N5[0:32], R5[0:32]).then_inc(ml_nat, 1)
            for sg in SEGS:
                a, b = sg[0], sg[0] + sg[1]
                nc.vector.tensor_copy(N5[32:64, :, a:b], R5[32:64, :, a:b][:, :, ::-1]
                                      ).then_inc(ml_nat, 1)
            nc.vector.tensor_scalar(Q[:, 0:4], Q[:, 0:4], float(P) ** -0.5, None, ALU.mult
                                    ).then_inc(ml_init, 1)
            nc.vector.memset(H[:], 0.0).then_inc(ml_init, 1)
            dve.wait_ge(ml_nat, 3)
            nc.vector.memset(CT[:], 0.0).then_inc(ml_init, 1)

        def ml_gates_pe(pe):
            pe.wait_ge(ml_nat, 3)
            pcol = ps[:, 6:8].rearrange("p a b -> p (a b)")
            for r in range(2):
                for c in range(6):
                    o = 384 * r + 64 * c
                    nc.tensor.transpose(pcol[:, o:o + 64], N5[:, 3 + r, 128 * c:128 * c + 128],
                                        ident[0:64, 0:64]).then_inc(ml_colp, 1)

        def chunks(eng, body):
            for lo, hi, flip in ORDER:
                with eng.Fori(0, hi - lo) as i:
                    for d in range(2):
                        c = eng.snap(i + lo if d == 0 else i * -1 + (flip - lo))
                        body(i * 2 + (2 * lo + d), d, c, eng.snap(c * P))

        def ml_pe(pe):
            pe.wait_ge(ml_col, 2)
            pe.wait_ge(ml_init, 4)

            def body(u, d, c, off):
                tok = bass.ds(off, P)
                pe.wait_ge(ml_kvt, u + 1)
                pe.wait_ge(ml_ct, u * 4)
                for j in range(8):
                    mm = nc.tensor.transpose(ps[:, j // 4, P * (j % 4):P * (j % 4) + P],
                                             KVT[:, j], ident)
                mm.then_inc(ml_tr, 1)
                pe.wait_ge(ml_w, u)
                pe.wait_ge(ml_exp, u * 6)
                for h in range(4):
                    nc.tensor.matmul(ps[:, 5, P * h:P * h + P], KVT[:, h], Q[:, h, tok],
                                     start=True, stop=True)
                for r, bank in ((0, 2), (1, 3), (2, 4)):
                    for h in range(4):
                        o = ps[:, bank, P * h:P * h + P]
                        mm = nc.tensor.matmul(
                            o, c0("sel", P * (4 * d + h), P)[0:64], N5[:, r, tok], start=True,
                            stop=(r != 0))
                        if r == 0:
                            nc.tensor.matmul(o, ident, c0("neg", P * d, P), start=False,
                                             stop=True)
                mm.then_inc(ml_bc, 1)
                pe.wait_ge(ml_kvk, u + 1)
                pe.wait_ge(ml_vw, u + 1)
                pe.wait_ge(ml_y, u)
                for h in range(4):
                    o = ps[:, 6, P * h:P * h + P]
                    nc.tensor.matmul(o, KVK[:, 4 + h], WM[:, h], start=True, stop=False)
                    nc.tensor.matmul(o, CT[:, d, h, 0:P], QT[:, h], start=False, stop=True)
                nc.tensor.matmul(ps[:, 7, :], ones, WM[:].rearrange("p h t -> p (h t)"),
                                 start=True, stop=False)
                pe.wait_ge(ml_nr, u + 1)
                for h in range(4):
                    mm = nc.tensor.matmul(ps[:, 7, P * h:P * h + P], NR[:, h], QT[:, h],
                                          start=False, stop=(h == 3))
                mm.then_inc(ml_num, 1)
                for h in range(4):
                    mm = nc.tensor.matmul(ps[:, h // 2, (P + 1) * (h % 2):(P + 1) * (h % 2) + P + 1],
                                          KVK[:, h], VW[:, h], start=True, stop=True)
                mm.then_inc(ml_cn, 1)
            chunks(pe, body)

        def ml_act(act):
            act.wait_ge(ml_init, 4)

            def body(u, d, c, off):
                act.wait_ge(ml_num, u)
                nc.scalar.activation(KVT[:], Q[:, 4:12, bass.ds(off, P)], ACT.Copy
                                     ).then_inc(ml_kvt, 1)
                act.wait_ge(ml_tr, u + 1)
                act.wait_ge(ml_cn, u)
                nc.scalar.activation(KVK[:].rearrange("p j t -> p (j t)"),
                                     ps[:, 0:2].rearrange("p a b -> p (a b)"), ACT.Copy
                                     ).then_inc(ml_kvk, 1)
                act.wait_ge(ml_ct, u * 4)
                nc.scalar.activation(NR[:], CT[:, d, :, P:P + 1].broadcast_to([P, 4, P]),
                                     ACT.Copy).then_inc(ml_nr, 1)
                act.wait_ge(ml_bc, u + 1)
                act.wait_ge(ml_w, u)
                for h in range(4):
                    nc.scalar.activation(
                        EE[:, h], ps[:, 2, P * h:P * h + P], ACT.Exp,
                        bias=CS[:, bass.ds(c, 1), 32 * d + h:32 * d + h + 1].rearrange(
                            "p a b -> p (a b)")).then_inc(ml_exp, 1)
                nc.scalar.activation(IW[:].rearrange("p h t -> p (h t)"), ps[:, 3], ACT.Exp
                                     ).then_inc(ml_exp, 1)
                act.wait_ge(ml_y, u)
                nc.scalar.activation(FL[:].rearrange("p h t -> p (h t)"), ps[:, 4], ACT.Exp
                                     ).then_inc(ml_exp, 1)
            chunks(act, body)

        def ml_dve(dve):
            dve.wait_ge(ml_init, 3)
            nc.vector.memset(VW[:], 0.0).then_inc(ml_init, 1)
            dve.wait_ge(ml_col, 2)

            def body(u, d, c, off):
                tok = bass.ds(off, P)
                dve.wait_ge(ml_exp, u * 6 + 4)
                dve.wait_ge(ml_num, u)
                dve.wait_ge(ml_cn, u)
                nc.vector.tensor_tensor(WM[:].rearrange("p h t -> p (h t)"),
                                        EE[:].rearrange("p h t -> p (h t)"), ps[:, 5],
                                        ALU.mult).then_inc(ml_w, 1)
                dve.wait_ge(ml_kvk, u + 1)
                ws = CW[:, bass.ds(c, 1), 32 * d:32 * d + 4].rearrange("p a (h b) -> p (a h) b",
                                                                      b=1)
                nc.vector.tensor_tensor(VW[:, :, 0:P], KVK[:, 4:8], ws.broadcast_to([P, 4, P]),
                                        ALU.mult)
                nc.vector.tensor_copy(VW[:, :, P:P + 1], ws)
                dve.wait_ge(ml_exp, u * 6 + 6)
                nc.vector.tensor_tensor(QT[:], Q[:, 0:4, tok], IW[:], ALU.mult
                                        ).then_inc(ml_vw, 1)
                dve.wait_ge(ml_cn, u + 1)
                dve.wait_ge(ml_nr, u + 1)
                last = P - 1 if d == 0 else 0
                for h in range(4):
                    o = (P + 1) * (h % 2)
                    nc.vector.scalar_tensor_tensor(
                        out=CT[:, d, h], in0=CT[:, d, h], scalar=IW[:, h, last:last + 1],
                        in1=ps[:, h // 2, o:o + P + 1], op0=ALU.mult, op1=ALU.add
                        ).then_inc(ml_ct, 1)
                fl = FL[:].rearrange("p h t -> p (h t)")
                nc.vector.tensor_tensor(fl, fl, ps[:, 7], ALU.max).then_inc(ml_g, 1)
                dve.wait_ge(ml_g, u * 4 + 30)
                nc.vector.scalar_tensor_tensor(out=fl, in0=ps[:, 7], scalar=-1.0, in1=fl,
                                               op0=ALU.mult, op1=ALU.max).then_inc(ml_g, 1)
                dve.wait_ge(ml_g, u * 4 + 31)
                nc.vector.reciprocal(YM[:], FL[:]).then_inc(ml_g, 1)
                dve.wait_ge(ml_g, u * 4 + 32)
                nc.vector.tensor_tensor(YM[:].rearrange("p h t -> p (h t)"), ps[:, 6],
                                        YM[:].rearrange("p h t -> p (h t)"), ALU.mult
                                        ).then_inc(ml_g, 1)
                dve.wait_ge(ml_g, u * 4 + 33)
                nc.vector.tensor_tensor(H[:, :, tok], H[:, :, tok], YM[:], ALU.add
                                        ).then_inc(ml_y, 1)
            chunks(dve, body)

        FB = dict(SQ=at("FSQ", RB, [P, T]), SD=at("FSD", RB + 3, [P, T]),
                  RS=at("FRS", RB + 6, [P, T]), SG=at("FSG", RB + 9, [P, T]),
                  Y=at("FY", RB + 12, [P, T]))

        def fin_pe(pe):
            for h in range(4):
                pe.wait_ge(fin_sq, h + 1)
                if h:
                    pe.wait_ge(fin_sd, 2 * h)
                nc.tensor.matmul(ps[:, 2], ones, FB["SQ"][:, LC:T], start=True, stop=True)
                nc.tensor.matmul(ps[:, 3, 0:LC], ones, FB["SQ"][:, 0:LC], start=True, stop=True
                                 ).then_inc(fin_st, 1)

        def fin_act(act):
            for h in range(4):
                if h:
                    act.wait_ge(fin_y, 2 * h)
                else:
                    act.wait_ge(ml_y, 12)
                nc.scalar.activation(FB["SG"][:], Q[:, 12 + h], ACT.Tanh, scale=0.5
                                     ).then_inc(fin_o, 1)
                act.wait_ge(fin_st, h + 1)
                nc.scalar.activation(FB["SD"][:, LC:T], ps[:, 2], ACT.Sqrt, bias=CO[:, 64:65],
                                     scale=1.0 / P).then_inc(fin_sd, 1)
                nc.scalar.activation(FB["SD"][:, 0:LC], ps[:, 3, 0:LC], ACT.Sqrt,
                                     bias=CO[:, 64:65], scale=1.0 / P).then_inc(fin_sd, 1)
                act.wait_ge(fin_y, 2 * h + 2)
                nc.scalar.activation(XH[:, h], FB["Y"][:], ACT.Copy).then_inc(fin_hi, 1)

        def fin_dve(dve):
            dve.wait_ge(ml_y, 12)
            for h in range(4):
                nc.vector.tensor_tensor(FB["SQ"][:], H[:, h], H[:, h], ALU.mult
                                        ).then_inc(fin_sq, 1)
                dve.wait_ge(fin_sd, 2 * h + 2)
                nc.vector.reciprocal(FB["RS"][:], FB["SD"][:]).then_inc(ml_g, 1)
                dve.wait_ge(fin_o, h + 1)
                nc.vector.tensor_scalar(FB["SG"][:], FB["SG"][:], 0.5, 0.5, ALU.mult, ALU.add
                                        ).then_inc(ml_g, 1)
                dve.wait_ge(ml_g, 78 + 2 * h + 1)
                if h:
                    dve.wait_ge(fin_hi, h)
                    dve.wait_ge(fin_lo, h)
                nc.vector.scalar_tensor_tensor(out=FB["Y"][:], in0=H[:, h],
                                               scalar=vec("out_g", h), in1=FB["RS"][:],
                                               op0=ALU.mult, op1=ALU.mult).then_inc(fin_y, 1)
                dve.wait_ge(fin_y, 2 * h + 1)
                nc.vector.tensor_tensor(FB["Y"][:], FB["Y"][:], FB["SG"][:], ALU.mult
                                        ).then_inc(fin_y, 1)
                dve.wait_ge(fin_hi, h + 1)
                nc.vector.tensor_tensor(XL[:, h], FB["Y"][:], XH[:, h].bitcast(F32),
                                        ALU.subtract).then_inc(fin_lo, 1)

        KD = at("KD", RB, [P, 2, T])
        VA = at("VA", RB + 6, [P, 6, P])
        ASQ = at("ASQ", RB + 9, [P, T])
        ASD = at("ASD", RB + 12, [P, T])
        ARS = at("ARS", RB + 15, [P, T])
        QZ = at("QZ", RB + 18, [P, 8, P])
        PP = at("PP", RB + 22, [P, 2, 640])
        PT = at("PT", RB + 27, [P, 2, 640])
        ON = at("ON", RB + 32, [P, 8, 64])
        SM = at("SM", RB + 34, [P, 6, 8])
        at_sq, at_st, at_sd, at_rs, at_n = (sem("at_sq"), sem("at_st"), sem("at_sd"),
                                            sem("at_rs"), sem("at_n"))
        at_perm, at_x, at_kd, at_va = sem("at_perm"), sem("at_x"), sem("at_kd"), sem("at_va")
        at_vt, at_z = sem("at_vt"), sem("at_z")
        at_qz, at_s, at_nb, at_p = sem("at_qz"), sem("at_s"), sem("at_nb"), sem("at_p")
        at_t, at_pt, at_o, at_es, at_r = (sem("at_t"), sem("at_pt"), sem("at_o"), sem("at_es"),
                                          sem("at_r"))
        at_on, at_ot, at_hi, at_lo = sem("at_on"), sem("at_ot"), sem("at_hi"), sem("at_lo")
        QS0, KS0, VS0 = 17, 21, 22
        SCALE = 64 ** -0.5
        KINDS = {"ctx": (0, 0, ()), "first": (2, 0, ((384, 1),)),
                 "mid": (3, -1, ((128, 0), (384, 1))), "last": (2, -1, ((256, 0),))}

        def blocks(eng, body):
            with eng.Fori(0, 2) as i:
                body(i, eng.snap(i * P), i, "ctx")
            body(2, LC, 2, "first")
            with eng.Fori(3, 5) as i:
                body(i, eng.snap(i * P), i, "mid")
            body(5, 5 * P, 5, "last")

        def attn_pe(pe):
            for i in range(5):
                pe.wait_ge(at_sq, i + 1)
                pe.wait_ge(at_sd, 2 * i)
                nc.tensor.matmul(ps[:, 0], bd, ASQ[:, LC:T], start=True, stop=True)
                nc.tensor.matmul(ps[:, 1, 0:LC], bd, ASQ[:, 0:LC], start=True, stop=True
                                 ).then_inc(at_st, 1)
                pe.wait_ge(at_n, i + 1)
                pe.wait_ge(at_x, i)
                nc.tensor.matmul(ps[:, 2], c0("perm", 0, P), Q[:, QS0 + i, LC:T], start=True,
                                 stop=True).then_inc(at_perm, 1)
            pv = ps[:, 3:5].rearrange("p a b -> p (a b)")
            for c in range(6):
                mm = nc.tensor.transpose(pv[:, P * c:P * c + P], Q[:, VS0, P * c:P * c + P], ident)
            mm.then_inc(at_vt, 1)
            pe.wait_ge(at_kd, 64)
            pe.wait_ge(at_va, 1)

            def body(b, tok, blk, kind):
                nb, rel, masks = KINDS[kind]
                ntr = nb + 2
                pe.wait_ge(at_lo, b)

                def scores(h):
                    s = h % 2
                    pe.wait_ge(at_qz, b * 2 + 2)
                    if h >= 2:
                        pe.wait_ge(at_p, b * 8 + (h - 1))
                    else:
                        pe.wait_ge(at_r, b * 2)
                    if nb:
                        o = ps[:, 2 * s, 512 - P * nb:512]
                        nc.tensor.matmul(o, QZ[:, h],
                                         KD[:, h // 4, bass.ds(tok + P * rel, P * nb)],
                                         start=True, stop=not masks)
                        for i, (col, m) in enumerate(masks):
                            nc.tensor.matmul(ps[:, 2 * s, col:col + P], ident,
                                             c0("neg", P * m, P), start=False,
                                             stop=i == len(masks) - 1)
                    nc.tensor.matmul(ps[:, 2 * s + 1, 0:LC], QZ[:, h], KD[:, h // 4, 0:LC],
                                     start=True, stop=True).then_inc(at_s, 1)

                def turn(h):
                    pe.wait_ge(at_p, b * 8 + (h + 1))
                    pe.wait_ge(at_pt, b * 8 + h)
                    pt = ps[:, 4:6].rearrange("p a b -> p (a b)")
                    for k in range(ntr):
                        mm = nc.tensor.transpose(pt[:, P * k:P * k + P],
                                                 PP[:, h % 2, P * k:P * k + P], ident)
                    mm.then_inc(at_t, 1)

                def values(h):
                    pe.wait_ge(at_pt, b * 8 + (h + 1))
                    if h == 0:
                        pe.wait_ge(at_on, b)
                    for k in range(ntr):
                        if k < nb:
                            v = VA[:, bass.ds(blk + (rel + k), 1), 64 * (h // 4):64 * (h // 4) + 64]
                            v = v.rearrange("p a c -> p (a c)")
                        else:
                            v = VA[:, k - nb, 64 * (h // 4):64 * (h // 4) + 64]
                        mm = nc.tensor.matmul(ps[:, 6, 64 * h:64 * h + 64],
                                              PT[:, h % 2, P * k:P * k + P], v, start=k == 0,
                                              stop=k == ntr - 1)
                    mm.then_inc(at_o, 1)
                for h in range(10):
                    if h < 8:
                        scores(h)
                    if h < 8:
                        adb_pe(pe, b, h)
                    if 1 <= h <= 8:
                        turn(h - 1)
                    if h >= 2:
                        values(h - 2)
                pe.wait_ge(at_on, b + 1)
                pe.wait_ge(adb_row, b * 2 + 2)
                for j in range(4):
                    mm = nc.tensor.transpose(ps[:, 7, P * j:P * j + P],
                                             ON[:, 2 * j:2 * j + 2].rearrange("p a c -> p (a c)"),
                                             ident)
                mm.then_inc(at_ot, 1)
            blocks(pe, body)

        def attn_act(act):
            for i in range(5):
                act.wait_ge(at_st, i + 1)
                act.wait_ge(at_rs, i)
                nc.scalar.activation(ASD[:, LC:T], ps[:, 0], ACT.Sqrt, bias=CO[:, 64:65],
                                     scale=1.0 / 64).then_inc(at_sd, 1)
                nc.scalar.activation(ASD[:, 0:LC], ps[:, 1, 0:LC], ACT.Sqrt, bias=CO[:, 64:65],
                                     scale=1.0 / 64).then_inc(at_sd, 1)
            act.wait_ge(at_vt, 1)
            nc.scalar.activation(VA[:].rearrange("p c t -> p (c t)"),
                                 ps[:, 3:5].rearrange("p a b -> p (a b)")[:, 0:T], ACT.Copy
                                 ).then_inc(at_va, 1)
            act.wait_ge(at_x, 5)
            act.wait_ge(at_z, 12)

            def body(b, tok, blk, kind):
                nb, rel, masks = KINDS[kind]
                n = P * (nb + 2)
                act.wait_ge(at_s, b * 8)
                for e in range(2):
                    nc.scalar.activation(
                        QZ[64 * e:64 * e + 64].rearrange("p (j e) t -> p j e t", e=2)[:, :, e],
                        Q[64 * e:64 * e + 64, QS0:QS0 + 4, bass.ds(tok, P)], ACT.Copy
                        ).then_inc(at_qz, 1)
                for h in range(9):
                    if h < 8:
                        s = h % 2
                        act.wait_ge(at_nb, b * 16 + (2 * h + 2))
                        if h >= 2:
                            act.wait_ge(at_t, b * 8 + (h - 1))
                        else:
                            act.wait_ge(at_t, b * 8)
                        src = ps[:, 2 * s:2 * s + 2].rearrange("p a b -> p (a b)")[
                            :, 512 - P * nb:512 + LC]
                        nc.scalar.activation(PP[:, s, 0:n], src, ACT.Exp,
                                             bias=SM[:, 1, h:h + 1], scale=SCALE,
                                             accum_out=SM[:, 2, h:h + 1]).then_inc(at_p, 1)
                    if h >= 1:
                        g = h - 1
                        act.wait_ge(at_t, b * 8 + (g + 1))
                        act.wait_ge(at_o, b * 8 + max(g - 1, 0))
                        nc.scalar.activation(PT[:, g % 2, 0:n],
                                             ps[:, 4:6].rearrange("p a b -> p (a b)")[:, 0:n],
                                             ACT.Copy).then_inc(at_pt, 1)
                act.wait_ge(at_r, b * 2 + 1)
                nc.scalar.activation(SM[:, 4], SM[:, 3], ACT.Exp).then_inc(at_es, 1)
                act.wait_ge(at_ot, b + 1)
                nc.scalar.activation(XH[:, 4:8, bass.ds(tok, P)],
                                     ps[:, 7].rearrange("p (j t) -> p j t", j=4), ACT.Copy
                                     ).then_inc(at_hi, 1)
            blocks(act, body)

        def attn_dve(dve):
            dve.wait_ge(fin_lo, 4)
            dve.wait_ge(fin_hi, 4)
            for i in range(5):
                x = Q[:, QS0 + i]
                dve.wait_ge(at_st, i)
                nc.vector.tensor_tensor(ASQ[:], x, x, ALU.mult).then_inc(at_sq, 1)
                dve.wait_ge(at_sd, 2 * i + 2)
                nc.vector.reciprocal(ARS[:], ASD[:]).then_inc(at_rs, 1)
                dve.wait_ge(at_rs, i + 1)
                nc.vector.scalar_tensor_tensor(out=x, in0=x, scalar=vec("q_g" if i < 4 else "k_g"),
                                               in1=ARS[:], op0=ALU.mult, op1=ALU.mult
                                               ).then_inc(at_n, 1)
                dve.wait_ge(at_perm, i + 1)
                nc.vector.tensor_tensor(ASQ[:, 0:512], ps[:, 2], c0("sin", 0, LAT), ALU.mult
                                        ).then_inc(at_z, 1)
                nc.vector.tensor_tensor(x[:, LC:T], x[:, LC:T], c0("cos", 0, LAT), ALU.mult
                                        ).then_inc(at_z, 1)
                dve.wait_ge(at_z, 2 * i + 2)
                nc.vector.tensor_tensor(x[:, LC:T], x[:, LC:T], ASQ[:, 0:512], ALU.add
                                        ).then_inc(at_x, 1)
                dve.wait_ge(at_x, i + 1)
            nc.vector.memset(QZ[:], 0.0).then_inc(at_z, 1)
            nc.vector.tensor_scalar(SM[:, 5], vec("sink", 0, 8), -1.0, None, ALU.mult
                                    ).then_inc(at_z, 1)
            dve.wait_ge(at_z, 12)

            def body(b, tok, blk, kind):
                nb, rel, masks = KINDS[kind]
                for h in range(8):
                    s = h % 2
                    dve.wait_ge(at_s, b * 8 + (h + 1))
                    src = ps[:, 2 * s:2 * s + 2].rearrange("p a b -> p (a b)")[
                        :, 512 - P * nb:512 + LC]
                    nc.vector.tensor_reduce(SM[:, 0, h:h + 1], src, AX.X, ALU.max
                                            ).then_inc(at_nb, 1)
                    dve.wait_ge(at_nb, b * 16 + (2 * h + 1))
                    if h == 4:
                        dve.wait_ge(mod_out, b * 16 + 16)
                        adb_dve(dve, b, 0)
                    nc.vector.tensor_scalar(SM[:, 1, h:h + 1], SM[:, 0, h:h + 1], -SCALE,
                                            SM[:, 5, h:h + 1], ALU.mult, ALU.min
                                            ).then_inc(at_nb, 1)
                adb_dve(dve, b, 1)
                dve.wait_ge(at_nb, b * 16 + 16)
                dve.wait_ge(at_es, b)
                nc.vector.tensor_tensor(SM[:, 3], SM[:, 1], vec("sink", 0, 8), ALU.add
                                        ).then_inc(at_r, 1)
                dve.wait_ge(at_es, b + 1)
                dve.wait_ge(at_p, b * 8 + 8)
                nc.vector.tensor_tensor(SM[:, 4], SM[:, 4], SM[:, 2], ALU.add).then_inc(at_r, 1)
                dve.wait_ge(at_r, b * 2 + 2)
                nc.vector.reciprocal(SM[:, 0], SM[:, 4]).then_inc(at_rs, 1)
                dve.wait_ge(at_rs, b + 6)
                dve.wait_ge(at_o, b * 8 + 8)
                dve.wait_ge(at_ot, b)
                nc.vector.tensor_tensor(ON[:], ps[:, 6].rearrange("p (h c) -> p h c", h=8),
                                        SM[:, 0][:, :, None].broadcast_to([P, 8, 64]), ALU.mult
                                        ).then_inc(at_on, 1)
                dve.wait_ge(at_ot, b + 1)
                dve.wait_ge(at_hi, b + 1)
                xs = bass.ds(tok, P)
                nc.vector.tensor_tensor(XL[:, 4:8, xs],
                                        ps[:, 7].rearrange("p (j t) -> p j t", j=4),
                                        XH[:, 4:8, xs].bitcast(F32), ALU.subtract
                                        ).then_inc(at_lo, 1)
            blocks(dve, body)

        def attn_pool(pool):
            pool.wait_ge(at_x, 5)
            for g in range(2):
                for e in range(2):
                    pool.dma_start(KD[64 * e:64 * e + 64, g], Q[64 * g:64 * g + 64, KS0]
                                   ).then_inc(at_kd, 16)
            with pool.Fori(0, 6) as b:
                o = pool.snap(b * D)
                pool.wait_ge(adb_row, b * 2 + 2)
                pool.sem_inc(waits_seen)
                pool.dma_start(mod_dram[1][:, bass.ds(o, D)], ROWB[:]).then_inc(mod_out, 16)
            pool.wait_ge(mod_out, 112)
            pool.dma_start(ROWT[:], mod_dram[1].rearrange("c (m n) -> (c m) n", n=P)
                           ).then_inc(rowt_in, 16)

        RR = at("RR", RB + 24.5, [P, KT, LAT])
        KK_ = at("KK_", RB + 40.5, [P, KT, T])
        VKB = at("VKB", RB + 64.5, [P, 2, 6, P])
        H1 = at("H1", RB + 76.5, [P, 2, T])
        G1 = at("G1", RB + 82.5, [P, 2, LAT])
        MX = at("MX", RB + 86.5, [P, 2, T])
        MC = at("MC", RB + 92.5, [P, 6, 8])
        mc_ready, mx_a, mx_b, mx_c = sem("mc_ready"), sem("mx_a"), sem("mx_b"), sem("mx_c")
        vk_t, vk_c, vk_out, vt_out = sem("vk_t"), sem("vk_c"), [sem("vk_out0"), sem("vk_out1")], sem("vt_out")
        g1_ready, cm1_in, z_out = sem("g1_ready"), sem("cm1_in"), sem("z_out")
        MIXES = [(3, T_V, 8, SEGS), (2, T_K, 8, SEGS), (1, T_W, 1, SEGS), (4, T_A, 1, SEGS),
                 (0, T_R, 8, (LATS,)), (5, T_G, 2, (LATS,))]

        def ushift(k, sg, by):
            a = 2 + 2 * SEGS.index(sg) + sg[0] + by
            return U[:, k, a:a + sg[1]]

        def mix_act(act, q):
            i, t0, n, segs = MIXES[q]
            a = segs[0][0]

            def scale(k):
                if k >= 2:
                    act.wait_ge(x_lo, 16 + 8 * q + k - 1)
                for sg in segs:
                    ins = nc.scalar.activation(MX[:, k % 2, sg[0]:sg[0] + sg[1]], ushift(k, sg, 0),
                                               ACT.Copy, scale=MC[:, i, k:k + 1])
                ins.then_inc(mx_a, 1)
            if q == 0:
                act.wait_ge(mc_ready, 2)
                act.wait_ge(n_h, 24)
            act.wait_ge(x_lo, 16 + 8 * q)
            for k in range(KT):
                if k == 0:
                    scale(0)
                if k + 1 < KT:
                    scale(k + 1)
                act.wait_ge(mx_c, 8 * q + k + 1)
                nc.scalar.activation(XH[:, k, a:T], MX[:, k % 2, a:T], ACT.Copy).then_inc(x_hi, 1)

        def mix_dve(dve, q):
            i, t0, n, segs = MIXES[q]
            a = segs[0][0]
            for k in range(KT):
                dve.wait_ge(mx_a, 8 * q + k + 1)
                for by, sm in ((-1, mx_b), (1, mx_c)):
                    for sg in segs:
                        m = MX[:, k % 2, sg[0]:sg[0] + sg[1]]
                        ins = nc.vector.scalar_tensor_tensor(
                            out=m, in0=ushift(k, sg, by),
                            scalar=vec("mu", 16 * i + (0 if by < 0 else 8) + k), in1=m,
                            op0=ALU.mult, op1=ALU.add)
                    ins.then_inc(sm, 1)
                    dve.wait_ge(sm, 8 * q + k + 1)
                dve.wait_ge(x_hi, 16 + 8 * q + k + 1)
                nc.vector.tensor_tensor(XL[:, k, a:T], MX[:, k % 2, a:T],
                                        XH[:, k, a:T].bitcast(F32), ALU.subtract
                                        ).then_inc(x_lo, 1)

        def at_tile(x, m, lo, hi):
            return x[:, bass.ds(m, 1), lo:hi].rearrange("p a t -> p (a t)")

        def mix_evict(q, eng):
            def act_side(t, m, s):
                if q <= 1:
                    nc.scalar.activation(at_tile(KK_, m, LC, T), acc(s, LATS), ACT.Copy
                                         ).then_inc(acc_lat, 1)
                elif q <= 3:
                    f = ACT.Tanh if q == 2 else ACT.Copy
                    nc.scalar.activation(H1[:, q - 2, 0:LC], acc(s, CTX), f).then_inc(acc_ctx, 1)
                    nc.scalar.activation(H1[:, q - 2, LC:T], acc(s, LATS), f).then_inc(acc_lat, 1)
                elif q == 4:
                    nc.scalar.activation(at_tile(RR, m, 0, LAT), acc(s, LATS), ACT.Copy
                                         ).then_inc(acc_lat, 1)
                else:
                    nc.scalar.activation(G1[:, m], acc(s, LATS), ACT.Tanh, scale=0.5
                                         ).then_inc(acc_lat, 1)

            def dve_side(t, m, s):
                if q <= 1:
                    nc.vector.tensor_copy(at_tile(KK_, m, 0, LC), acc(s, CTX)).then_inc(acc_ctx, 1)
            return act_side if eng == "act" else dve_side

        def vk_pe(pe):
            pe.wait_ge(acc_lat, T_V + 8)
            pe.wait_ge(acc_ctx, T_V + 8)
            for m in range(8):
                if m >= 2:
                    pe.wait_ge(vk_c, m - 1)
                b = 4 + 2 * (m % 2)
                o = ps[:, b:b + 2].rearrange("p a b -> p (a b)")
                for c in range(6):
                    mm = nc.tensor.transpose(o[:, P * c:P * c + P], KK_[:, m, P * c:P * c + P],
                                             ident)
                mm.then_inc(vk_t, 1)

        def vk_act(act):
            for m in range(8):
                act.wait_ge(vk_t, m + 1)
                if m >= 2:
                    act.wait_ge(vk_out[m % 2], 16 * (m // 2))
                b = 4 + 2 * (m % 2)
                nc.scalar.activation(VKB[:, m % 2].rearrange("p c t -> p (c t)"),
                                     ps[:, b:b + 2].rearrange("p a b -> p (a b)")[:, 0:T],
                                     ACT.Copy).then_inc(vk_c, 1)

        def vk_pool(pool):
            pool.wait_ge(n_h, 24)
            pool.dma_start(z_dram, z[:, :, LC:T]).then_inc(z_out, 16)
            pool.wait_ge(acc_lat, T_V + 8)
            pool.dma_start(vt_dram, KK_[:, :, LC:T]).then_inc(vt_out, 16)
            for m in range(8):
                pool.wait_ge(vk_c, m + 1)
                pool.dma_start(vk_dram[:, P * m:P * m + P].rearrange("(c p) n -> p c n", p=P),
                               VKB[:, m % 2]).then_inc(vk_out[m % 2], 16)

        KN = at("KN", RB, [P, KT, T])
        KQ = at("KQ", RB + 64.5, [P, T])
        KSQ = at("KSQ", RB + 67.5, [P, T])
        KSD = at("KSD", RB + 70.5, [P, T])
        KRS = at("KRS", RB + 73.5, [P, T])
        kk_sq, kk_st, kk_sd, kk_n = sem("kk_sq"), sem("kk_st"), sem("kk_sd"), sem("kk_n")

        def kk_pe(pe):
            for m in range(8):
                pe.wait_ge(kk_sq, 3 * m + 2)
                nc.tensor.matmul(ps[:, 4], bd, KSQ[:, LC:T], start=True, stop=True)
                nc.tensor.matmul(ps[:, 5, 0:LC], bd, KSQ[:, 0:LC], start=True, stop=True
                                 ).then_inc(kk_st, 1)

        def kk_act(act):
            for m in range(8):
                act.wait_ge(kk_sq, 3 * m + 3)
                nc.scalar.activation(KSD[:], KSD[:], ACT.Sqrt).then_inc(kk_sd, 1)

        def kk_dve(dve):
            dve.wait_ge(vk_out[0], 64)
            dve.wait_ge(vk_out[1], 64)
            dve.wait_ge(acc_lat, T_G + 2)
            nc.vector.tensor_scalar(G1[:], G1[:], 0.5, 0.5, ALU.mult, ALU.add
                                    ).then_inc(g1_ready, 1)
            for m in range(8):
                nc.vector.tensor_scalar(KQ[:], KK_[:, m], vec("k_k", m), None, ALU.mult
                                        ).then_inc(kk_sq, 1)
                dve.wait_ge(kk_sq, 3 * m + 1)
                nc.vector.tensor_tensor(KSQ[:], KQ[:], KQ[:], ALU.mult).then_inc(kk_sq, 1)
                dve.wait_ge(kk_st, m + 1)
                nc.vector.tensor_scalar(KSD[:, LC:T], ps[:, 4], 1e-24, None, ALU.max)
                nc.vector.tensor_scalar(KSD[:, 0:LC], ps[:, 5, 0:LC], 1e-24, None, ALU.max
                                        ).then_inc(kk_sq, 1)
                dve.wait_ge(kk_sd, m + 1)
                nc.vector.reciprocal(KRS[:], KSD[:]).then_inc(kk_n, 1)
                dve.wait_ge(kk_n, 2 * m + 1)
                nc.vector.tensor_tensor(KN[:, m], KQ[:], KRS[:], ALU.mult).then_inc(kk_n, 1)
                dve.wait_ge(kk_n, 2 * m + 2)

        L2 = at("L2", 0, [P, 2, D])
        DOT = at("DOT", 20, [16, LAT])

        def two(name, a, b, shape):
            return [at(f"{name}{d}", o, shape) for d, o in enumerate((a, b))]

        def temp(name, i):
            return two(name, RB + 64.5 + 2 * i, 8 + 2 * i, [P, 8, L])
        TA, TB, TC, TE, TQ, TK = (temp("TA", 0), temp("TB", 1), temp("TC", 2), temp("TE", 3),
                                  temp("TQ", 4), temp("TK", 5))
        GP = two("GP", RA, RA + 8, [P, 2, 8, 2, L])
        BK = two("BK", RA + 16, RA + 20, [P, 8, 2, L])
        AR = two("AR", RA + 24, RA + 28, [P, 8, 2, L])
        UV = two("UV", RA + 32, RA + 36, [P, 8, 2, L])
        ST = two("ST", RA + 40, RA + 42, [P, 8, L])
        PB = two("PB", RA + 44, RA + 46, [P, 8, L])
        ZZ = two("ZZ", RB + 86.5, RB + 88.5, [P, 8, L])
        XX = two("XX", RB + 90.5, RB + 92.5, [P, 8, L])
        HS = at("HS", RB + 94.5, [P, 2, 2, L])
        RK = at("RK", RB + 95.5, [P, 8, 16])
        PL = at("PL", 52.75, [P, 2, 8])
        OK = at("OK", 52.8125, [P, 8])
        l2_in, sc_init = sem("l2_in"), sem("sc_init")
        pr_hs, pr_lo, pr_x, pr_t, pr_g, pr_e = (sem("pr_hs"), sem("pr_lo"), sem("pr_x"),
                                                sem("pr_t"), sem("pr_g"), sem("pr_e"))
        pr_q, pr_rr, fin, pr_dp, pr_dt = (sem("pr_q"), sem("pr_rr"), sem("fin"), sem("pr_dp"),
                                          sem("pr_dt"))
        gA, gT, eA, eT = sem("gA"), sem("gT"), sem("eA"), sem("eT")
        zi, z0, iX, iP, iC, iZ, iM = (sem("zi"), sem("z0"), sem("iX"), sem("iP"), sem("iC"),
                                      sem("iZ"), sem("iM"))
        sc, ac = sem("sc"), sem("ac")
        cH, rH, cU, uU, cY, yS, cS, sA, sU = (sem("cH"), sem("rH"), sem("cU"), sem("uU"),
                                              sem("cY"), sem("yS"), sem("cS"), sem("sA"),
                                              sem("sU"))
        yO, vI = [sem("yO0"), sem("yO1")], [sem("vI0"), sem("vI1")]
        ROWS = (slice(0, 64), slice(64, 128))
        CC, CL = LC // L, T // L

        def turns(eng, body):
            body(0, "ctx", "ctx")
            with eng.Fori(1, CC - 1) as i:
                body(i, "ctx", "ctx")
            body(CC - 1, "ctx", "lat")
            body(CC, "lat", "lat")
            with eng.Fori(CC + 1, CL - 1) as i:
                body(i, "lat", "lat")
            body(CL - 1, "lat", None)

        def chunk_at(eng, it, kind):
            if kind == "ctx":
                a, b = it * L, it * -L + (LC - L)
            else:
                a, b = it * L, it * -L + (LC + T - L)
            return [a, b] if isinstance(it, int) else [eng.snap(a), eng.snap(b)]

        def in_lat(eng, off):
            return off - LC if isinstance(off, int) else eng.snap(off + -LC)

        def toks(x, off):
            return x[:, :, bass.ds(off, L)]

        def scan_pe(pe):
            pe.wait_ge(l2_in, 16)
            pe.wait_ge(sc_init, 9)
            pe.wait_ge(cm1_in, 16)

            def lora(n):
                pe.wait_ge(pr_hs, n * 2 + 2)
                for j in range(2):
                    o = ps[:, 4 * j + 2:4 * j + 4].rearrange("p a b -> p (a b)")
                    for p in range(8):
                        mm = nc.tensor.matmul(o[:, P * p:P * p + P], L2[:, j, P * p:P * p + P],
                                              HS[:, j].rearrange("p d t -> p (d t)"),
                                              start=True, stop=True)
                mm.then_inc(pr_lo, 1)
            lora(0)

            def body(it, kind, nxt):
                for d in range(2):
                    pe.wait_ge(fin, it * 2 + (d + 1))
                    if kind == "lat" and not (isinstance(it, int) and it == CC):
                        pe.wait_ge(yS, it * 2 + (d - 1 - 2 * CC))
                    for e in range(2):
                        o = ps[:, 4 * d + 2 * e:4 * d + 2 * e + 2].rearrange("p a b -> p (a b)")
                        for p in range(8):
                            mm = nc.tensor.matmul(
                                o[:, P * p:P * p + P],
                                BK[d][ROWS[e], p].rearrange("p a t -> p (a t)"),
                                AR[d][ROWS[e], p].rearrange("p a t -> p (a t)"), start=True,
                                stop=True)
                        mm.then_inc(gA, 1)
                for d in range(2):
                    pe.wait_ge(eA, it * 4 + (2 * d + 1))
                    o = ps[:, 4 * d:4 * d + 2].rearrange("p a b -> p (a b)")
                    for p in range(8):
                        mm = nc.tensor.transpose(o[:, P * p:P * p + P],
                                                 BK[d][:, p].rearrange("p a t -> p (a t)"),
                                                 ident)
                    mm.then_inc(gT, 1)
                if nxt:
                    pe.wait_ge(eA, it * 4 + 4)
                    lora(it + 1)
                for l in range(5):
                    for d in range(2):
                        pe.wait_ge(iX, it * 10 + (2 * l + d + 1))
                        if l == 0:
                            pe.wait_ge(eT, it * 2 + (d + 1))
                        pe.sem_inc(waits_seen)
                        for e in range(2):
                            for p in range(8):
                                mm = nc.tensor.matmul(
                                    ps[ROWS[e], 4 * d, L * p:L * p + L],
                                    GP[d][ROWS[e], e, p, 0], XX[d][ROWS[e], p], start=True,
                                    stop=True)
                        mm.then_inc(iP, 1)
                    for d in range(2):
                        pe.wait_ge(iC, it * 10 + (2 * l + d + 1))
                        pe.sem_inc(waits_seen)
                        for e in range(2):
                            for p in range(8):
                                mm = nc.tensor.matmul(
                                    ps[ROWS[e], 4 * d + 1, L * p:L * p + L],
                                    PB[d][ROWS[e], p], ZZ[d][ROWS[e], p], start=True, stop=True)
                        mm.then_inc(iZ, 1)
                for d in range(2):
                    pe.wait_ge(vI[d], it * 32 + 32)
                    pe.wait_ge(sc, it * 2 + (d + 1))
                    pe.wait_ge(ac, it * 2 + (d + 1))
                    if nxt:
                        pe.wait_ge(pr_x, it * 4 + 8)
                    for e in range(2):
                        for p in range(8):
                            mm = nc.tensor.matmul(ps[ROWS[e], 4 * d + 2, L * p:L * p + L],
                                                  GP[d][:, e, p, 0], UV[d][:, p, e],
                                                  start=True, stop=True)
                    mm.then_inc(cH, 1)
                if nxt == "lat":
                    for d in range(2):
                        pe.wait_ge(pr_rr, it * 2 + (d + 3 - 2 * CC))
                        for p in range(8):
                            mm = nc.tensor.matmul(ps[0:16, 4 * d, 0:L], RK[:, p], TB[d][:, p],
                                                  start=p == 0, stop=p == 7)
                        mm.then_inc(pr_dp, 1)
                for d in range(2):
                    pe.wait_ge(rH, it * 2 + (d + 1))
                    pe.wait_ge(iM, it * 10 + (9 + d))
                    pe.sem_inc(waits_seen)
                    for e in range(2):
                        for p in range(8):
                            mm = nc.tensor.matmul(ps[ROWS[e], 4 * d + 3, L * p:L * p + L],
                                                  ZZ[d][ROWS[e], p], XX[d][ROWS[e], p],
                                                  start=True, stop=True)
                    mm.then_inc(cU, 1)
                for d in range(2):
                    pe.wait_ge(uU, it * 2 + (d + 1))
                    for e in range(2):
                        for p in range(8):
                            mm = nc.tensor.matmul(ps[ROWS[e], 4 * d + 3, L * p:L * p + L],
                                                  BK[d][:, p, e], UV[d][:, p, e], start=True,
                                                  stop=True)
                    mm.then_inc(cS, 1)
                    if kind == "lat":
                        for e in range(2):
                            for p in range(8):
                                o = ps[ROWS[e], 4 * d + 2, L * p:L * p + L]
                                nc.tensor.matmul(o, ST[d][ROWS[e], p], AR[d][ROWS[e], p, 1],
                                                 start=True, stop=False)
                                mm = nc.tensor.matmul(o, UV[d][:, p, e], GP[d][:, e, p, 1],
                                                      start=False, stop=True)
                        mm.then_inc(cY, 1)
            turns(pe, body)

        def scan_act(act):
            act.wait_ge(sc_init, 9)

            def hidden(n, kind):
                if not (isinstance(n, int) and n == 0):
                    act.wait_ge(pr_lo, n)
                off = chunk_at(act, n, kind)
                for d in range(2):
                    nc.scalar.activation(HS[ROWS[d], :, d], H1[ROWS[d], :, bass.ds(off[d], L)],
                                         ACT.Copy).then_inc(pr_hs, 1)

            def tanhs(n, d):
                for j, x in enumerate((TA[d], TB[d])):
                    act.wait_ge(pr_x, n * 4 + (2 * d + j + 1))
                    nc.scalar.activation(x[:], x[:], ACT.Tanh, scale=0.5).then_inc(pr_t, 1)

            def exps(n, d):
                act.wait_ge(pr_g, n * 8 + (4 * d + 4))
                nc.scalar.activation(TE[d][:], TC[d][:], ACT.Exp, scale=-KAPPA).then_inc(pr_e, 1)
                nc.scalar.activation(TA[d][:], TA[d][:], ACT.Exp, scale=-KAPPA).then_inc(pr_e, 1)
                act.wait_ge(pr_e, n * 6 + (3 * d + 1))
                nc.scalar.activation(TC[d][:], TC[d][:], ACT.Exp, scale=KAPPA).then_inc(pr_e, 1)
            hidden(0, "ctx")
            for d in range(2):
                tanhs(0, d)
            for d in range(2):
                exps(0, d)

            def body(it, kind, nxt):
                for d in range(2):
                    if not (isinstance(it, int) and it == 0):
                        act.wait_ge(cU, it * 2 + (d - 1))
                    nc.scalar.activation(ZZ[d][:], c1("eye", 0, L)[:, None, :].broadcast_to(
                        [P, 8, L]), ACT.Copy).then_inc(zi, 1)
                if nxt:
                    hidden(it + 1, nxt)
                for d in range(2):
                    if not (isinstance(it, int) and it == 0):
                        act.wait_ge(sU, it * 2 + (d - 1))
                    for e in range(2):
                        ins = nc.scalar.activation(UV[d][ROWS[e], :, e], ST[d][ROWS[e]],
                                                   ACT.Copy)
                    ins.then_inc(sc, 1)
                for d in range(2):
                    act.wait_ge(gT, it * 2 + (d + 1))
                    nc.scalar.activation(BK[d][:].rearrange("p m a t -> p (m a t)"),
                                         ps[:, 4 * d:4 * d + 2].rearrange("p a b -> p (a b)"),
                                         ACT.Copy).then_inc(eT, 1)
                for l in range(5):
                    for d in range(2):
                        act.wait_ge(iP, it * 10 + (2 * l + d + 1))
                        nc.scalar.activation(PB[d][:].rearrange("p a t -> p (a t)"),
                                             ps[:, 4 * d], ACT.Copy).then_inc(iC, 1)
                        if l == 4:
                            for e in range(2):
                                ins = nc.scalar.activation(GP[d][ROWS[e], e, :, 0],
                                                           AR[d][ROWS[e], :, 0], ACT.Copy)
                            ins.then_inc(ac, 1)
                    if nxt and l == 1:
                        tanhs(it + 1, 0)
                    if nxt and l == 2:
                        exps(it + 1, 0)
                        tanhs(it + 1, 1)
                    if nxt and l == 3:
                        exps(it + 1, 1)
                for d in range(2):
                    act.wait_ge(cH, it * 2 + (d + 1))
                    nc.scalar.activation(XX[d][:].rearrange("p a t -> p (a t)"),
                                         ps[:, 4 * d + 2], ACT.Copy).then_inc(rH, 1)
                for d in range(2):
                    act.wait_ge(cU, it * 2 + (d + 1))
                    act.wait_ge(cH, it * 2 + (d + 1))
                    for e in range(2):
                        ins = nc.scalar.activation(
                            UV[d][ROWS[e], :, e],
                            ps[ROWS[e], 4 * d + 3].rearrange("p (a t) -> p a t", t=L), ACT.Copy)
                    ins.then_inc(uU, 1)
                if kind == "lat":
                    for d in range(2):
                        act.wait_ge(cY, it * 2 + (d + 1 - 2 * CC))
                        nc.scalar.activation(XX[d][:], ps[:, 4 * d + 2].rearrange(
                            "p (a t) -> p a t", t=L), ACT.Copy).then_inc(yS, 1)
            turns(act, body)

        def scan_dve(dve):
            dve.wait_ge(z_out, 16)
            dve.wait_ge(tile_done, T_G + 2)
            dve.wait_ge(cm1_in, 16)
            dve.wait_ge(kk_n, 16)
            nc.vector.memset(DOT[:], 0.0).then_inc(sc_init, 1)
            nc.vector.memset(HS[:], 0.0).then_inc(sc_init, 1)
            for d in range(2):
                nc.vector.memset(ST[d][:], 0.0).then_inc(sc_init, 1)
                nc.vector.memset(AR[d][:, :, 1], 0.0).then_inc(sc_init, 1)
            nc.vector.tensor_tensor(
                RK[:], c1("hsel", 0, P).rearrange("p (m h) -> p m h", m=8),
                vec("r_k", 0, 8)[:, :, None].broadcast_to([P, 8, 16]), ALU.mult
                ).then_inc(sc_init, 1)
            nc.vector.memset(PL[:], 0.0).then_inc(sc_init, 1)
            nc.vector.tensor_scalar(OK[:], vec("k_a", 0, 8), -1.0, 1.0, ALU.mult, ALU.add
                                    ).then_inc(sc_init, 1)

            def fl(x):
                return x.rearrange("p a t -> p (a t)")

            def rates(n, d, kind):
                dve.wait_ge(pr_lo, n + 1)
                if not (isinstance(n, int) and n == 0):
                    dve.wait_ge(fin, n * 2 + (d - 1))
                if kind == "lat" and not (isinstance(n, int) and n == CC):
                    dve.wait_ge(pr_dp, n * 2 + (d - 1 - 2 * CC))
                for j, (x, w) in enumerate(((TA[d], "w0"), (TB[d], "a0"))):
                    o = ps[:, 4 * j + 2:4 * j + 4].rearrange("p a (m c t) -> p (a m) c t", c=2,
                                                             t=L)
                    nc.vector.tensor_tensor(
                        x[:], o[:, :, d],
                        vec(w, 8 * d, 8)[:, :, None].broadcast_to([P, 8, L]), ALU.add
                        ).then_inc(pr_x, 1)

            def sums(n, d):
                for j, x in enumerate((TA[d], TB[d])):
                    dve.wait_ge(pr_t, n * 4 + (2 * d + j + 1))
                    nc.vector.tensor_scalar(x[:], x[:], 0.5, 0.5, ALU.mult, ALU.add
                                            ).then_inc(pr_g, 1)
                dve.wait_ge(pr_g, n * 8 + (4 * d + 2))
                step = 1 if d == 0 else -1
                nc.vector.tensor_tensor_scan(fl(TC[d][:])[:, ::step], c1("reset", 0, 512),
                                             fl(TA[d][:])[:, ::step], 0.0, ALU.mult, ALU.add
                                             ).then_inc(pr_g, 1)
                dve.wait_ge(pr_g, n * 8 + (4 * d + 3))
                nc.vector.tensor_tensor(TA[d][:], TC[d][:], TA[d][:], ALU.subtract
                                        ).then_inc(pr_g, 1)

            def factors(n, d, kind):
                off = chunk_at(dve, n, kind)[d]
                dve.wait_ge(pr_e, n * 6 + (3 * d + 3))
                if not (isinstance(n, int) and n == 0):
                    dve.wait_ge(cS, n * 2 + (d - 1))
                    dve.wait_ge(sU, n * 2 + (d - 1))
                if kind == "lat" and not (isinstance(n, int) and n == CC):
                    dve.wait_ge(cY, n * 2 + (d - 1 - 2 * CC))
                nc.vector.scalar_tensor_tensor(out=AR[d][:, :, 0], in0=toks(KN, off),
                                               scalar=-1.0, in1=TA[d][:], op0=ALU.mult,
                                               op1=ALU.mult)
                nc.vector.tensor_copy(PL[:, d], TE[d][:, :, L - 1 if d == 0 else 0])
                if kind == "lat":
                    nc.vector.tensor_tensor(AR[d][:, :, 1], toks(RR, in_lat(dve, off)), TE[d][:],
                                            ALU.mult)
                dve.wait_ge(pr_q, n * 8 + (4 * d + 4))
                for e in range(2):
                    nc.vector.tensor_tensor(BK[d][ROWS[e], :, e], TK[d][ROWS[e]],
                                            TC[d][ROWS[e]], ALU.mult)
                    ins = nc.vector.tensor_tensor(BK[d][ROWS[e], :, 1 - e], TQ[d][ROWS[e]],
                                                  TC[d][ROWS[e]], ALU.mult)
                ins.then_inc(fin, 1)

            def dots(n, kind):
                off = chunk_at(dve, n, kind)
                for d in range(2):
                    dve.wait_ge(pr_dp, n * 2 + (d + 1 - 2 * CC))
                    dv = DOT[:, bass.ds(in_lat(dve, off[d]), L)]
                    if not (isinstance(n, int) and n == CC and d == 0):
                        dve.wait_ge(pr_dt, n * 2 + (d - 2 * CC))
                    nc.vector.tensor_tensor(dv, dv, ps[0:16, 4 * d, 0:L], ALU.add
                                            ).then_inc(pr_dt, 1)
            dve.wait_ge(sc_init, 9)
            for d in range(2):
                rates(0, d, "ctx")
            for d in range(2):
                sums(0, d)
            for d in range(2):
                factors(0, d, "ctx")

            def body(it, kind, nxt):
                for d in range(2):
                    for e in range(2):
                        dve.wait_ge(gA, it * 4 + (2 * d + e + 1))
                        nc.vector.tensor_tensor(
                            GP[d][:, e].rearrange("p m a t -> p m (a t)"),
                            ps[:, 4 * d + 2 * e:4 * d + 2 * e + 2].rearrange(
                                "p a (m t) -> p (a m) t", t=P),
                            c1("tri", P * d, P)[:, None, :].broadcast_to([P, 8, P]), ALU.mult
                            ).then_inc(eA, 1)

                def lvl(d, l, r=slice(0, P)):
                    m = c1("lvl", L * (6 * d + l), L)[r].bitcast(U32)
                    return m[:, None, :].broadcast_to([m.shape[0], 8, L])

                def turn(d, l):
                    nc.vector.transpose(fl(XX[d][:]), fl(ZZ[d][:])).then_inc(iX, 1)
                for d in range(2):
                    dve.wait_ge(zi, it * 2 + (d + 1))
                    dve.wait_ge(eA, it * 4 + (2 * d + 2))
                    dve.sem_inc(waits_seen)
                    for e in range(2):
                        ins = nc.vector.copy_predicated(ZZ[d][ROWS[e]], lvl(d, 0, ROWS[e]),
                                                        GP[d][ROWS[e], e, :, 0])
                    ins.then_inc(z0, 1)
                    dve.wait_ge(z0, it * 2 + (d + 1))
                    if not (isinstance(it, int) and it == 0):
                        dve.wait_ge(cU, it * 2 + (d - 1))
                    if kind == "lat" and not (isinstance(it, int) and it == CC):
                        dve.wait_ge(yO[d], it * 16 + -16 * CC)
                    turn(d, 0)
                for l in range(5):
                    for d in range(2):
                        dve.wait_ge(iZ, it * 10 + (2 * l + d + 1))
                        dve.sem_inc(waits_seen)
                        nc.vector.copy_predicated(
                            ZZ[d][:], lvl(d, l + 1),
                            ps[:, 4 * d + 1].rearrange("p (a t) -> p a t", t=L)
                            ).then_inc(iM, 1)
                        if l < 4:
                            dve.wait_ge(iM, it * 10 + (2 * l + d + 1))
                            turn(d, l + 1)
                    if nxt and l == 0:
                        rates(it + 1, 0, nxt)
                    if nxt and l == 1:
                        sums(it + 1, 0)
                        rates(it + 1, 1, nxt)
                    if nxt and l == 2:
                        sums(it + 1, 1)
                if nxt == "lat":
                    dots(it + 1, nxt)
                for d in range(2):
                    dve.wait_ge(cS, it * 2 + (d + 1))
                    if kind == "lat":
                        dve.wait_ge(cY, it * 2 + (d + 1 - 2 * CC))
                    nc.vector.tensor_tensor(ST[d][:], ST[d][:], ps[:, 4 * d + 3].rearrange(
                        "p (a t) -> p a t", t=L), ALU.add).then_inc(sA, 1)
                    dve.wait_ge(sA, it * 2 + (d + 1))
                    nc.vector.tensor_tensor(ST[d][:], ST[d][:], PL[:, d][:, :, None
                                            ].broadcast_to([P, 8, L]), ALU.mult
                                            ).then_inc(sU, 1)
                    if nxt:
                        factors(it + 1, d, nxt)
            turns(dve, body)

        def scan_pool(pool):
            pool.dma_start(CM1[:], cm1[:, 0:NC1 - D]).then_inc(cm1_in, 16)
            pool.wait_ge(z_out, 16)
            pool.dma_start(L2[:], lora2).then_inc(l2_in, 16)
            pool.wait_ge(sc_init, 9)

            def keys(n, kind):
                off = chunk_at(pool, n, kind)
                for d in range(2):
                    pool.wait_ge(pr_g, n * 8 + (4 * d + 2))
                    nc.gpsimd.tensor_tensor(TQ[d][:], TB[d][:], vec("k_a", 0, 8)[:, :, None
                                            ].broadcast_to([P, 8, L]), ALU.mult
                                            ).then_inc(pr_q, 1)
                    nc.gpsimd.tensor_tensor(TK[d][:], toks(KN, off[d]), TB[d][:], ALU.mult
                                            ).then_inc(pr_q, 1)
                    pool.wait_ge(pr_q, n * 8 + (4 * d + 1))
                    nc.gpsimd.tensor_tensor(TQ[d][:], TQ[d][:], OK[:][:, :, None].broadcast_to(
                        [P, 8, L]), ALU.add).then_inc(pr_q, 1)
                    pool.wait_ge(pr_q, n * 8 + (4 * d + 3))
                    nc.gpsimd.tensor_tensor(TQ[d][:], TQ[d][:], toks(KK_, off[d]), ALU.mult
                                            ).then_inc(pr_q, 1)
                    if kind == "lat":
                        pool.wait_ge(pr_q, n * 8 + (4 * d + 4))
                        nc.gpsimd.tensor_tensor(TB[d][:], TQ[d][:],
                                                toks(RR, in_lat(pool, off[d])), ALU.mult
                                                ).then_inc(pr_rr, 1)
            keys(0, "ctx")
            turns(pool, lambda it, kind, nxt: keys(it + 1, nxt) if nxt else None)

        def scan_sync(sp):
            for b in range(2):
                sp.wait_ge(vk_out[b], 64)
            sp.wait_ge(sc_init, 9)
            vk = vk_dram.rearrange("t (m e n) -> t m e n", e=2, n=L)

            def body(it, kind, nxt):
                off = chunk_at(sp, it, kind)
                if kind == "lat":
                    loff = [in_lat(sp, o) for o in off]
                for d in range(2):
                    if kind == "lat" and not (isinstance(it, int) and it == CC):
                        sp.wait_ge(cY, it * 2 + (d - 1 - 2 * CC))
                    elif not (isinstance(it, int) and it == 0):
                        sp.wait_ge(cS, it * 2 + (d - 1))
                    for e in range(2):
                        sp.dma_start(UV[d][ROWS[1 - e], :, e], vk[bass.ds(off[d], L), :, e]
                                     ).then_inc(vI[d], 16)
                if kind == "lat":
                    for d in range(2):
                        sp.wait_ge(yS, it * 2 + (d + 1 - 2 * CC))
                        sp.dma_start(y_dram[d][:, :, bass.ds(loff[d], L)], XX[d][:]
                                     ).then_inc(yO[d], 16)
            turns(sp, body)

        G2 = at("G2", RB + 40.5, [P, 2, D])
        HB = at("HB", RB + 16, [16, D])
        YA = at("YA", RB + 48.5, [P, 2, 3, LAT])
        YC = at("YC", RB, [P, 2, LAT])
        YQ = at("YQ", RB + 4, [P, LAT])
        YD = at("YD", RB + 6, [P, LAT])
        YR = at("YR", RB + 8, [P, LAT])
        YB = at("YB", RB + 10, [P, LAT])
        YT = at("YT", RB + 12, [P, 2, LAT])
        g2_in, y_in, z_in = sem("g2_in"), [sem("y_in0"), sem("y_in1")], sem("z_in")
        po_m, po_q, po_v, po_d = sem("po_m"), sem("po_q"), sem("po_v"), sem("po_d")
        po_t, po_y, po_hi, po_lo = sem("po_t"), sem("po_y"), sem("po_hi"), sem("po_lo")

        def post_pool(pool):
            for d in range(2):
                pool.wait_ge(yO[d], 128)
            pool.wait_ge(sU, 24)
            pool.wait_ge(pr_dt, 16)
            pool.dma_start(G2[:], g2w).then_inc(g2_in, 16)
            pool.dma_start(HB[:], cm1[0:16, C1OFF["hbc"]:C1OFF["hbc"] + D]).then_inc(g2_in, 16)
            pool.wait_ge(vt_out, 16)
            for m in range(8):
                if m >= 2:
                    pool.wait_ge(po_y, m - 1)
                for i, src in enumerate((y_dram[0], y_dram[1], vt_dram)):
                    pool.dma_start(YA[:, m % 2, i], src[:, m]).then_inc(y_in[m % 2], 16)

        def post_zin(pool):
            pool.wait_ge(po_lo, 8)
            pool.dma_start(z[:, :, LC:T], z_dram).then_inc(z_in, 16)

        def post_pe(pe):
            pe.wait_ge(g2_in, 32)
            pe.wait_ge(g1_ready, 1)
            for m in range(8):
                pe.wait_ge(po_t, 6 * m + 1)
                nc.tensor.matmul(ps[:, 4], bd, YC[:, m % 2], start=True, stop=True
                                 ).then_inc(po_m, 1)
                pe.wait_ge(po_y, m)
                nc.tensor.matmul(ps[:, 5], HB[:, P * m:P * m + P], DOT[:], start=True,
                                 stop=True)
                nc.tensor.matmul(ps[:, 6], G2[:, 0, P * m:P * m + P], G1[:, 0], start=True,
                                 stop=False)
                nc.tensor.matmul(ps[:, 6], G2[:, 1, P * m:P * m + P], G1[:, 1], start=False,
                                 stop=True)
                pe.wait_ge(po_q, m + 1)
                nc.tensor.matmul(ps[:, 7], bd, YQ[:], start=True, stop=True).then_inc(po_v, 1)

        def post_act(act):
            for m in range(8):
                act.wait_ge(po_t, 6 * m + 2)
                nc.scalar.activation(YQ[:], YC[:, m % 2], ACT.Square).then_inc(po_q, 1)
                act.wait_ge(po_v, m + 1)
                act.wait_ge(po_t, 6 * m)
                nc.scalar.activation(YD[:], ps[:, 7], ACT.Sqrt, bias=CO[:, 65:66], scale=1.0 / L
                                     ).then_inc(po_d, 1)
                act.wait_ge(po_y, m + 1)
                nc.scalar.activation(XH[:, m, LC:T], YT[:, m % 2], ACT.Copy).then_inc(po_hi, 1)

        def post_dve(dve):
            dve.wait_ge(pr_dt, 16)
            for m in range(8):
                dve.wait_ge(y_in[m % 2], 48 * (m // 2 + 1))
                yc = YC[:, m % 2]
                nc.vector.tensor_tensor(yc, YA[:, m % 2, 0], YA[:, m % 2, 1], ALU.add
                                        ).then_inc(po_t, 1)
                dve.wait_ge(po_m, m + 1)
                nc.vector.scalar_tensor_tensor(out=yc, in0=ps[:, 4], scalar=-1.0 / L, in1=yc,
                                               op0=ALU.mult, op1=ALU.add).then_inc(po_t, 1)
                dve.wait_ge(po_d, m + 1)
                nc.vector.reciprocal(YR[:], YD[:]).then_inc(po_t, 1)
                dve.wait_ge(po_t, 6 * m + 3)
                yt = YT[:, m % 2]
                if m >= 2:
                    dve.wait_ge(po_hi, m - 1)
                    dve.wait_ge(po_lo, m - 1)
                nc.vector.tensor_tensor(yt, yc, YR[:], ALU.mult).then_inc(po_t, 1)
                nc.vector.tensor_tensor(YB[:], ps[:, 5], YA[:, m % 2, 2], ALU.mult)
                dve.wait_ge(po_t, 6 * m + 4)
                nc.vector.tensor_scalar(yt, yt, vec("ln_g", m), vec("ln_b", m), ALU.mult, ALU.add
                                        ).then_inc(po_t, 1)
                dve.wait_ge(po_t, 6 * m + 5)
                nc.vector.tensor_tensor(yt, yt, YB[:], ALU.add).then_inc(po_t, 1)
                dve.wait_ge(po_t, 6 * m + 6)
                nc.vector.tensor_tensor(yt, ps[:, 6], yt, ALU.mult).then_inc(po_y, 1)
                dve.wait_ge(po_hi, m + 1)
                nc.vector.tensor_tensor(XL[:, m, LC:T], yt, XH[:, m, LC:T].bitcast(F32),
                                        ALU.subtract).then_inc(po_lo, 1)

        block = ctx.enter_context(nc.Block())

        @block.sync
        def _(sp):
            sp.dma_start(PV[:], pv).then_inc(consts_in, 16)
            sp.dma_start(CM[:], cm).then_inc(consts_in, 16)
            ada_sync(sp)
            sp.dma_start(z[:], zin).then_inc(consts_in, 16)
            load_weights(sp)
            sp.wait_ge(acc_lat, NT)
            sp.dma_start(out, z[:, :, LC:T]).then_inc(out_done, 16)
            sp.wait_ge(out_done, 16)

        @block.gpsimd
        def _(pool):
            ada_pool(pool)
            pool.dma_start(CM0[:], cm0).then_inc(cm0_in, 16)
            attn_pool(pool)
            vk_pool(pool)
            scan_pool(pool)
            post_pool(pool)
            post_zin(pool)

        @block.tensor
        def _(pe):
            pe.wait_ge(consts_in, 32)
            ada_pe(pe)
            mod_pe(pe, 0)
            norm_pe(pe, 0, SEGS)
            gemm_pe(pe, T_IN, N_IN, SEGS, 0, XH, XL, x_wait=(x_lo, 8))
            ml_gates_pe(pe)
            ml_pe(pe)
            fin_pe(pe)
            attn_pe(pe)
            gemm_pe(pe, T_OUT0, 8, SEGS, T_OUT0, XH, XL, x_wait=(at_lo, 6))
            mod_pe(pe, 1)
            norm_pe(pe, 1, SEGS)
            mlp(pe, "pe", 0, T_MLP0, SEGS, T_MLP0, (x_lo, 16))
            norm_pe(pe, 2, SEGS)
            for q, (i, t0, n, segs) in enumerate(MIXES):
                gemm_pe(pe, t0, n, segs, t0, XH, XL, x_wait=(x_lo, 24 + 8 * q))
                if q == 0:
                    vk_pe(pe)
            kk_pe(pe)
            scan_pe(pe)
            post_pe(pe)
            gemm_pe(pe, T_OUT1, 8, (LATS,), 0, XH, XL, x_wait=(po_lo, 8))
            norm_pe(pe, 3, (LATS,))
            mlp(pe, "pe", 1, T_MLP1, (LATS,), 0, (x_lo, 72))

        @block.scalar
        def _(act):
            ada_act(act)
            split_hi(0, 0, 0)
            split_hi(1, 0, 1)
            norm_act(act, 0, SEGS, [(consts_in, 48)], True)
            step_act(act, T_IN, N_IN, in_act)
            ml_gates_act(act)
            ml_act(act)
            fin_act(act)
            attn_act(act)
            step_act(act, T_OUT0, 8, None)
            norm_act(act, 1, SEGS, [(acc_lat, T_MLP0), (acc_ctx, T_MLP0)], True)
            mlp(act, "act", 0, T_MLP0, SEGS, T_MLP0, None)
            norm_act(act, 2, SEGS, [(acc_lat, T_V), (acc_ctx, T_V)], False)
            for q, (i, t0, n, segs) in enumerate(MIXES):
                if q == 1:
                    vk_act(act)
                mix_act(act, q)
                if q == 1:
                    act.wait_ge(vt_out, 16)
                    act.wait_ge(vk_t, 8)
                step_act(act, t0, n, mix_evict(q, "act"))
            kk_act(act)
            scan_act(act)
            post_act(act)
            step_act(act, T_OUT1, 8, None)
            norm_act(act, 3, (LATS,), [(acc_lat, T_MLP1)], True)
            mlp(act, "act", 1, T_MLP1, (LATS,), 0, None)

        @block.vector
        def _(dve):
            ada_dve(dve)
            split_lo(0, 0, 0)
            split_lo(1, 0, 1)
            mod_dve(dve, 0)
            norm_dve(dve, 0, SEGS, [(consts_in, 48)], 0, True)
            step_dve(dve, T_IN, N_IN, in_dve)
            ml_gates_dve(dve)
            ml_dve(dve)
            fin_dve(dve)
            attn_dve(dve)
            step_dve(dve, T_OUT0, 8, res_dve(0, 2, SEGS))
            mod_dve(dve, 1)
            norm_dve(dve, 1, SEGS, [(acc_lat, T_MLP0), (acc_ctx, T_MLP0)], 8, True)
            mlp(dve, "dve", 0, T_MLP0, SEGS, T_MLP0, None)
            norm_dve(dve, 2, SEGS, [(acc_lat, T_V), (acc_ctx, T_V)], 16, False)
            mu = vec("mu", 0, 96).rearrange("p (i s k) -> p i s k", i=6, s=2)
            nc.vector.scalar_tensor_tensor(out=MC[:], in0=mu[:, :, 0], scalar=-1.0,
                                           in1=mu[:, :, 1], op0=ALU.mult, op1=ALU.subtract
                                           ).then_inc(mc_ready, 1)
            dve.wait_ge(mc_ready, 1)
            nc.vector.tensor_scalar(MC[:], MC[:], 1.0, None, ALU.add).then_inc(mc_ready, 1)
            for q, (i, t0, n, segs) in enumerate(MIXES):
                mix_dve(dve, q)
                if q == 1:
                    dve.wait_ge(vt_out, 16)
                    dve.wait_ge(vk_t, 8)
                step_dve(dve, t0, n, mix_evict(q, "dve"))
            kk_dve(dve)
            scan_dve(dve)
            post_dve(dve)
            dve.wait_ge(z_in, 16)
            step_dve(dve, T_OUT1, 8, res_dve(1, 2, (LATS,)))
            norm_dve(dve, 3, (LATS,), [(acc_lat, T_MLP1)], 64, True)
            mlp(dve, "dve", 1, T_MLP1, (LATS,), 0, None)


def _tiles(w):
    return w.reshape(KT, P, -1, P).transpose(2, 1, 0, 3)


def _cols(v):
    v = v.reshape(-1, P)
    return v.T


GATE_ROWS = np.concatenate([np.arange(4) + r for r in (0, 32, 64, 96)])
GATE_COLS = np.concatenate([np.arange(4) + g for g in (0, 8, 4, 12)])


def pack(a):
    f = np.float32
    a = {k: np.ascontiguousarray(v) for k, v in a.items()}
    zz = np.concatenate([a["ctx"][0], a["x"][0]], 0)
    zin = zz.T.reshape(KT, P, T).transpose(1, 0, 2)
    wi = a["ev_w_in"][0]
    bi = a["ev_b_in"][0]
    gw = np.zeros((D, P), f)
    gb = np.zeros((P,), f)
    gw[:, GATE_ROWS] = wi[:, 2048 + GATE_COLS]
    gb[GATE_ROWS] = bi[2048 + GATE_COLS]
    fb = np.zeros((P,), f)
    fb[[64, 65, 66, 67]] = a["ml_f_bias"][0, 0]
    fb[[96, 97, 98, 99]] = a["ml_f_bias"][0, 1]
    w_in = np.concatenate([wi[:, :2048], gw, wi[:, 2064:]], 1)
    b_in = np.concatenate([bi[:2048], gb, bi[2064:]])

    def mlp(layer):
        w1, w2 = _tiles(a["mlp_w1"][layer]), a["mlp_w2"][layer]
        return [x for g in range(4) for x in (w1[8 * g:8 * g + 8], _tiles(w2[D * g:D * g + D]))]
    g1 = np.concatenate([a["rw_g1"][0], np.zeros((D, 256 - 160), f)], 1)
    rkv = a["rw_w_rkv"][0]
    wall = np.concatenate(
        [_tiles(w_in), _tiles(a["ev_w_out"][0]), *mlp(0), _tiles(rkv[2]), _tiles(rkv[1]),
         _tiles(np.concatenate([a["rw_w1"][0, 0], a["rw_w1"][0, 1]], 1)),
         _tiles(np.concatenate([a["rw_a1"][0, 0], a["rw_a1"][0, 1]], 1)), _tiles(rkv[0]),
         _tiles(g1), _tiles(a["rw_w_out"][0]), *mlp(1)], 0)
    ada = np.concatenate([_tiles(a["ada_w"][0]), _tiles(a["ada_w"][1])], 0)
    cc = np.stack([a["c_ctx"], a["c"][0]], 0).reshape(2, KT, P).transpose(2, 1, 0).reshape(P, 16)
    pv = np.concatenate(
        [cc, _cols(a["ada_b"]), _cols(a["norm1_g"]), _cols(a["norm2_g"]), _cols(b_in),
         fb[:, None], _cols(a["ml_out_g"][0]), np.tile(a["at_q_g"][0], 2)[:, None],
         np.tile(a["at_k_g"][0], 2)[:, None], np.broadcast_to(a["at_sink"][0], (P, 8)),
         _cols(a["rw_mu"][0]), _cols(a["rw_w0"][0]), _cols(a["rw_a0"][0]), _cols(a["rw_k_k"][0]),
         _cols(a["rw_k_a"][0]), _cols(a["rw_r_k"][0]), _cols(a["rw_ln_g"][0]),
         _cols(a["rw_ln_b"][0])], 1)
    lora2 = np.stack([a["rw_w2"][0].reshape(P, D), a["rw_a2"][0].reshape(P, D)], 1)
    g2 = np.zeros((P, 2, D), f)
    g2[:, 0] = a["rw_g2"][0, :P]
    g2[:160 - P, 1] = a["rw_g2"][0, P:]
    return dict(zin=zin, wall=wall, ada=ada, pv=pv, lora2=lora2, g2w=g2, **tables())


def tables():
    f = np.float32
    i = np.arange(P)
    cm = np.concatenate([np.eye(P), np.ones((P, P)), (i[:, None] // 64 == i[None] // 64)], 1)
    perm = np.zeros((P, P))
    for m in range(P):
        if m % 32 < 16:
            perm[m + 16, m] = -1.0
        else:
            perm[m - 16, m] = 1.0
    neg = np.concatenate([np.where(i[:, None] <= i[None], 0, NEG),
                          np.where(i[:, None] >= i[None], 0, NEG)], 1)
    inv = (10000.0 ** (-np.arange(16, dtype=f) / f(16))).astype(f)
    t = np.arange(LAT)
    pos = np.where((i[:, None] % 64) < 32, (t // 64)[None], (t % 64)[None]).astype(f)
    ang = (pos * inv[i % 16][:, None]).astype(f)
    sel = np.zeros((P, 8, P))
    for d in range(2):
        for h in range(4):
            sel[32 * d + h, 4 * d + h] = 1
    reset = np.broadcast_to(np.arange(T) % P != 0, (P, T))
    cm0 = np.concatenate([perm, neg, np.cos(ang), np.sin(ang), sel.reshape(P, -1), reset], 1)
    j, r = np.arange(64), (i % 64)[:, None]
    lvl = [[], []]
    for s in (1, 2, 4, 8, 16, 32):
        pair = r // (2 * s) == j[None] // (2 * s)
        low, high = r % (2 * s) < s, j[None] % (2 * s) >= s
        lvl[0].append(pair & low & high)
        lvl[1].append(pair & ~low & ~high)
    hsel = np.zeros((P, 8, 16))
    hbc = np.zeros((P, 8, P))
    for p in range(8):
        for e in range(2):
            hsel[64 * e:64 * e + 64, p, 2 * p + e] = 1
            hbc[2 * p + e, p, 64 * e:64 * e + 64] = 1
    j = j[None]
    cm1 = np.concatenate([r < j, r <= j, r > j, r >= j, *lvl[0], *lvl[1], r == j,
                          np.broadcast_to(np.arange(512) % 64 != 0, (P, 512)),
                          hsel.reshape(P, -1), hbc.reshape(P, -1)], 1)
    return {"cm": cm.astype(f), "cm0": cm0.astype(f), "cm1": cm1.astype(f)}


SCRATCH = [("z_dram", (P, KT, LAT)), ("vt_dram", (P, KT, LAT)), ("vk_dram", (T, D)),
           ("y_dram", (2, P, KT, LAT)), ("mod_dram", (2, 2, 6 * D))]


def kernel(**inputs):
    import concourse.bacc as _bacc
    from concourse.bass_utils import run_bass_kernel_spmd as _run

    packed = {k: np.ascontiguousarray(v, dtype=np.float32)
              for k, v in pack({k: np.asarray(v) for k, v in inputs.items()}).items()}
    nc = _bacc.Bacc("TRN2", target_bir_lowering=False, num_devices=1)
    dram = {k: nc.dram_tensor(f"{k}_dram", v.shape, F32, kind="ExternalInput").ap()
            for k, v in packed.items()}
    scratch = {k: nc.dram_tensor(k, shape, F32, kind="Internal").ap() for k, shape in SCRATCH}
    out = nc.dram_tensor("out_dram", (P, KT, LAT), F32, kind="ExternalOutput").ap()
    trunk(nc, out=out, **dram, **scratch)
    r = _run(nc, [{f"{k}_dram": v for k, v in packed.items()}], core_ids=[0])
    y = r.results[0]["out_dram"]
    return np.ascontiguousarray(y.transpose(2, 1, 0)).reshape(1, LAT, D)
```

```python
from contextlib import ExitStack

import numpy as np

import concourse.bass as bass
from concourse import mybir

F32 = mybir.dt.float32
F32R = mybir.dt.float32r
U32 = mybir.dt.uint32
ALU = mybir.AluOpType
ACT = mybir.ActivationFunctionType
AX = mybir.AxisListType

P = 128
D = 1024
KT = D // P
LC = 256
LAT = 512
T = LC + LAT
EPS = 1e-6
LN_EPS = 64e-5
CAP = 15.0
NEG = -1e30
KAPPA = float(np.exp(-0.5))
L = 64
SEGS = ((0, LC), (LC, LAT))
CTX, LATS = SEGS

N_IN = 23
T_IN = 0
T_OUT0 = T_IN + N_IN
T_MLP0 = T_OUT0 + 8
T_V = T_MLP0 + 64
T_K = T_V + 8
T_W = T_K + 8
T_A = T_W + 1
T_R = T_A + 1
T_G = T_R + 8
T_OUT1 = T_G + 2
T_MLP1 = T_OUT1 + 8
NT = T_MLP1 + 64


def offsets(table):
    at, n = {}, 0
    for name, width in table:
        at[name] = n
        n += width
    return at, n


VOFF, NV = offsets([("c", 16), ("ada_b", 96), ("g1", 16), ("g2", 16), ("b_in", N_IN), ("fb", 1),
                    ("out_g", 4), ("q_g", 1), ("k_g", 1), ("sink", 8), ("mu", 96), ("w0", 16),
                    ("a0", 16), ("k_k", 8), ("k_a", 8), ("r_k", 8), ("ln_g", 8), ("ln_b", 8)])
COFF, NC = offsets([("ident", 128), ("ones", 128), ("bd", 128)])
C0OFF, NC0 = offsets([("perm", 128), ("neg", 256), ("cos", 512), ("sin", 512), ("sel", 1024),
                      ("reset", 768), ("nsel", 144), ("nbc", 1152)])
C1OFF, NC1 = offsets([("tri", 256), ("lvl", 768), ("eye", 64),
                      ("reset", 512), ("hsel", 128), ("hbc", 1024)])


def trunk(nc, zin, wall, ada, pv, cm, cm0, cm1, lora2, g2w, out, z_dram, vt_dram, vk_dram,
          y_dram, mod_dram):
    ctx = ExitStack()
    with ctx:
        BASE = 16512

        def at(name, kb, shape, dt=F32):
            return nc.alloc_sbuf_tensor_at(name, shape, dt, offset=BASE + int(kb * 1024))

        def sem(name):
            return ctx.enter_context(nc.semaphore(name))

        z = at("z", 0, [P, KT, T])
        WR = at("WR", 24, [P, 2, KT, P])
        WH = at("WH", 32, [P, 2, KT, P], F32R)
        WL = at("WL", 40, [P, 2, KT, P], F32R)
        PV = at("PV", 48, [P, NV])
        MOD = at("MOD", 50, [P, 2, 48, 2])
        CO = at("CO", 50.75, [P, 80])
        CM = at("CM", 51.125, [P, NC])
        CM1 = at("CM1", 53, [P, NC1 - D])
        RA = 62
        RB = RA + 48
        XH = at("XH", RA, [P, KT, T], F32R)
        XL = at("XL", RA + 24, [P, KT, T], F32R)
        ps = ctx.enter_context(nc.psum_tensor("ps", [P, 8, 512], F32))
        SILU = at("SILU", 51.0625, [P, 16])
        SG = at("SG", 52.625, [P, 32])
        ADA = at("ADA", RB + 27, [P, 4, 2, KT, P])
        ROW = at("ROW", RB + 59, [2, 6 * D])
        ROWT = at("ROWT", 60, [96, P])
        NS = [{k: at(f"{k}{i}", o + b, s) for k, b, s in (
            ("SQ", 0, [P, 2, T]), ("ACC", 6, [P, T]), ("STD", 9, [P, T]), ("RS", 12, [P, T]),
            ("TM", 15, [P, 2, T]), ("HF", 21, [P, 2, T]))}
            for i, o in enumerate((RB, RB + 60))]
        Q = at("Q", RB, [P, N_IN, T])
        H = at("H", RB + 69, [P, 4, T])
        CM0 = at("CM0", RB + 81, [P, C0OFF["nsel"]])
        N5 = at("N5", RA, [64, 5, T])
        R5 = at("R5", RA + 15, [64, 5, T])
        BC = at("BC", RA + 30, [64, T])
        GM = at("GM", RA + 33, [64, T])
        IG = at("IG", RA + 36, [64, T])
        LF = at("LF", RA + 39, [64, T])
        GX = at("GX", RA + 42, [P, T])
        GF = at("GF", RA + 45, [64, T])
        MM = at("MM", 52.75, [64, 8])
        KVT = at("KVT", RA + 15, [P, 8, P])
        KVK = at("KVK", RA + 19, [P, 8, P])
        EE = at("EE", RA + 23, [P, 4, P])
        IW = at("IW", RA + 25, [P, 4, P])
        FL = at("FL", RA + 27, [P, 4, P])
        WM = at("WM", RA + 29, [P, 4, P])
        QT = at("QT", RA + 31, [P, 4, P])
        VW = at("VW", RA + 33, [P, 4, P + 1])
        YM = at("YM", RA + 35.25, [P, 4, P])
        CT = at("CT", RA + 37.25, [P, 2, 4, P + 1])
        NR = at("NR", RA + 41.5, [P, 4, P])
        CS = at("CS", RA + 43.5, [P, 6, 64])
        CW = at("CW", RA + 45, [P, 6, 64])

        def vec(name, j=0, n=1):
            return PV[:, VOFF[name] + j:VOFF[name] + j + n]

        def vecd(name, j):
            return PV[:, bass.ds(j + VOFF[name], 1)]

        def cmat(name, n=128):
            return CM[:, COFF[name]:COFF[name] + n]

        def c0(name, a, n):
            return CM0[:, C0OFF[name] + a:C0OFF[name] + a + n]

        def c1(name, a, n):
            return CM1[:, C1OFF[name] + a:C1OFF[name] + a + n]

        ident, ones, bd = cmat("ident"), cmat("ones"), cmat("bd")

        consts_in = sem("consts_in")
        cm0_in = sem("cm0_in")
        ada_in = [sem(f"ada_in{j}") for j in range(4)]
        silu = sem("silu")
        ada_done, ada_row, rowt_in, mod_t = (sem("ada_done"), sem("ada_row"), sem("rowt_in"),
                                             sem("mod_t"))
        mod_out = sem("mod_out")
        mod_ready = sem("mod_ready")
        w_in = [sem("w_in0"), sem("w_in1")]
        w_hi, w_lo, tile_done = sem("w_hi"), sem("w_lo"), sem("tile_done")
        acc_lat, acc_ctx = sem("acc_lat"), sem("acc_ctx")
        n_sq, n_acc, n_stat, n_std = sem("n_sq"), sem("n_acc"), sem("n_stat"), sem("n_std")
        n_tm, n_h = sem("n_tm"), sem("n_h")
        x_hi, x_lo = sem("x_hi"), sem("x_lo")
        hid_sq, hid_hi, hid_lo = sem("hid_sq"), sem("hid_hi"), sem("hid_lo")
        out_done = sem("out_done")
        waits_seen = sem("waits_seen")

        def tile_loop(eng, t0, n, body, peel=0, skip=0):
            for m in range(min(peel, n)):
                body(t0 + m, (t0 + m) // 2, m, (t0 + m) % 2)
            peel = max(peel, skip)
            pairs = (n - peel) // 2
            if pairs > 1:
                with eng.Fori(0, pairs) as i:
                    for j in range(2):
                        b = t0 + peel + j
                        body(i * 2 + b, i + b // 2, i * 2 + (peel + j), b % 2)
            else:
                pairs = 0
            for m in range(peel + 2 * pairs, n):
                body(t0 + m, (t0 + m) // 2, m, (t0 + m) % 2)

        def load_weights(sp):

            def body(t, half, m, s):
                sp.wait_ge(w_hi, t - 1)
                sp.wait_ge(w_lo, t - 1)
                sp.dma_start(WR[:, s], wall[bass.ds(t, 1)].rearrange("a p k m -> (a p) k m")
                             ).then_inc(w_in[s], 16)

            def until(a, b):
                tile_loop(sp, a, b - a, body)
            until(2, T_OUT0 + 4)
            until(T_OUT0 + 4, T_OUT1 + 4)
            scan_sync(sp)
            post_sync(sp)
            until(T_OUT1 + 4, NT)

        def split_hi(t, half, s):
            nc.scalar.wait_ge(w_in[s], (half + 1) * 16)
            nc.scalar.activation(WH[:, s], WR[:, s], ACT.Copy).then_inc(w_hi, 1)

        def split_lo(t, half, s):
            nc.vector.wait_ge(w_in[s], (half + 1) * 16)
            nc.vector.wait_ge(w_hi, t + 1)
            nc.vector.tensor_tensor(WL[:, s], WR[:, s], WH[:, s].bitcast(F32),
                                    ALU.subtract).then_inc(w_lo, 1)

        def gemm_pe(pe, t0, n, segs, c_before, xh, xl, x_wait=None, last_wait=None, paced=None):
            def ready(t, m):
                pe.wait_ge(w_hi, t + 1)
                pe.wait_ge(w_lo, t + 1)
                if not isinstance(t, int) or t >= 2:
                    pe.wait_ge(acc_lat, t - 1)
                if CTX in segs:
                    cc = c_before + m - 1
                    if not isinstance(cc, int) or cc >= 1:
                        pe.wait_ge(acc_ctx, cc)

            def products(s, k):
                for a, b, first in ((WH, xh, True), (WH, xl, False), (WL, xh, False)):
                    for sg in segs:
                        bank = 2 * s + (0 if sg is LATS else 1)
                        mm = nc.tensor.matmul(
                            ps[:, bank, 0:sg[1]], a[:, s, k], b[:, k, sg[0]:sg[0] + sg[1]],
                            start=(k == 0 and first), stop=(k == KT - 1 and a is WL))
                return mm

            def body(t, half, m, s):
                if x_wait is not None:
                    pe.wait_ge(*x_wait)
                ready(t, m)
                for k in range(KT):
                    if k == KT - 1 and last_wait is not None:
                        pe.wait_ge(*last_wait)
                    mm = products(s, k)
                mm.then_inc(tile_done, 1)

            side = 0
            if paced is not None:
                side = min(2, n)
                for k in range(KT):
                    pe.wait_ge(paced[0], paced[1] + k + 1)
                    for j in range(side):
                        if k == 0:
                            ready(t0 + j, j)
                        mm = products((t0 + j) % 2, k)
                        if k == KT - 1:
                            mm.then_inc(tile_done, 1)
            tile_loop(pe, t0, n, body, skip=side)

        def acc(s, sg):
            return ps[:, 2 * s + (0 if sg is LATS else 1), 0:sg[1]]

        def step_act(act, t0, n, evict, peel=0):
            def body(t, half, m, s):
                act.wait_ge(tile_done, t + 1)
                if evict is not None:
                    evict(t, m, s)
                if not isinstance(t, int) or t + 2 < NT:
                    split_hi(t + 2, half + 1, s)
            lim = max(0, min(n, NT - 2 - t0))
            tile_loop(act, t0, lim, body, peel)
            for m in range(lim, n):
                body(t0 + m, (t0 + m) // 2, m, (t0 + m) % 2)

        def step_dve(dve, t0, n, evict, peel=0):
            def body(t, half, m, s):
                dve.wait_ge(tile_done, t + 1)
                if evict is not None:
                    evict(t, m, s)
                if not isinstance(t, int) or t + 2 < NT:
                    split_lo(t + 2, half + 1, s)
            lim = max(0, min(n, NT - 2 - t0))
            tile_loop(dve, t0, lim, body, peel)
            for m in range(lim, n):
                body(t0 + m, (t0 + m) // 2, m, (t0 + m) % 2)


        def ada_sync(sp, lo, hi):
            def group(g, slot):
                sp.dma_start(ADA[:, slot], ada[bass.ds(g * 2, 2)].rearrange(
                    "a p k m -> p a k m")).then_inc(ada_in[slot], 16)
            if lo == 0:
                for j in range(4):
                    group(j, j)
                lo = 4
            with sp.Fori(lo // 4, hi // 4) as i:
                for j in range(4):
                    sp.wait_ge(ada_done, i * 4 + (j - 3))
                    group(i * 4 + j, j)

        def ada_pe(pe, lo, hi):
            def group(i, j):
                pe.wait_ge(ada_in[j], i * 16 + 16)
                if not (isinstance(i, int) and j < 2):
                    pe.wait_ge(ada_row, i * 4 + (j - 1))
                for k in range(KT):
                    mm = nc.tensor.matmul(ps[0:2, 4 + j % 2, 0:256], SILU[:, 2 * k:2 * k + 2],
                                          ADA[:, j, :, k], start=k == 0, stop=k == KT - 1)
                mm.then_inc(ada_done, 1)
            if lo == 0:
                pe.wait_ge(silu, 3)
                for j in range(4):
                    group(0, j)
                lo = 4
            with pe.Fori(lo // 4, hi // 4) as i:
                for j in range(4):
                    group(i, j)

        def silu_act(act):
            act.wait_ge(consts_in, 32)
            nc.scalar.activation(SG[:, 0:16], vec("c", 0, 16), ACT.Tanh, scale=0.5
                                 ).then_inc(silu, 1)

        def ada_act(act, layer, g, s):
            act.wait_ge(ada_done, g + (24 * layer + 1))
            nc.scalar.activation(ROW[:, bass.ds(g * 256, 256)], ps[0:2, 4 + s, 0:256], ACT.Copy
                                 ).then_inc(ada_row, 1)

        def ada_pool(pool, layer):
            pool.wait_ge(ada_row, 24 * layer + 24)
            pool.dma_start(mod_dram[layer], ROW[:]).then_inc(mod_out, 16)
            pool.wait_ge(mod_out, 16 * layer + 16)
            if layer:
                pool.wait_ge(mod_t, 1)
            pool.dma_start(ROWT[:], mod_dram[layer].rearrange("c (m n) -> (c m) n", n=P)
                           ).then_inc(rowt_in, 16)

        def mod_pe(pe, layer):
            pe.wait_ge(rowt_in, 16 * layer + 16)
            nc.tensor.transpose(ps[:, 5 * layer, 0:96], ROWT[:], ident[0:96, 0:96]
                                ).then_inc(mod_t, 1)

        def silu_dve(dve):
            dve.wait_ge(consts_in, 32)
            dve.wait_ge(silu, 1)
            nc.vector.tensor_scalar(SG[:, 16:32], SG[:, 0:16], 0.5, 0.5, ALU.mult, ALU.add
                                    ).then_inc(silu, 1)
            dve.wait_ge(silu, 2)
            nc.vector.tensor_tensor(SILU[:], SG[:, 16:32], vec("c", 0, 16), ALU.mult
                                    ).then_inc(silu, 1)
            nc.vector.memset(CO[:, 64:65], EPS).then_inc(mod_ready, 1)
            nc.vector.memset(CO[:, 65:66], LN_EPS).then_inc(mod_ready, 1)
            nc.vector.memset(CO[:, 66:67], 1.0).then_inc(mod_ready, 1)

        def mod_dve(dve, layer):
            dve.wait_ge(mod_t, layer + 1)
            nc.vector.tensor_tensor(
                MOD[:, layer], ps[:, 5 * layer, 0:96].rearrange("p (c m) -> p m c", c=2),
                vec("ada_b", 48 * layer, 48)[:, :, None].broadcast_to([P, 48, 2]), ALU.add
                ).then_inc(mod_ready, 1)
            dve.wait_ge(mod_ready, 4 + 3 * layer)
            for n in (2 * layer, 2 * layer + 1):
                sc = MOD[:, layer, 8 + 24 * (n % 2):16 + 24 * (n % 2), :]
                g = vec("g1" if n % 2 == 0 else "g2", 8 * layer, 8)
                nc.vector.scalar_tensor_tensor(
                    out=CO[:, 16 * n:16 * n + 16].rearrange("p (k c) -> p k c", c=2), in0=sc,
                    scalar=1.0, in1=g[:, :, None].broadcast_to([P, 8, 2]), op0=ALU.add,
                    op1=ALU.mult).then_inc(mod_ready, 1)

        def norm_pe(pe, n, segs):
            pe.wait_ge(n_acc, 8 * n + 8)
            for sg in segs:
                mm = nc.tensor.matmul(ps[:, 6 if sg is LATS else 7, 0:sg[1]], ones,
                                      NS[NSI[n]]["ACC"][:, sg[0]:sg[0] + sg[1]], start=True,
                                      stop=True)
            mm.then_inc(n_stat, 1)

        NSI = {0: 0, 1: 1, 2: 1, 3: 1}
        NZ = {1: ((acc_lat, T_MLP0), (acc_ctx, T_MLP0)), 2: ((acc_lat, T_V), (acc_ctx, T_V)),
              3: ((acc_lat, T_MLP1),)}
        ZA = {0: 0, 1: 0, 2: 0, 3: LC}

        def square(act, n, k, z_wait):
            for name, v in z_wait:
                act.wait_ge(name, v - (KT - 1 - k) if n else v)
            if k >= 2:
                act.wait_ge(n_acc, 8 * n + k - 1)
            nc.scalar.activation(NS[NSI[n]]["SQ"][:, k % 2, ZA[n]:T], z[:, k, ZA[n]:T],
                                 ACT.Square).then_inc(n_sq, 1)

        def add_square(dve, n, k):
            B, a = NS[NSI[n]], ZA[n]
            dve.wait_ge(n_sq, 8 * n + k + 1)
            if k == 0:
                nc.vector.tensor_copy(B["ACC"][:, a:T], B["SQ"][:, 0, a:T]).then_inc(n_acc, 1)
            else:
                dve.wait_ge(n_acc, 8 * n + k)
                nc.vector.tensor_tensor(B["ACC"][:, a:T], B["ACC"][:, a:T],
                                        B["SQ"][:, k % 2, a:T], ALU.add).then_inc(n_acc, 1)

        def last_act(n, z_wait):
            def evict(t, m, s):
                if m:
                    square(nc.scalar, n, m - 1, z_wait)
            return evict

        def last_dve(n, residual):
            def evict(t, m, s):
                residual(t, m, s)
                if m:
                    add_square(nc.vector, n, m - 1)
            return evict

        def norm_act(act, n, segs, z_wait, split):
            B = NS[NSI[n]]
            a = ZA[n]
            if n == 0:
                act.wait_ge(mod_out, 16)
            for k in range(KT - 1 if n else 0, KT):
                square(act, n, k, z_wait)
                if n == 0:
                    ada_act(act, 1, k, k % 2)
            act.wait_ge(n_stat, n + 1)
            act.wait_ge(mod_ready, 6 if n < 2 else 9)
            for sg in segs:
                nc.scalar.activation(B["STD"][:, sg[0]:sg[0] + sg[1]],
                                     ps[:, 6 if sg is LATS else 7, 0:sg[1]], ACT.Sqrt,
                                     bias=CO[:, 64:65], scale=1.0 / D).then_inc(n_std, 1)
            if split:
                for k in range(KT):
                    act.wait_ge(n_h, 8 * n + k + 1)
                    nc.scalar.activation(XH[:, k, a:T], B["HF"][:, k % 2, a:T], ACT.Copy
                                         ).then_inc(x_hi, 1)
                    if n == 0:
                        for g in (8 + 2 * k, 9 + 2 * k):
                            ada_act(act, 1, g, g % 2)

        def norm_dve(dve, n, segs, z_wait, x0, split):
            B = NS[NSI[n]]
            a = ZA[n]
            for w in z_wait:
                dve.wait_ge(*w)
            if not split:
                for c in (1, 258, 259, T + 4):
                    nc.vector.memset(U[:, :, c:c + 1], 0.0)
            for k in range(KT - 1 if n else 0, KT):
                add_square(dve, n, k)
            if n == 0:
                mod_dve(dve, 0)
            dve.wait_ge(n_std, NSTD[n] + len(segs))
            nc.vector.reciprocal(B["RS"][:, a:T], B["STD"][:, a:T]).then_inc(n_tm, 1)
            dve.wait_ge(n_tm, 9 * n + 1)
            sh = 24 * (n % 2)
            for k in range(KT):
                if k >= 2:
                    dve.wait_ge(n_h, 8 * n + k - 1)
                nc.vector.tensor_tensor(B["TM"][:, k % 2, a:T], z[:, k, a:T], B["RS"][:, a:T],
                                        ALU.mult).then_inc(n_tm, 1)
                dve.wait_ge(n_tm, 9 * n + k + 2)
                if split and k >= 2:
                    dve.wait_ge(x_hi, x0 + k - 1)
                    dve.wait_ge(x_lo, x0 + k - 1)
                for i, sg in enumerate(segs):
                    v = SEGS.index(sg)
                    if split:
                        o = B["HF"][:, k % 2, sg[0]:sg[0] + sg[1]]
                    else:
                        o = U[:, k, 2 + 2 * v + sg[0]:2 + 2 * v + sg[0] + sg[1]]
                    ins = nc.vector.tensor_scalar(
                        o, B["TM"][:, k % 2, sg[0]:sg[0] + sg[1]],
                        CO[:, 16 * n + 2 * k + v:16 * n + 2 * k + v + 1],
                        MOD[:, n // 2, sh + k, v:v + 1], ALU.mult, ALU.add)
                ins.then_inc(n_h, 1)

        def norm_pool(pool, n, x0):
            a = ZA[n]
            for k in range(KT):
                pool.wait_ge(x_hi, x0 + k + 1)
                nc.gpsimd.tensor_tensor(XL[:, k, a:T], NS[NSI[n]]["HF"][:, k % 2, a:T],
                                        XH[:, k, a:T].bitcast(F32), ALU.subtract
                                        ).then_inc(x_lo, 1)

        NSTD = {0: 0, 1: 2, 2: 4, 3: 6}
        U = at("U", RB, [P, KT, T + 6])

        def in_act(t, m, s):
            nc.scalar.activation(q_lat(m), acc(s, LATS), ACT.Identity,
                                 bias=vecd("b_in", m)).then_inc(acc_lat, 1)

        def in_dve(t, m, s):
            nc.vector.tensor_scalar(q_ctx(m), acc(s, CTX), vecd("b_in", m), None, ALU.add
                                    ).then_inc(acc_ctx, 1)

        def q_lat(m):
            return Q[:, bass.ds(m, 1), LC:T]

        def q_ctx(m):
            return Q[:, bass.ds(m, 1), 0:LC]

        def res_dve(layer, gate, segs):
            def evict(t, m, s):
                nc.vector.wait_ge(acc_lat, t)
                for sg in segs:
                    v = SEGS.index(sg)
                    zz = z[:, bass.ds(m, 1), sg[0]:sg[0] + sg[1]].rearrange("p a t -> p (a t)")
                    nc.vector.scalar_tensor_tensor(
                        out=zz, in0=acc(s, sg),
                        scalar=MOD[:, layer, bass.ds(m + 8 * gate, 1), v:v + 1].rearrange(
                            "p a b -> p (a b)"), in1=zz, op0=ALU.mult, op1=ALU.add
                        ).then_inc(acc_lat if sg is LATS else acc_ctx, 1)
            return evict

        HH = at("HH", RB, [P, KT, T], F32R)
        HL = at("HL", RB + 24, [P, KT, T], F32R)
        HR = at("HR", RB + 48, [P, 2, T])
        HS_ = at("HS_", RB + 54, [P, 2, T])

        def mlp(eng, which, layer, t0, segs, c0_, x_ready):
            a = 0 if CTX in segs else LC

            def up_act(hb):
                def evict(t, m, s):
                    n = m + hb
                    if not isinstance(n, int) or n >= 2:
                        nc.scalar.wait_ge(hid_sq, n - 1)
                    if CTX in segs:
                        nc.scalar.activation(HR[:, s, 0:LC], acc(s, CTX), ACT.Relu
                                             ).then_inc(acc_ctx, 1)
                    nc.scalar.activation(HR[:, s, LC:T], acc(s, LATS), ACT.Relu
                                         ).then_inc(acc_lat, 1)
                    nc.scalar.wait_ge(hid_sq, n + 1)
                    nc.scalar.activation(hh(HH, m), HS_[:, s, a:T], ACT.Copy
                                         ).then_inc(hid_hi, 1)
                return evict

            def up_dve(hb):
                def evict(t, m, s):
                    n = m + hb
                    nc.vector.wait_ge(acc_lat, t + 1)
                    if not isinstance(n, int) or n >= 2:
                        nc.vector.wait_ge(hid_hi, n - 1)
                        nc.vector.wait_ge(hid_lo, n - 1)
                    nc.vector.tensor_tensor(HS_[:, s, a:T], HR[:, s, a:T], HR[:, s, a:T],
                                            ALU.mult).then_inc(hid_sq, 1)
                    nc.vector.wait_ge(hid_hi, n + 1)
                    nc.vector.tensor_tensor(hh(HL, m), HS_[:, s, a:T], hh(HH, m).bitcast(F32),
                                            ALU.subtract).then_inc(hid_lo, 1)
                return evict

            def hh(x, m):
                return x[:, bass.ds(m, 1), a:T].rearrange("p a t -> p (a t)")

            for g in range(4):
                hb = 32 * layer + 8 * g
                tu, td = t0 + 16 * g, t0 + 16 * g + 8
                cu = c0_ + 16 * g
                if which == "pe":
                    gemm_pe(eng, tu, 8, segs, cu, XH, XL,
                            paced=x_ready if g == 0 else None)
                    gemm_pe(eng, td, 8, segs, cu + 8, HH, HL, x_wait=(hid_lo, hb + 7),
                            last_wait=(hid_lo, hb + 8))
                elif which == "act":
                    step_act(eng, tu, 8, up_act(hb), peel=2 if hb == 0 else 0)
                    if g == 3 and layer == 0:
                        step_act(eng, td, 8, last_act(2, NZ[2]), peel=8)
                    else:
                        step_act(eng, td, 8, None)
                else:
                    step_dve(eng, tu, 8, up_dve(hb), peel=2 if hb == 0 else 0)
                    if g == 3 and layer == 0:
                        step_dve(eng, td, 8, last_dve(2, res_dve(layer, 5, segs)), peel=8)
                    else:
                        step_dve(eng, td, 8, res_dve(layer, 5, segs))

        ml_gx, ml_gf, ml_sc, ml_g, ml_nat = (sem("ml_gx"), sem("ml_gf"), sem("ml_sc"),
                                             sem("ml_g"), sem("ml_nat"))
        ml_colp, ml_col = sem("ml_colp"), sem("ml_col")
        ml_kvt, ml_tr, ml_kvk = sem("ml_kvt"), sem("ml_tr"), sem("ml_kvk")
        ml_bc, ml_exp, ml_w, ml_vw = sem("ml_bc"), sem("ml_exp"), sem("ml_w"), sem("ml_vw")
        ml_num, ml_cn, ml_y, ml_ct, ml_nr = (sem("ml_num"), sem("ml_cn"), sem("ml_y"),
                                             sem("ml_ct"), sem("ml_nr"))
        ml_init = sem("ml_init")
        fin_o, fin_y, fin_hi = sem("fin_o"), sem("fin_y"), sem("fin_hi")
        fin_lo = sem("fin_lo")
        ORDER = [(0, 2, 1), (2, 6, 7)]

        def ml_gates_act(act):
            act.wait_ge(acc_lat, N_IN)
            act.wait_ge(acc_ctx, N_IN)
            act.wait_ge(ml_sc, 1)
            nc.scalar.activation(GX[:], Q[:, 16], ACT.Tanh, bias=CO[:, 67:68], scale=1.0 / CAP
                                 ).then_inc(ml_gx, 1)
            act.wait_ge(ml_gx, 1)
            act.wait_ge(cm0_in, 48)
            act.dma_start(GF[:], GX[64:128]).then_inc(ml_gf, 16)
            act.wait_ge(ml_gf, 16)
            nc.scalar.activation(GM[:], GF[:], ACT.Exp, scale=-CAP).then_inc(ml_gx, 1)
            act.wait_ge(ml_gx, 2)
            nc.scalar.activation(BC[:], GM[:], ACT.Ln, bias=CO[0:64, 66:67]).then_inc(ml_gx, 1)
            act.wait_ge(ml_colp, 12)
            pcol = ps[:, 6:8].rearrange("p a b -> p (a b)")
            nc.scalar.activation(CW[:], pcol[:, 384:768].rearrange("p (c r) -> p c r", c=6),
                                 ACT.Exp).then_inc(ml_col, 1)
            nc.scalar.activation(CS[:], pcol[:, 0:384].rearrange("p (c r) -> p c r", c=6),
                                 ACT.Copy).then_inc(ml_col, 1)

        def ml_gates_dve(dve):
            nc.vector.tensor_scalar(CO[:, 67:68], vec("fb"), 1.0 / CAP, None, ALU.mult
                                    ).then_inc(ml_sc, 1)
            dve.wait_ge(ml_gx, 3)
            nc.vector.tensor_scalar(IG[0:32], GX[0:32], CAP, None, ALU.mult).then_inc(ml_sc, 1)
            nc.vector.tensor_scalar(LF[0:32], BC[0:32], -1.0, None, ALU.mult).then_inc(ml_sc, 1)
            for sg in SEGS:
                a, b = sg[0], sg[0] + sg[1]
                nc.vector.tensor_scalar(IG[32:64, a:b], GX[32:64, a:b][:, ::-1], CAP, None,
                                        ALU.mult).then_inc(ml_sc, 1)
                nc.vector.tensor_scalar(LF[32:64, a:b], BC[32:64, a:b][:, ::-1], -1.0, None,
                                        ALU.mult).then_inc(ml_sc, 1)
            dve.wait_ge(ml_sc, 7)
            dve.wait_ge(cm0_in, 48)
            nc.vector.tensor_tensor_scan(BC[:], c0("reset", 0, T)[0:64], LF[:], 0.0, ALU.mult,
                                         ALU.add).then_inc(ml_g, 1)
            nc.vector.memset(MM[:, 0:1], 0.0).then_inc(ml_g, 1)
            dve.wait_ge(ml_g, 2)
            nc.vector.tensor_tensor(R5[:, 3], IG[:], BC[:], ALU.subtract).then_inc(ml_g, 1)
            dve.wait_ge(ml_g, 3)
            for c in range(6):
                a, b = 128 * c, 128 * c + 128
                nc.vector.tensor_tensor_scan(GM[:, a:b], R5[:, 3, a:b], R5[:, 3, a:b],
                                             MM[:, c:c + 1], ALU.max, ALU.max).then_inc(ml_g, 1)
                dve.wait_ge(ml_g, 4 + 2 * c)
                nc.vector.tensor_tensor(MM[:, c + 1:c + 2], BC[:, b - 1:b], GM[:, b - 1:b],
                                        ALU.add).then_inc(ml_g, 1)
                dve.wait_ge(ml_g, 5 + 2 * c)
            nc.vector.tensor_scalar(R5[:, 0], GM[:], -1.0, None, ALU.mult).then_inc(ml_g, 1)
            nc.vector.scalar_tensor_tensor(out=R5[:, 2], in0=BC[:], scalar=-1.0, in1=GM[:],
                                           op0=ALU.mult, op1=ALU.subtract).then_inc(ml_g, 1)
            for c in range(6):
                a, b = 128 * c, 128 * c + 128
                nc.vector.tensor_scalar(R5[:, 1, a:b], GM[:, a:b], -1.0, MM[:, c:c + 1],
                                        ALU.mult, ALU.add).then_inc(ml_g, 1)
                nc.vector.tensor_scalar(R5[:, 4, a:b], R5[:, 3, a:b], GM[:, b - 1:b], None,
                                        ALU.subtract).then_inc(ml_g, 1)
            dve.wait_ge(ml_g, 29)
            nc.vector.tensor_copy(N5[0:32], R5[0:32]).then_inc(ml_nat, 1)
            for sg in SEGS:
                a, b = sg[0], sg[0] + sg[1]
                nc.vector.tensor_copy(N5[32:64, :, a:b], R5[32:64, :, a:b][:, :, ::-1]
                                      ).then_inc(ml_nat, 1)
            nc.vector.tensor_scalar(Q[:, 0:4], Q[:, 0:4], float(P) ** -0.5, None, ALU.mult
                                    ).then_inc(ml_init, 1)
            nc.vector.memset(H[:], 0.0).then_inc(ml_init, 1)
            dve.wait_ge(ml_nat, 3)
            nc.vector.memset(CT[:], 0.0).then_inc(ml_init, 1)

        def ml_gates_pe(pe):
            pe.wait_ge(ml_nat, 3)
            pcol = ps[:, 6:8].rearrange("p a b -> p (a b)")
            for r in range(2):
                for c in range(6):
                    o = 384 * r + 64 * c
                    nc.tensor.transpose(pcol[:, o:o + 64], N5[:, 3 + r, 128 * c:128 * c + 128],
                                        ident[0:64, 0:64]).then_inc(ml_colp, 1)

        def chunks(eng, body):
            for lo, hi, flip in ORDER:
                with eng.Fori(0, hi - lo) as i:
                    for d in range(2):
                        c = eng.snap(i + lo if d == 0 else i * -1 + (flip - lo))
                        body(i * 2 + (2 * lo + d), d, c, eng.snap(c * P))

        def ml_pe(pe):
            pe.wait_ge(ml_col, 2)
            pe.wait_ge(ml_init, 4)

            def body(u, d, c, off):
                tok = bass.ds(off, P)
                pe.wait_ge(ml_kvt, u + 1)
                pe.wait_ge(ml_ct, u * 4)
                for j in range(8):
                    mm = nc.tensor.transpose(ps[:, j // 4, P * (j % 4):P * (j % 4) + P],
                                             KVT[:, j], ident)
                mm.then_inc(ml_tr, 1)
                pe.wait_ge(ml_w, u)
                pe.wait_ge(ml_exp, u * 6)
                for h in range(4):
                    nc.tensor.matmul(ps[:, 5, P * h:P * h + P], KVT[:, h], Q[:, h, tok],
                                     start=True, stop=True)
                for r, bank in ((0, 2), (1, 3), (2, 4)):
                    for h in range(4):
                        o = ps[:, bank, P * h:P * h + P]
                        mm = nc.tensor.matmul(
                            o, c0("sel", P * (4 * d + h), P)[0:64], N5[:, r, tok], start=True,
                            stop=(r != 0))
                        if r == 0:
                            nc.tensor.matmul(o, ident, c0("neg", P * d, P), start=False,
                                             stop=True)
                mm.then_inc(ml_bc, 1)
                pe.wait_ge(ml_kvk, u + 1)
                pe.wait_ge(ml_vw, u + 1)
                pe.wait_ge(ml_y, u)
                for h in range(4):
                    o = ps[:, 6, P * h:P * h + P]
                    nc.tensor.matmul(o, KVK[:, 4 + h], WM[:, h], start=True, stop=False)
                    nc.tensor.matmul(o, CT[:, d, h, 0:P], QT[:, h], start=False, stop=True)
                nc.tensor.matmul(ps[:, 7, :], ones, WM[:].rearrange("p h t -> p (h t)"),
                                 start=True, stop=False)
                pe.wait_ge(ml_nr, u + 1)
                for h in range(4):
                    mm = nc.tensor.matmul(ps[:, 7, P * h:P * h + P], NR[:, h], QT[:, h],
                                          start=False, stop=(h == 3))
                mm.then_inc(ml_num, 1)
                for h in range(4):
                    mm = nc.tensor.matmul(ps[:, h // 2, (P + 1) * (h % 2):(P + 1) * (h % 2) + P + 1],
                                          KVK[:, h], VW[:, h], start=True, stop=True)
                mm.then_inc(ml_cn, 1)
            chunks(pe, body)

        def ml_act(act):
            act.wait_ge(ml_init, 4)

            def body(u, d, c, off):
                act.wait_ge(ml_num, u)
                nc.scalar.activation(KVT[:], Q[:, 4:12, bass.ds(off, P)], ACT.Copy
                                     ).then_inc(ml_kvt, 1)
                act.wait_ge(ml_tr, u + 1)
                act.wait_ge(ml_cn, u)
                nc.scalar.activation(KVK[:].rearrange("p j t -> p (j t)"),
                                     ps[:, 0:2].rearrange("p a b -> p (a b)"), ACT.Copy
                                     ).then_inc(ml_kvk, 1)
                act.wait_ge(ml_ct, u * 4)
                nc.scalar.activation(NR[:], CT[:, d, :, P:P + 1].broadcast_to([P, 4, P]),
                                     ACT.Copy).then_inc(ml_nr, 1)
                act.wait_ge(ml_bc, u + 1)
                act.wait_ge(ml_w, u)
                for h in range(4):
                    nc.scalar.activation(
                        EE[:, h], ps[:, 2, P * h:P * h + P], ACT.Exp,
                        bias=CS[:, bass.ds(c, 1), 32 * d + h:32 * d + h + 1].rearrange(
                            "p a b -> p (a b)")).then_inc(ml_exp, 1)
                nc.scalar.activation(IW[:].rearrange("p h t -> p (h t)"), ps[:, 3], ACT.Exp
                                     ).then_inc(ml_exp, 1)
                act.wait_ge(ml_y, u)
                nc.scalar.activation(FL[:].rearrange("p h t -> p (h t)"), ps[:, 4], ACT.Exp
                                     ).then_inc(ml_exp, 1)
            chunks(act, body)

        def ml_dve(dve):
            dve.wait_ge(ml_init, 3)
            nc.vector.memset(VW[:], 0.0).then_inc(ml_init, 1)
            dve.wait_ge(ml_col, 2)

            def body(u, d, c, off):
                tok = bass.ds(off, P)
                dve.wait_ge(ml_exp, u * 6 + 4)
                dve.wait_ge(ml_num, u)
                dve.wait_ge(ml_cn, u)
                nc.vector.tensor_tensor(WM[:].rearrange("p h t -> p (h t)"),
                                        EE[:].rearrange("p h t -> p (h t)"), ps[:, 5],
                                        ALU.mult).then_inc(ml_w, 1)
                dve.wait_ge(ml_kvk, u + 1)
                ws = CW[:, bass.ds(c, 1), 32 * d:32 * d + 4].rearrange("p a (h b) -> p (a h) b",
                                                                      b=1)
                nc.vector.tensor_tensor(VW[:, :, 0:P], KVK[:, 4:8], ws.broadcast_to([P, 4, P]),
                                        ALU.mult)
                nc.vector.tensor_copy(VW[:, :, P:P + 1], ws)
                dve.wait_ge(ml_exp, u * 6 + 6)
                nc.vector.tensor_tensor(QT[:], Q[:, 0:4, tok], IW[:], ALU.mult
                                        ).then_inc(ml_vw, 1)
                dve.wait_ge(ml_cn, u + 1)
                dve.wait_ge(ml_nr, u + 1)
                last = P - 1 if d == 0 else 0
                for h in range(4):
                    o = (P + 1) * (h % 2)
                    nc.vector.scalar_tensor_tensor(
                        out=CT[:, d, h], in0=CT[:, d, h], scalar=IW[:, h, last:last + 1],
                        in1=ps[:, h // 2, o:o + P + 1], op0=ALU.mult, op1=ALU.add
                        ).then_inc(ml_ct, 1)
                fl = FL[:].rearrange("p h t -> p (h t)")
                nc.vector.tensor_tensor(fl, fl, ps[:, 7], ALU.max).then_inc(ml_g, 1)
                dve.wait_ge(ml_g, u * 4 + 30)
                nc.vector.scalar_tensor_tensor(out=fl, in0=ps[:, 7], scalar=-1.0, in1=fl,
                                               op0=ALU.mult, op1=ALU.max).then_inc(ml_g, 1)
                dve.wait_ge(ml_g, u * 4 + 31)
                nc.vector.reciprocal(YM[:], FL[:]).then_inc(ml_g, 1)
                dve.wait_ge(ml_g, u * 4 + 32)
                nc.vector.tensor_tensor(YM[:].rearrange("p h t -> p (h t)"), ps[:, 6],
                                        YM[:].rearrange("p h t -> p (h t)"), ALU.mult
                                        ).then_inc(ml_g, 1)
                dve.wait_ge(ml_g, u * 4 + 33)
                nc.vector.tensor_tensor(H[:, :, tok], H[:, :, tok], YM[:], ALU.add
                                        ).then_inc(ml_y, 1)
            chunks(dve, body)

        HSQ = at("HSQ", RB, [P, 2, T])
        HSD = at("HSD", RB + 6, [16, T])
        HRS = at("HRS", RB + 9, [16, T])
        FY = at("FY", RB + 12, [P, 2, T])
        ROT = at("ROT", RB + 18, [P, 2, LAT])
        NSEL = at("NSEL", 53, [P, 9 * 16])
        NBC = at("NBC", 53.75, [16, 9 * P])
        hn_sqa, hn_sqv, hn_st, hn_sd, hn_b, hn_n = (sem("hn_sqa"), sem("hn_sqv"), sem("hn_st"),
                                                    sem("hn_sd"), sem("hn_b"), sem("hn_n"))

        def hn_tile(j):
            return Q[:, QS0 + j] if j < 5 else H[:, j - 5]

        def hn_pe(pe):
            for j in range(9):
                pe.wait_ge(hn_sqv if j % 2 else hn_sqa, j // 2 + 1)
                for b, lo, n in ((0, 0, 512), (1, 512, LC)):
                    mm = nc.tensor.matmul(ps[0:16, b, 0:n], NSEL[:, 16 * j:16 * j + 16],
                                          HSQ[:, j % 2, lo:lo + n], start=j == 0, stop=j == 8)
                mm.then_inc(hn_st, 1)
            pe.wait_ge(hn_sd, 2)

            def partner(i):
                pe.wait_ge(hn_n, i + 1)
                if i >= 2:
                    pe.wait_ge(at_rot, i - 1)
                nc.tensor.matmul(ps[:, 6 + i % 2], c0("perm", 0, P), Q[:, QS0 + i, LC:T],
                                 start=True, stop=True).then_inc(at_perm, 1)
            for j in range(9):
                if j >= 2:
                    pe.wait_ge(hn_n, j - 1)
                for b, lo, n in ((0, 0, 512), (1, 512, LC)):
                    mm = nc.tensor.matmul(ps[:, 2 + 2 * (j % 2) + b, 0:n],
                                          NBC[:, P * j:P * j + P], HRS[:, lo:lo + n],
                                          start=True, stop=True)
                mm.then_inc(hn_b, 1)
                if 1 <= j <= 5:
                    partner(j - 1)

        def hn_act(act):
            act.wait_ge(ml_y, 12)
            for j in range(0, 9, 2):
                if j:
                    act.wait_ge(hn_st, j - 1)
                nc.scalar.activation(HSQ[:, 0], hn_tile(j), ACT.Square).then_inc(hn_sqa, 1)
            act.wait_ge(hn_st, 9)
            nc.scalar.activation(HSD[:], ps[0:16, 0:2].rearrange("p a b -> p (a b)")[:, 0:T],
                                 ACT.Sqrt, bias=CO[0:16, 64:65]).then_inc(hn_sd, 1)
            for h in range(4):
                nc.scalar.activation(Q[:, 12 + h], Q[:, 12 + h], ACT.Tanh, scale=0.5
                                     ).then_inc(fin_o, 1)
            for h in range(4):
                act.wait_ge(fin_y, h + 1)
                nc.scalar.activation(XH[:, h], FY[:, h % 2], ACT.Copy).then_inc(fin_hi, 1)

        def hn_pool(pool):
            def cos_part(i):
                pool.wait_ge(at_perm, i + 1)
                x = Q[:, QS0 + i, LC:T]
                nc.gpsimd.tensor_tensor(x, x, c0("cos", 0, LAT), ALU.mult).then_inc(hn_pl, 1)

            for i in range(5):
                cos_part(i)
                if i < 4:
                    pool.wait_ge(fin_o, i + 1)
                    nc.gpsimd.tensor_scalar(Q[:, 12 + i], Q[:, 12 + i], 0.5, 0.5, ALU.mult,
                                            ALU.add).then_inc(hn_pl, 1)

        def hn_dve(dve):
            dve.wait_ge(ml_y, 12)
            for j in range(1, 9, 2):
                if j > 1:
                    dve.wait_ge(hn_st, j - 1)
                nc.vector.tensor_tensor(HSQ[:, 1], hn_tile(j), hn_tile(j), ALU.mult
                                        ).then_inc(hn_sqv, 1)
            dve.wait_ge(hn_sd, 1)
            nc.vector.reciprocal(HRS[:], HSD[:]).then_inc(hn_sd, 1)

            def spread(j):
                return ps[:, 2 + 2 * (j % 2):4 + 2 * (j % 2)].rearrange("p a b -> p (a b)")[:, 0:T]

            def rope(i):
                x = Q[:, QS0 + i, LC:T]
                dve.wait_ge(at_perm, i + 1)
                if i >= 2:
                    dve.wait_ge(at_x, i - 1)
                nc.vector.tensor_tensor(ROT[:, i % 2], ps[:, 6 + i % 2], c0("sin", 0, LAT),
                                        ALU.mult).then_inc(at_rot, 1)
                dve.wait_ge(at_rot, i + 1)
                dve.wait_ge(hn_pl, 2 * i + 1)
                nc.vector.tensor_tensor(x, x, ROT[:, i % 2], ALU.add).then_inc(at_x, 1)

            def gate(h):
                dve.wait_ge(hn_n, 6 + h)
                dve.wait_ge(hn_pl, 2 * h + 2)
                nc.vector.tensor_tensor(FY[:, h % 2], FY[:, h % 2], Q[:, 12 + h], ALU.mult
                                        ).then_inc(fin_y, 1)

            def low(h):
                dve.wait_ge(fin_hi, h + 1)
                nc.vector.tensor_tensor(XL[:, h], FY[:, h % 2], XH[:, h].bitcast(F32),
                                        ALU.subtract).then_inc(fin_lo, 1)
            for j in range(9):
                h = j - 5
                dve.wait_ge(hn_b, j + 1)
                if j < 5:
                    nc.vector.scalar_tensor_tensor(
                        out=hn_tile(j), in0=hn_tile(j), scalar=vec("q_g" if j < 4 else "k_g"),
                        in1=spread(j), op0=ALU.mult, op1=ALU.mult).then_inc(hn_n, 1)
                else:
                    if h >= 2:
                        dve.wait_ge(fin_lo, h - 1)
                    nc.vector.scalar_tensor_tensor(
                        out=FY[:, h % 2], in0=H[:, h], scalar=vec("out_g", h), in1=spread(j),
                        op0=ALU.mult, op1=ALU.mult).then_inc(hn_n, 1)
                if 1 <= j <= 5:
                    rope(j - 1)
                if h >= 0:
                    gate(h)
                if h >= 1:
                    low(h - 1)
            low(3)

        KD = at("KD", RB, [P, 2, T])
        VA = at("VA", RB + 6, [P, 6, P])
        QZ = at("QZ", RB + 18, [P, 8, P])
        PP = at("PP", RB + 22, [P, 2, 640])
        PT = at("PT", RB + 27, [P, 2, 640])
        ON = at("ON", RB + 32, [P, 8, 64])
        SM = at("SM", RB + 34, [P, 6, 8])
        at_rot, hn_pl = sem("at_rot"), sem("hn_pl")
        at_perm, at_x, at_kd, at_va = sem("at_perm"), sem("at_x"), sem("at_kd"), sem("at_va")
        at_vt, at_z = sem("at_vt"), sem("at_z")
        at_qz, at_s, at_nb, at_p = sem("at_qz"), sem("at_s"), sem("at_nb"), sem("at_p")
        at_t, at_pt, at_o, at_es, at_r = (sem("at_t"), sem("at_pt"), sem("at_o"), sem("at_es"),
                                          sem("at_r"))
        at_on, at_ot, at_hi, at_lo = sem("at_on"), sem("at_ot"), sem("at_hi"), sem("at_lo")
        QS0, KS0, VS0 = 17, 21, 22
        SCALE = 64 ** -0.5
        KINDS = {"ctx": (0, 0, ()), "first": (2, 0, ((384, 1),)),
                 "mid": (3, -1, ((128, 0), (384, 1))), "last": (2, -1, ((256, 0),))}

        def blocks(eng, body):
            with eng.Fori(0, 2) as i:
                body(i, eng.snap(i * P), i, "ctx")
            body(2, LC, 2, "first")
            with eng.Fori(3, 5) as i:
                body(i, eng.snap(i * P), i, "mid")
            body(5, 5 * P, 5, "last")

        def attn_pe(pe):
            pv = ps[:, 0:2].rearrange("p a b -> p (a b)")
            for c in range(6):
                mm = nc.tensor.transpose(pv[:, P * c:P * c + P], Q[:, VS0, P * c:P * c + P], ident)
            mm.then_inc(at_vt, 1)
            pe.wait_ge(hn_n, 9)
            pe.wait_ge(at_rot, 5)
            pe.wait_ge(at_kd, 64)
            pe.wait_ge(at_va, 1)

            def body(b, tok, blk, kind):
                nb, rel, masks = KINDS[kind]
                ntr = nb + 2

                def scores(h):
                    s = h % 2
                    pe.wait_ge(at_qz, b * 2 + 2)
                    if h >= 2:
                        pe.wait_ge(at_p, b * 8 + (h - 1))
                    else:
                        pe.wait_ge(at_r, b * 3)
                    if nb:
                        o = ps[:, 2 * s, 512 - P * nb:512]
                        nc.tensor.matmul(o, QZ[:, h],
                                         KD[:, h // 4, bass.ds(tok + P * rel, P * nb)],
                                         start=True, stop=not masks)
                        for i, (col, m) in enumerate(masks):
                            nc.tensor.matmul(ps[:, 2 * s, col:col + P], ident,
                                             c0("neg", P * m, P), start=False,
                                             stop=i == len(masks) - 1)
                    nc.tensor.matmul(ps[:, 2 * s + 1, 0:LC], QZ[:, h], KD[:, h // 4, 0:LC],
                                     start=True, stop=True).then_inc(at_s, 1)

                def turn(h):
                    pe.wait_ge(at_p, b * 8 + (h + 1))
                    pe.wait_ge(at_pt, b * 8 + h)
                    pt = ps[:, 4:6].rearrange("p a b -> p (a b)")
                    for k in range(ntr):
                        mm = nc.tensor.transpose(pt[:, P * k:P * k + P],
                                                 PP[:, h % 2, P * k:P * k + P], ident)
                    mm.then_inc(at_t, 1)

                def values(h):
                    pe.wait_ge(at_pt, b * 8 + (h + 1))
                    if h == 0:
                        pe.wait_ge(at_on, b)
                    for k in range(ntr):
                        if k < nb:
                            v = VA[:, bass.ds(blk + (rel + k), 1), 64 * (h // 4):64 * (h // 4) + 64]
                            v = v.rearrange("p a c -> p (a c)")
                        else:
                            v = VA[:, k - nb, 64 * (h // 4):64 * (h // 4) + 64]
                        mm = nc.tensor.matmul(ps[:, 6, 64 * h:64 * h + 64],
                                              PT[:, h % 2, P * k:P * k + P], v, start=k == 0,
                                              stop=k == ntr - 1)
                    mm.then_inc(at_o, 1)
                for h in range(10):
                    if h < 8:
                        scores(h)
                    if 1 <= h <= 8:
                        turn(h - 1)
                    if h >= 2:
                        values(h - 2)
                pe.wait_ge(at_on, b + 1)
                pe.wait_ge(at_lo, b)
                for j in range(4):
                    mm = nc.tensor.transpose(ps[:, 7, P * j:P * j + P],
                                             ON[:, 2 * j:2 * j + 2].rearrange("p a c -> p (a c)"),
                                             ident)
                mm.then_inc(at_ot, 1)
            blocks(pe, body)

        def attn_act(act):
            act.wait_ge(at_vt, 1)
            nc.scalar.activation(VA[:].rearrange("p c t -> p (c t)"),
                                 ps[:, 0:2].rearrange("p a b -> p (a b)")[:, 0:T], ACT.Copy
                                 ).then_inc(at_va, 1)
            act.wait_ge(at_x, 5)
            act.wait_ge(at_z, 2)

            def body(b, tok, blk, kind):
                nb, rel, masks = KINDS[kind]
                n = P * (nb + 2)
                act.wait_ge(at_s, b * 8)
                for e in range(2):
                    nc.scalar.activation(
                        QZ[64 * e:64 * e + 64].rearrange("p (j e) t -> p j e t", e=2)[:, :, e],
                        Q[64 * e:64 * e + 64, QS0:QS0 + 4, bass.ds(tok, P)], ACT.Copy
                        ).then_inc(at_qz, 1)
                for h in range(9):
                    if h < 8:
                        s = h % 2
                        act.wait_ge(at_nb, b * 16 + (2 * h + 2))
                        if h >= 2:
                            act.wait_ge(at_t, b * 8 + (h - 1))
                        else:
                            act.wait_ge(at_t, b * 8)
                        src = ps[:, 2 * s:2 * s + 2].rearrange("p a b -> p (a b)")[
                            :, 512 - P * nb:512 + LC]
                        nc.scalar.activation(PP[:, s, 0:n], src, ACT.Exp,
                                             bias=SM[:, 1, h:h + 1], scale=SCALE,
                                             accum_out=SM[:, 2, h:h + 1]).then_inc(at_p, 1)
                    if h >= 1:
                        g = h - 1
                        act.wait_ge(at_t, b * 8 + (g + 1))
                        act.wait_ge(at_o, b * 8 + max(g - 1, 0))
                        nc.scalar.activation(PT[:, g % 2, 0:n],
                                             ps[:, 4:6].rearrange("p a b -> p (a b)")[:, 0:n],
                                             ACT.Copy).then_inc(at_pt, 1)
                act.wait_ge(at_r, b * 3 + 1)
                nc.scalar.activation(SM[:, 4], SM[:, 3], ACT.Exp).then_inc(at_es, 1)
                act.wait_ge(at_ot, b + 1)
                nc.scalar.activation(XH[:, 4:8, bass.ds(tok, P)],
                                     ps[:, 7].rearrange("p (j t) -> p j t", j=4), ACT.Copy
                                     ).then_inc(at_hi, 1)
            blocks(act, body)

        def attn_dve(dve):
            dve.wait_ge(at_x, 5)
            dve.wait_ge(fin_lo, 4)
            nc.vector.memset(QZ[:], 0.0).then_inc(at_z, 1)
            nc.vector.tensor_scalar(SM[:, 5], vec("sink", 0, 8), -1.0, None, ALU.mult
                                    ).then_inc(at_z, 1)
            dve.wait_ge(at_z, 2)

            def body(b, tok, blk, kind):
                nb, rel, masks = KINDS[kind]
                for h in range(8):
                    s = h % 2
                    dve.wait_ge(at_s, b * 8 + (h + 1))
                    src = ps[:, 2 * s:2 * s + 2].rearrange("p a b -> p (a b)")[
                        :, 512 - P * nb:512 + LC]
                    nc.vector.tensor_reduce(SM[:, 0, h:h + 1], src, AX.X, ALU.max
                                            ).then_inc(at_nb, 1)
                    dve.wait_ge(at_nb, b * 16 + (2 * h + 1))
                    nc.vector.tensor_scalar(SM[:, 1, h:h + 1], SM[:, 0, h:h + 1], -SCALE,
                                            SM[:, 5, h:h + 1], ALU.mult, ALU.min
                                            ).then_inc(at_nb, 1)
                dve.wait_ge(at_nb, b * 16 + 16)
                dve.wait_ge(at_es, b)
                nc.vector.tensor_tensor(SM[:, 3], SM[:, 1], vec("sink", 0, 8), ALU.add
                                        ).then_inc(at_r, 1)
                dve.wait_ge(at_es, b + 1)
                dve.wait_ge(at_p, b * 8 + 8)
                nc.vector.tensor_tensor(SM[:, 4], SM[:, 4], SM[:, 2], ALU.add).then_inc(at_r, 1)
                dve.wait_ge(at_r, b * 3 + 2)
                nc.vector.reciprocal(SM[:, 0], SM[:, 4]).then_inc(at_r, 1)
                dve.wait_ge(at_r, b * 3 + 3)
                dve.wait_ge(at_o, b * 8 + 8)
                dve.wait_ge(at_ot, b)
                nc.vector.tensor_tensor(ON[:], ps[:, 6].rearrange("p (h c) -> p h c", h=8),
                                        SM[:, 0][:, :, None].broadcast_to([P, 8, 64]), ALU.mult
                                        ).then_inc(at_on, 1)
                dve.wait_ge(at_ot, b + 1)
                dve.wait_ge(at_hi, b + 1)
                xs = bass.ds(tok, P)
                nc.vector.tensor_tensor(XL[:, 4:8, xs],
                                        ps[:, 7].rearrange("p (j t) -> p j t", j=4),
                                        XH[:, 4:8, xs].bitcast(F32), ALU.subtract
                                        ).then_inc(at_lo, 1)
            blocks(dve, body)

        def attn_pool(pool):
            pool.wait_ge(at_x, 5)
            for g in range(2):
                for e in range(2):
                    pool.dma_start(KD[64 * e:64 * e + 64, g], Q[64 * g:64 * g + 64, KS0]
                                   ).then_inc(at_kd, 16)

        RR = at("RR", RB + 24.5, [P, KT, LAT])
        KK_ = at("KK_", RB + 40.5, [P, KT, T])
        VKB = at("VKB", RB + 64.5, [P, 2, 6, P])
        H1 = at("H1", RB + 76.5, [P, 2, T])
        G1 = at("G1", RB + 82.5, [P, 2, LAT])
        MX = at("MX", RB + 86.5, [P, 2, T])
        MC = at("MC", RB + 92.5, [P, 6, 8])
        mc_ready, mx_a, mx_b, mx_c = sem("mc_ready"), sem("mx_a"), sem("mx_b"), sem("mx_c")
        vk_t, vk_c, vt_out = sem("vk_t"), sem("vk_c"), sem("vt_out")
        vk_out = [sem("vk_out0"), sem("vk_out1")]
        cm1_in, z_out = sem("cm1_in"), sem("z_out")
        MIXES = [(3, T_V, 8, SEGS), (2, T_K, 8, SEGS), (1, T_W, 1, SEGS), (4, T_A, 1, SEGS),
                 (0, T_R, 8, (LATS,)), (5, T_G, 2, (LATS,))]

        def ushift(k, sg, by):
            a = 2 + 2 * SEGS.index(sg) + sg[0] + by
            return U[:, k, a:a + sg[1]]

        def mix_act(act, q):
            i, t0, n, segs = MIXES[q]
            a = segs[0][0]

            def scale(k):
                if k >= 2:
                    act.wait_ge(x_lo, 16 + 8 * q + k - 1)
                for sg in segs:
                    ins = nc.scalar.activation(MX[:, k % 2, sg[0]:sg[0] + sg[1]], ushift(k, sg, 0),
                                               ACT.Copy, scale=MC[:, i, k:k + 1])
                ins.then_inc(mx_a, 1)
            if q == 0:
                act.wait_ge(mc_ready, 2)
                act.wait_ge(n_h, 24)
            act.wait_ge(x_lo, 16 + 8 * q)
            for k in range(KT):
                if k == 0:
                    scale(0)
                if k + 1 < KT:
                    scale(k + 1)
                act.wait_ge(mx_c, 8 * q + k + 1)
                nc.scalar.activation(XH[:, k, a:T], MX[:, k % 2, a:T], ACT.Copy).then_inc(x_hi, 1)

        def mix_dve(dve, q):
            i, t0, n, segs = MIXES[q]
            a = segs[0][0]
            for k in range(KT):
                dve.wait_ge(mx_a, 8 * q + k + 1)
                for by, sm in ((-1, mx_b), (1, mx_c)):
                    for sg in segs:
                        m = MX[:, k % 2, sg[0]:sg[0] + sg[1]]
                        ins = nc.vector.scalar_tensor_tensor(
                            out=m, in0=ushift(k, sg, by),
                            scalar=vec("mu", 16 * i + (0 if by < 0 else 8) + k), in1=m,
                            op0=ALU.mult, op1=ALU.add)
                    ins.then_inc(sm, 1)
                    dve.wait_ge(sm, 8 * q + k + 1)

        def mix_pool(pool, q):
            a = MIXES[q][3][0][0]
            for k in range(KT):
                pool.wait_ge(x_hi, 16 + 8 * q + k + 1)
                nc.gpsimd.tensor_tensor(XL[:, k, a:T], MX[:, k % 2, a:T],
                                        XH[:, k, a:T].bitcast(F32), ALU.subtract
                                        ).then_inc(x_lo, 1)

        def at_tile(x, m, lo, hi):
            return x[:, bass.ds(m, 1), lo:hi].rearrange("p a t -> p (a t)")

        def mix_evict(q, eng):
            def act_side(t, m, s):
                if q <= 1:
                    nc.scalar.activation(at_tile(KK_, m, LC, T), acc(s, LATS), ACT.Copy
                                         ).then_inc(acc_lat, 1)
                elif q <= 3:
                    f = ACT.Tanh if q == 2 else ACT.Copy
                    nc.scalar.activation(H1[:, q - 2, 0:LC], acc(s, CTX), f).then_inc(acc_ctx, 1)
                    nc.scalar.activation(H1[:, q - 2, LC:T], acc(s, LATS), f).then_inc(acc_lat, 1)
                elif q == 4:
                    nc.scalar.activation(at_tile(RR, m, 0, LAT), acc(s, LATS), ACT.Copy
                                         ).then_inc(acc_lat, 1)
                else:
                    nc.scalar.activation(G1[:, m], acc(s, LATS), ACT.Tanh, scale=0.5
                                         ).then_inc(acc_lat, 1)

            def dve_side(t, m, s):
                if q <= 1:
                    nc.vector.tensor_copy(at_tile(KK_, m, 0, LC), acc(s, CTX)).then_inc(acc_ctx, 1)
            return act_side if eng == "act" else dve_side

        def vk_pe(pe):
            pe.wait_ge(acc_lat, T_V + 8)
            pe.wait_ge(acc_ctx, T_V + 8)
            for m in range(8):
                if m >= 2:
                    pe.wait_ge(vk_c, m - 1)
                b = 4 + 2 * (m % 2)
                o = ps[:, b:b + 2].rearrange("p a b -> p (a b)")
                for c in range(6):
                    mm = nc.tensor.transpose(o[:, P * c:P * c + P], KK_[:, m, P * c:P * c + P],
                                             ident)
                mm.then_inc(vk_t, 1)

        def vk_act(act):
            for m in range(8):
                act.wait_ge(vk_t, m + 1)
                if m >= 2:
                    act.wait_ge(vk_out[m % 2], 16 * (m // 2))
                b = 4 + 2 * (m % 2)
                nc.scalar.activation(VKB[:, m % 2].rearrange("p c t -> p (c t)"),
                                     ps[:, b:b + 2].rearrange("p a b -> p (a b)")[:, 0:T],
                                     ACT.Copy).then_inc(vk_c, 1)

        def vk_pool(pool):
            pool.dma_start(CM1[:], cm1[:, 0:NC1 - D]).then_inc(cm1_in, 16)
            pool.wait_ge(n_h, 24)
            pool.dma_start(z_dram, z[:, :, LC:T]).then_inc(z_out, 16)
            pool.wait_ge(acc_lat, T_V + 8)
            pool.dma_start(vt_dram, KK_[:, :, LC:T]).then_inc(vt_out, 16)
            for m in range(8):
                pool.wait_ge(vk_c, m + 1)
                pool.dma_start(vk_dram[:, P * m:P * m + P].rearrange("(c p) n -> p c n", p=P),
                               VKB[:, m % 2]).then_inc(vk_out[m % 2], 16)

        KN = at("KN", RB, [P, KT, T])
        KSQ = at("KSQ", RB + 64.5, [P, 2, T])
        KSD = at("KSD", RB + 70.5, [16, T])
        KRS = at("KRS", RB + 73.5, [16, T])
        HK = at("HK", RB + 86.5, [16, D])
        kk_sq, kk_st, kk_sd, kk_b, kk_n = (sem("kk_sq"), sem("kk_st"), sem("kk_sd"),
                                                  sem("kk_b"), sem("kk_n"))

        def kk_pe(pe):
            pe.wait_ge(cm1_in, 16)
            for m in range(8):
                pe.wait_ge(kk_sq, m + 1)
                for b, sg in ((4, LATS), (5, CTX)):
                    mm = nc.tensor.matmul(ps[0:16, b, 0:sg[1]], c1("hsel", 16 * m, 16),
                                          KSQ[:, m % 2, sg[0]:sg[0] + sg[1]], start=m == 0,
                                          stop=m == 7)
                mm.then_inc(kk_st, 1)
            pe.wait_ge(cm1_in, 32)
            pe.wait_ge(kk_sd, 4)
            for m in range(8):
                if m >= 2:
                    pe.wait_ge(kk_n, m - 1)
                for b, sg in ((0, LATS), (1, CTX)):
                    mm = nc.tensor.matmul(ps[:, 4 + 2 * (m % 2) + b, 0:sg[1]],
                                          HK[:, P * m:P * m + P], KRS[:, sg[0]:sg[0] + sg[1]],
                                          start=True, stop=True)
                mm.then_inc(kk_b, 1)

        def kk_act(act):
            for b in range(2):
                act.wait_ge(vk_out[b], 64)
            act.wait_ge(acc_ctx, T_K + 8)
            for m in range(8):
                if m >= 2:
                    act.wait_ge(kk_st, m - 1)
                nc.scalar.activation(KSQ[:, m % 2], KK_[:, m], ACT.Square, scale=vec("k_k", m)
                                     ).then_inc(kk_sq, 1)
            act.wait_ge(kk_sd, 2)
            nc.scalar.activation(KSD[:], KSD[:], ACT.Sqrt).then_inc(kk_sd, 1)

        def kk_dve(dve):
            dve.wait_ge(acc_lat, T_G + 2)
            nc.vector.tensor_scalar(G1[:], G1[:], 0.5, 0.5, ALU.mult, ALU.add)
            dve.wait_ge(kk_st, 8)
            nc.vector.tensor_scalar(KSD[:, LC:T], ps[0:16, 4], 1e-24, None, ALU.max
                                    ).then_inc(kk_sd, 1)
            nc.vector.tensor_scalar(KSD[:, 0:LC], ps[0:16, 5, 0:LC], 1e-24, None, ALU.max
                                    ).then_inc(kk_sd, 1)
            dve.wait_ge(kk_sd, 3)
            nc.vector.reciprocal(KRS[:], KSD[:]).then_inc(kk_sd, 1)
            for m in range(8):
                dve.wait_ge(kk_b, m + 1)
                for b, sg in ((0, LATS), (1, CTX)):
                    ins = nc.vector.scalar_tensor_tensor(
                        out=KN[:, m, sg[0]:sg[0] + sg[1]], in0=KK_[:, m, sg[0]:sg[0] + sg[1]],
                        scalar=vec("k_k", m), in1=ps[:, 4 + 2 * (m % 2) + b, 0:sg[1]],
                        op0=ALU.mult, op1=ALU.mult)
                ins.then_inc(kk_n, 1)

        L2 = at("L2", 0, [P, 2, D])
        DOT = at("DOT", 20, [16, LAT])

        def two(name, a, b, shape):
            return [at(f"{name}{d}", o, shape) for d, o in enumerate((a, b))]

        def temp(name, i):
            return two(name, RB + 64.5 + 2 * i, 8 + 2 * i, [P, 8, L])
        TA, TB, TC, TE, TQ, TK = (temp("TA", 0), temp("TB", 1), temp("TC", 2), temp("TE", 3),
                                  temp("TQ", 4), temp("TK", 5))
        GP = two("GP", RA, RA + 8, [P, 2, 8, 2, L])
        BK = two("BK", RA + 16, RA + 20, [P, 8, 2, L])
        AR = two("AR", RA + 24, RA + 28, [P, 8, 2, L])
        UV = two("UV", RA + 32, RA + 36, [P, 8, 2, L])
        ST = two("ST", RA + 40, RA + 42, [P, 8, L])
        PB = two("PB", RA + 44, RA + 46, [P, 8, L])
        ZZ = two("ZZ", RB + 86.5, RB + 88.5, [P, 8, L])
        XX = two("XX", RB + 90.5, RB + 92.5, [P, 8, L])
        HS = at("HS", RB + 94.5, [P, 2, 2, L])
        RK = at("RK", RB + 95.5, [P, 8, 16])
        PL = at("PL", 52.75, [P, 2, 8])
        OK = at("OK", 52.8125, [P, 8])
        l2_in, sc_init = sem("l2_in"), sem("sc_init")
        pr_hs, pr_lo, pr_x, pr_t, pr_g, pr_e = (sem("pr_hs"), sem("pr_lo"), sem("pr_x"),
                                                sem("pr_t"), sem("pr_g"), sem("pr_e"))
        pr_q, pr_rr, fin, pr_dp, pr_dt = (sem("pr_q"), sem("pr_rr"), sem("fin"), sem("pr_dp"),
                                          sem("pr_dt"))
        gA, gT, eA, eT = sem("gA"), sem("gT"), sem("eA"), sem("eT")
        zi, z0, iX, iP, iC, iZ, iM = (sem("zi"), sem("z0"), sem("iX"), sem("iP"), sem("iC"),
                                      sem("iZ"), sem("iM"))
        sc, ac = sem("sc"), sem("ac")
        cH, rH, cU, uU, cY, yS, cS, sA, sU = (sem("cH"), sem("rH"), sem("cU"), sem("uU"),
                                              sem("cY"), sem("yS"), sem("cS"), sem("sA"),
                                              sem("sU"))
        yO, vI = [sem("yO0"), sem("yO1")], [sem("vI0"), sem("vI1")]
        ROWS = (slice(0, 64), slice(64, 128))
        CC, CL = LC // L, T // L

        def turns(eng, body):
            body(0, "ctx", "ctx")
            with eng.Fori(1, CC - 1) as i:
                body(i, "ctx", "ctx")
            body(CC - 1, "ctx", "lat")
            body(CC, "lat", "lat")
            with eng.Fori(CC + 1, CL - 1) as i:
                body(i, "lat", "lat")
            body(CL - 1, "lat", None)

        def chunk_at(eng, it, kind):
            if kind == "ctx":
                a, b = it * L, it * -L + (LC - L)
            else:
                a, b = it * L, it * -L + (LC + T - L)
            return [a, b] if isinstance(it, int) else [eng.snap(a), eng.snap(b)]

        def in_lat(eng, off):
            return off - LC if isinstance(off, int) else eng.snap(off + -LC)

        def toks(x, off):
            return x[:, :, bass.ds(off, L)]

        def scan_pe(pe):
            pe.wait_ge(l2_in, 16)
            pe.wait_ge(sc_init, 9)
            pe.wait_ge(cm1_in, 16)

            def lora(n):
                pe.wait_ge(pr_hs, n * 2 + 2)
                for j in range(2):
                    o = ps[:, 4 * j + 2:4 * j + 4].rearrange("p a b -> p (a b)")
                    for p in range(8):
                        mm = nc.tensor.matmul(o[:, P * p:P * p + P], L2[:, j, P * p:P * p + P],
                                              HS[:, j].rearrange("p d t -> p (d t)"),
                                              start=True, stop=True)
                mm.then_inc(pr_lo, 1)
            lora(0)

            def body(it, kind, nxt):
                for d in range(2):
                    pe.wait_ge(fin, it * 2 + (d + 1))
                    if kind == "lat" and not (isinstance(it, int) and it == CC):
                        pe.wait_ge(yS, it * 2 + (d - 1 - 2 * CC))
                    for e in range(2):
                        o = ps[:, 4 * d + 2 * e:4 * d + 2 * e + 2].rearrange("p a b -> p (a b)")
                        for p in range(8):
                            mm = nc.tensor.matmul(
                                o[:, P * p:P * p + P],
                                BK[d][ROWS[e], p].rearrange("p a t -> p (a t)"),
                                AR[d][ROWS[e], p].rearrange("p a t -> p (a t)"), start=True,
                                stop=True)
                        mm.then_inc(gA, 1)
                for d in range(2):
                    pe.wait_ge(eA, it * 4 + (2 * d + 1))
                    o = ps[:, 4 * d:4 * d + 2].rearrange("p a b -> p (a b)")
                    for p in range(8):
                        mm = nc.tensor.transpose(o[:, P * p:P * p + P],
                                                 BK[d][:, p].rearrange("p a t -> p (a t)"),
                                                 ident)
                    mm.then_inc(gT, 1)
                if nxt:
                    pe.wait_ge(eA, it * 4 + 4)
                    lora(it + 1)
                for l in range(5):
                    for d in range(2):
                        pe.wait_ge(iX, it * 10 + (2 * l + d + 1))
                        if l == 0:
                            pe.wait_ge(eT, it * 2 + (d + 1))
                        pe.sem_inc(waits_seen)
                        for e in range(2):
                            for p in range(8):
                                mm = nc.tensor.matmul(
                                    ps[ROWS[e], 4 * d, L * p:L * p + L],
                                    GP[d][ROWS[e], e, p, 0], XX[d][ROWS[e], p], start=True,
                                    stop=True)
                        mm.then_inc(iP, 1)
                    for d in range(2):
                        pe.wait_ge(iC, it * 10 + (2 * l + d + 1))
                        pe.sem_inc(waits_seen)
                        for e in range(2):
                            for p in range(8):
                                mm = nc.tensor.matmul(
                                    ps[ROWS[e], 4 * d + 1, L * p:L * p + L],
                                    PB[d][ROWS[e], p], ZZ[d][ROWS[e], p], start=True, stop=True)
                        mm.then_inc(iZ, 1)
                for d in range(2):
                    pe.wait_ge(vI[d], it * 32 + 32)
                    pe.wait_ge(sc, it * 2 + (d + 1))
                    pe.wait_ge(ac, it * 2 + (d + 1))
                    if nxt:
                        pe.wait_ge(pr_x, it * 4 + 8)
                    for e in range(2):
                        for p in range(8):
                            mm = nc.tensor.matmul(ps[ROWS[e], 4 * d + 2, L * p:L * p + L],
                                                  GP[d][:, e, p, 0], UV[d][:, p, e],
                                                  start=True, stop=True)
                    mm.then_inc(cH, 1)
                if nxt == "lat":
                    for d in range(2):
                        pe.wait_ge(pr_rr, it * 2 + (d + 3 - 2 * CC))
                        for p in range(8):
                            mm = nc.tensor.matmul(ps[0:16, 4 * d, 0:L], RK[:, p], TB[d][:, p],
                                                  start=p == 0, stop=p == 7)
                        mm.then_inc(pr_dp, 1)
                for d in range(2):
                    pe.wait_ge(rH, it * 2 + (d + 1))
                    pe.wait_ge(iM, it * 10 + (9 + d))
                    pe.sem_inc(waits_seen)
                    for e in range(2):
                        for p in range(8):
                            mm = nc.tensor.matmul(ps[ROWS[e], 4 * d + 3, L * p:L * p + L],
                                                  ZZ[d][ROWS[e], p], XX[d][ROWS[e], p],
                                                  start=True, stop=True)
                    mm.then_inc(cU, 1)
                for d in range(2):
                    pe.wait_ge(uU, it * 2 + (d + 1))
                    for e in range(2):
                        for p in range(8):
                            mm = nc.tensor.matmul(ps[ROWS[e], 4 * d + 3, L * p:L * p + L],
                                                  BK[d][:, p, e], UV[d][:, p, e], start=True,
                                                  stop=True)
                    mm.then_inc(cS, 1)
                    if kind == "lat":
                        for e in range(2):
                            for p in range(8):
                                o = ps[ROWS[e], 4 * d + 2, L * p:L * p + L]
                                nc.tensor.matmul(o, ST[d][ROWS[e], p], AR[d][ROWS[e], p, 1],
                                                 start=True, stop=False)
                                mm = nc.tensor.matmul(o, UV[d][:, p, e], GP[d][:, e, p, 1],
                                                      start=False, stop=True)
                        mm.then_inc(cY, 1)
            turns(pe, body)

        def scan_act(act):
            act.wait_ge(sc_init, 9)

            def hidden(n, kind):
                if not (isinstance(n, int) and n == 0):
                    act.wait_ge(pr_lo, n)
                off = chunk_at(act, n, kind)
                for d in range(2):
                    nc.scalar.activation(HS[ROWS[d], :, d], H1[ROWS[d], :, bass.ds(off[d], L)],
                                         ACT.Copy).then_inc(pr_hs, 1)

            def tanhs(n, d):
                for j, x in enumerate((TA[d], TB[d])):
                    act.wait_ge(pr_x, n * 4 + (2 * d + j + 1))
                    nc.scalar.activation(x[:], x[:], ACT.Tanh, scale=0.5).then_inc(pr_t, 1)

            def exps(n, d):
                act.wait_ge(pr_g, n * 8 + (4 * d + 4))
                nc.scalar.activation(TE[d][:], TC[d][:], ACT.Exp, scale=-KAPPA).then_inc(pr_e, 1)
                nc.scalar.activation(TA[d][:], TA[d][:], ACT.Exp, scale=-KAPPA).then_inc(pr_e, 1)
                act.wait_ge(pr_e, n * 6 + (3 * d + 1))
                nc.scalar.activation(TC[d][:], TC[d][:], ACT.Exp, scale=KAPPA).then_inc(pr_e, 1)
            hidden(0, "ctx")
            for d in range(2):
                tanhs(0, d)
            for d in range(2):
                exps(0, d)

            def body(it, kind, nxt):
                for d in range(2):
                    if not (isinstance(it, int) and it == 0):
                        act.wait_ge(cU, it * 2 + (d - 1))
                    nc.scalar.activation(ZZ[d][:], c1("eye", 0, L)[:, None, :].broadcast_to(
                        [P, 8, L]), ACT.Copy).then_inc(zi, 1)
                if nxt:
                    hidden(it + 1, nxt)
                for d in range(2):
                    if not (isinstance(it, int) and it == 0):
                        act.wait_ge(sU, it * 2 + (d - 1))
                    for e in range(2):
                        ins = nc.scalar.activation(UV[d][ROWS[e], :, e], ST[d][ROWS[e]],
                                                   ACT.Copy)
                    ins.then_inc(sc, 1)
                for d in range(2):
                    act.wait_ge(gT, it * 2 + (d + 1))
                    nc.scalar.activation(BK[d][:].rearrange("p m a t -> p (m a t)"),
                                         ps[:, 4 * d:4 * d + 2].rearrange("p a b -> p (a b)"),
                                         ACT.Copy).then_inc(eT, 1)
                for l in range(5):
                    for d in range(2):
                        act.wait_ge(iP, it * 10 + (2 * l + d + 1))
                        nc.scalar.activation(PB[d][:].rearrange("p a t -> p (a t)"),
                                             ps[:, 4 * d], ACT.Copy).then_inc(iC, 1)
                        if l == 4:
                            for e in range(2):
                                ins = nc.scalar.activation(GP[d][ROWS[e], e, :, 0],
                                                           AR[d][ROWS[e], :, 0], ACT.Copy)
                            ins.then_inc(ac, 1)
                    if nxt and l == 1:
                        tanhs(it + 1, 0)
                    if nxt and l == 2:
                        exps(it + 1, 0)
                        tanhs(it + 1, 1)
                    if nxt and l == 3:
                        exps(it + 1, 1)
                for d in range(2):
                    act.wait_ge(cH, it * 2 + (d + 1))
                    nc.scalar.activation(XX[d][:].rearrange("p a t -> p (a t)"),
                                         ps[:, 4 * d + 2], ACT.Copy).then_inc(rH, 1)
                for d in range(2):
                    act.wait_ge(cU, it * 2 + (d + 1))
                    act.wait_ge(cH, it * 2 + (d + 1))
                    for e in range(2):
                        ins = nc.scalar.activation(
                            UV[d][ROWS[e], :, e],
                            ps[ROWS[e], 4 * d + 3].rearrange("p (a t) -> p a t", t=L), ACT.Copy)
                    ins.then_inc(uU, 1)
                if kind == "lat":
                    for d in range(2):
                        act.wait_ge(cY, it * 2 + (d + 1 - 2 * CC))
                        nc.scalar.activation(XX[d][:], ps[:, 4 * d + 2].rearrange(
                            "p (a t) -> p a t", t=L), ACT.Copy).then_inc(yS, 1)
            turns(act, body)

        def scan_dve(dve):
            dve.wait_ge(z_out, 16)
            dve.wait_ge(tile_done, T_G + 2)
            dve.wait_ge(cm1_in, 16)
            dve.wait_ge(kk_n, 8)
            nc.vector.memset(DOT[:], 0.0).then_inc(sc_init, 1)
            nc.vector.memset(HS[:], 0.0).then_inc(sc_init, 1)
            for d in range(2):
                nc.vector.memset(ST[d][:], 0.0).then_inc(sc_init, 1)
                nc.vector.memset(AR[d][:, :, 1], 0.0).then_inc(sc_init, 1)
            nc.vector.tensor_tensor(
                RK[:], c1("hsel", 0, P).rearrange("p (m h) -> p m h", m=8),
                vec("r_k", 0, 8)[:, :, None].broadcast_to([P, 8, 16]), ALU.mult
                ).then_inc(sc_init, 1)
            nc.vector.memset(PL[:], 0.0).then_inc(sc_init, 1)
            nc.vector.tensor_scalar(OK[:], vec("k_a", 0, 8), -1.0, 1.0, ALU.mult, ALU.add
                                    ).then_inc(sc_init, 1)

            def fl(x):
                return x.rearrange("p a t -> p (a t)")

            def rates(n, d, kind):
                dve.wait_ge(pr_lo, n + 1)
                if not (isinstance(n, int) and n == 0):
                    dve.wait_ge(fin, n * 2 + (d - 1))
                if kind == "lat" and not (isinstance(n, int) and n == CC):
                    dve.wait_ge(pr_dp, n * 2 + (d - 1 - 2 * CC))
                for j, (x, w) in enumerate(((TA[d], "w0"), (TB[d], "a0"))):
                    o = ps[:, 4 * j + 2:4 * j + 4].rearrange("p a (m c t) -> p (a m) c t", c=2,
                                                             t=L)
                    nc.vector.tensor_tensor(
                        x[:], o[:, :, d],
                        vec(w, 8 * d, 8)[:, :, None].broadcast_to([P, 8, L]), ALU.add
                        ).then_inc(pr_x, 1)

            def sums(n, d):
                for j, x in enumerate((TA[d], TB[d])):
                    dve.wait_ge(pr_t, n * 4 + (2 * d + j + 1))
                    nc.vector.tensor_scalar(x[:], x[:], 0.5, 0.5, ALU.mult, ALU.add
                                            ).then_inc(pr_g, 1)
                dve.wait_ge(pr_g, n * 8 + (4 * d + 2))
                step = 1 if d == 0 else -1
                nc.vector.tensor_tensor_scan(fl(TC[d][:])[:, ::step], c1("reset", 0, 512),
                                             fl(TA[d][:])[:, ::step], 0.0, ALU.mult, ALU.add
                                             ).then_inc(pr_g, 1)
                dve.wait_ge(pr_g, n * 8 + (4 * d + 3))
                nc.vector.tensor_tensor(TA[d][:], TC[d][:], TA[d][:], ALU.subtract
                                        ).then_inc(pr_g, 1)

            def factors(n, d, kind):
                off = chunk_at(dve, n, kind)[d]
                dve.wait_ge(pr_e, n * 6 + (3 * d + 3))
                if not (isinstance(n, int) and n == 0):
                    dve.wait_ge(cS, n * 2 + (d - 1))
                    dve.wait_ge(sU, n * 2 + (d - 1))
                if kind == "lat" and not (isinstance(n, int) and n == CC):
                    dve.wait_ge(cY, n * 2 + (d - 1 - 2 * CC))
                nc.vector.scalar_tensor_tensor(out=AR[d][:, :, 0], in0=toks(KN, off),
                                               scalar=-1.0, in1=TA[d][:], op0=ALU.mult,
                                               op1=ALU.mult)
                nc.vector.tensor_copy(PL[:, d], TE[d][:, :, L - 1 if d == 0 else 0])
                if kind == "lat":
                    nc.vector.tensor_tensor(AR[d][:, :, 1], toks(RR, in_lat(dve, off)), TE[d][:],
                                            ALU.mult)
                dve.wait_ge(pr_q, n * 8 + (4 * d + 4))
                for e in range(2):
                    nc.vector.tensor_tensor(BK[d][ROWS[e], :, e], TK[d][ROWS[e]],
                                            TC[d][ROWS[e]], ALU.mult)
                    ins = nc.vector.tensor_tensor(BK[d][ROWS[e], :, 1 - e], TQ[d][ROWS[e]],
                                                  TC[d][ROWS[e]], ALU.mult)
                ins.then_inc(fin, 1)

            def dots(n, kind):
                off = chunk_at(dve, n, kind)
                for d in range(2):
                    dve.wait_ge(pr_dp, n * 2 + (d + 1 - 2 * CC))
                    dv = DOT[:, bass.ds(in_lat(dve, off[d]), L)]
                    if not (isinstance(n, int) and n == CC and d == 0):
                        dve.wait_ge(pr_dt, n * 2 + (d - 2 * CC))
                    nc.vector.tensor_tensor(dv, dv, ps[0:16, 4 * d, 0:L], ALU.add
                                            ).then_inc(pr_dt, 1)
            dve.wait_ge(sc_init, 9)
            for d in range(2):
                rates(0, d, "ctx")
            for d in range(2):
                sums(0, d)
            for d in range(2):
                factors(0, d, "ctx")

            def body(it, kind, nxt):
                for d in range(2):
                    for e in range(2):
                        dve.wait_ge(gA, it * 4 + (2 * d + e + 1))
                        nc.vector.tensor_tensor(
                            GP[d][:, e].rearrange("p m a t -> p m (a t)"),
                            ps[:, 4 * d + 2 * e:4 * d + 2 * e + 2].rearrange(
                                "p a (m t) -> p (a m) t", t=P),
                            c1("tri", P * d, P)[:, None, :].broadcast_to([P, 8, P]), ALU.mult
                            ).then_inc(eA, 1)

                def lvl(d, l, r=slice(0, P)):
                    m = c1("lvl", L * (6 * d + l), L)[r].bitcast(U32)
                    return m[:, None, :].broadcast_to([m.shape[0], 8, L])

                def turn(d, l):
                    nc.vector.transpose(fl(XX[d][:]), fl(ZZ[d][:])).then_inc(iX, 1)
                for d in range(2):
                    dve.wait_ge(zi, it * 2 + (d + 1))
                    dve.wait_ge(eA, it * 4 + (2 * d + 2))
                    dve.sem_inc(waits_seen)
                    for e in range(2):
                        ins = nc.vector.copy_predicated(ZZ[d][ROWS[e]], lvl(d, 0, ROWS[e]),
                                                        GP[d][ROWS[e], e, :, 0])
                    ins.then_inc(z0, 1)
                    dve.wait_ge(z0, it * 2 + (d + 1))
                    if not (isinstance(it, int) and it == 0):
                        dve.wait_ge(cU, it * 2 + (d - 1))
                    if kind == "lat" and not (isinstance(it, int) and it == CC):
                        dve.wait_ge(yO[d], it * 16 + -16 * CC)
                    turn(d, 0)
                for l in range(5):
                    for d in range(2):
                        dve.wait_ge(iZ, it * 10 + (2 * l + d + 1))
                        dve.sem_inc(waits_seen)
                        nc.vector.copy_predicated(
                            ZZ[d][:], lvl(d, l + 1),
                            ps[:, 4 * d + 1].rearrange("p (a t) -> p a t", t=L)
                            ).then_inc(iM, 1)
                        if l < 4:
                            dve.wait_ge(iM, it * 10 + (2 * l + d + 1))
                            turn(d, l + 1)
                    if nxt and l == 0:
                        rates(it + 1, 0, nxt)
                    if nxt and l == 1:
                        sums(it + 1, 0)
                        rates(it + 1, 1, nxt)
                    if nxt and l == 2:
                        sums(it + 1, 1)
                if nxt == "lat":
                    dots(it + 1, nxt)
                for d in range(2):
                    dve.wait_ge(cS, it * 2 + (d + 1))
                    if kind == "lat":
                        dve.wait_ge(cY, it * 2 + (d + 1 - 2 * CC))
                    nc.vector.tensor_tensor(ST[d][:], ST[d][:], ps[:, 4 * d + 3].rearrange(
                        "p (a t) -> p a t", t=L), ALU.add).then_inc(sA, 1)
                    dve.wait_ge(sA, it * 2 + (d + 1))
                    nc.vector.tensor_tensor(ST[d][:], ST[d][:], PL[:, d][:, :, None
                                            ].broadcast_to([P, 8, L]), ALU.mult
                                            ).then_inc(sU, 1)
                    if nxt:
                        factors(it + 1, d, nxt)
            turns(dve, body)

        def scan_pool(pool):
            pool.wait_ge(z_out, 16)
            pool.dma_start(L2[:], lora2).then_inc(l2_in, 16)
            pool.wait_ge(sc_init, 9)

            def keys(n, kind):
                off = chunk_at(pool, n, kind)
                for d in range(2):
                    pool.wait_ge(pr_g, n * 8 + (4 * d + 2))
                    nc.gpsimd.tensor_tensor(TQ[d][:], TB[d][:], vec("k_a", 0, 8)[:, :, None
                                            ].broadcast_to([P, 8, L]), ALU.mult
                                            ).then_inc(pr_q, 1)
                    nc.gpsimd.tensor_tensor(TK[d][:], toks(KN, off[d]), TB[d][:], ALU.mult
                                            ).then_inc(pr_q, 1)
                    pool.wait_ge(pr_q, n * 8 + (4 * d + 1))
                    nc.gpsimd.tensor_tensor(TQ[d][:], TQ[d][:], OK[:][:, :, None].broadcast_to(
                        [P, 8, L]), ALU.add).then_inc(pr_q, 1)
                    pool.wait_ge(pr_q, n * 8 + (4 * d + 3))
                    nc.gpsimd.tensor_tensor(TQ[d][:], TQ[d][:], toks(KK_, off[d]), ALU.mult
                                            ).then_inc(pr_q, 1)
                    if kind == "lat":
                        pool.wait_ge(pr_q, n * 8 + (4 * d + 4))
                        nc.gpsimd.tensor_tensor(TB[d][:], TQ[d][:],
                                                toks(RR, in_lat(pool, off[d])), ALU.mult
                                                ).then_inc(pr_rr, 1)
            keys(0, "ctx")
            turns(pool, lambda it, kind, nxt: keys(it + 1, nxt) if nxt else None)

        def scan_sync(sp):
            for b in range(2):
                sp.wait_ge(vk_out[b], 64)
            sp.wait_ge(sc_init, 9)
            vk = vk_dram.rearrange("t (m e n) -> t m e n", e=2, n=L)

            def body(it, kind, nxt):
                off = chunk_at(sp, it, kind)
                if kind == "lat":
                    loff = [in_lat(sp, o) for o in off]
                for d in range(2):
                    if kind == "lat" and not (isinstance(it, int) and it == CC):
                        sp.wait_ge(cY, it * 2 + (d - 1 - 2 * CC))
                    elif not (isinstance(it, int) and it == 0):
                        sp.wait_ge(cS, it * 2 + (d - 1))
                    for e in range(2):
                        sp.dma_start(UV[d][ROWS[1 - e], :, e], vk[bass.ds(off[d], L), :, e]
                                     ).then_inc(vI[d], 16)
                if kind == "lat":
                    for d in range(2):
                        sp.wait_ge(yS, it * 2 + (d + 1 - 2 * CC))
                        sp.dma_start(y_dram[d][:, :, bass.ds(loff[d], L)], XX[d][:]
                                     ).then_inc(yO[d], 16)
            turns(sp, body)

        YC = at("YC", RB, [P, KT, LAT])
        HB = at("HB", RB + 16, [16, D])
        YQ = at("YQ", RB + 20, [P, 2, LAT])
        YD = at("YD", RB + 26, [16, LAT])
        YR = at("YR", RB + 28, [16, LAT])
        YB = at("YB", RB + 30, [P, 2, LAT])
        YT = at("YT", RB + 34, [P, 2, LAT])
        G2 = at("G2", RB + 40.5, [P, 2, D])
        YA = at("YA", RB + 48.5, [P, 2, 2, LAT])
        YV = at("YV", RB + 56.5, [P, 2, LAT])
        g2_in, y_in, v_in, z_in = (sem("g2_in"), [sem("y_in0"), sem("y_in1")],
                                   [sem("v_in0"), sem("v_in1")], sem("z_in"))
        po_s, po_m, po_c, po_q, po_v, po_d = (sem("po_s"), sem("po_m"), sem("po_c"),
                                              sem("po_q"), sem("po_v"), sem("po_d"))
        po_p, po_t, po_y, po_hi, po_lo = (sem("po_p"), sem("po_t"), sem("po_y"), sem("po_hi"),
                                          sem("po_lo"))

        def post_sync(sp):
            for d in range(2):
                sp.wait_ge(yO[d], 128)
            sp.wait_ge(sU, 24)
            for m in range(8):
                if m >= 2:
                    sp.wait_ge(po_s, m - 1)
                for d in range(2):
                    sp.dma_start(YA[:, m % 2, d], y_dram[d][:, m]).then_inc(y_in[m % 2], 16)
            sp.wait_ge(vt_out, 16)
            for m in range(8):
                if m >= 2:
                    sp.wait_ge(po_t, 3 * m - 4)
                sp.dma_start(YV[:, m % 2], vt_dram[:, m]).then_inc(v_in[m % 2], 16)

        def post_pool(pool):
            pool.wait_ge(sU, 24)
            pool.wait_ge(pr_dt, 16)
            pool.dma_start(G2[:], g2w).then_inc(g2_in, 16)
            pool.dma_start(HB[:], cm1[0:16, C1OFF["hbc"]:C1OFF["hbc"] + D]).then_inc(g2_in, 16)
            pool.wait_ge(po_lo, 8)
            pool.dma_start(z[:, :, LC:T], z_dram).then_inc(z_in, 16)

        def post_pe(pe):
            for m in range(9):
                if m < 8:
                    pe.wait_ge(po_s, m + 1)
                    if m >= 2:
                        pe.wait_ge(po_c, m - 1)
                    nc.tensor.matmul(ps[:, 4 + m % 2], bd, YC[:, m], start=True, stop=True
                                     ).then_inc(po_m, 1)
                if m:
                    pe.wait_ge(po_q, m)
                    nc.tensor.matmul(ps[0:16, 6], c1("hsel", 16 * (m - 1), 16),
                                     YQ[:, (m - 1) % 2], start=m == 1, stop=m == 8
                                     ).then_inc(po_v, 1)
            pe.wait_ge(g2_in, 32)
            pe.wait_ge(kk_n, 8)
            for m in range(8):
                b = 4 * (m % 2)
                if m >= 2:
                    pe.wait_ge(po_y, m - 1)
                elif m == 1:
                    pe.wait_ge(po_d, 1)
                for i in range(2):
                    nc.tensor.matmul(ps[:, b + 2], G2[:, i, P * m:P * m + P], G1[:, i],
                                     start=i == 0, stop=i == 1)
                nc.tensor.matmul(ps[:, b + 1], HB[:, P * m:P * m + P], DOT[:], start=True,
                                 stop=True)
                if m == 0:
                    pe.wait_ge(po_d, 2)
                nc.tensor.matmul(ps[:, b], HB[:, P * m:P * m + P], YR[:], start=True,
                                 stop=True).then_inc(po_p, 1)

        def post_act(act):
            for m in range(8):
                act.wait_ge(po_c, m + 1)
                if m >= 2:
                    act.wait_ge(po_v, m - 1)
                nc.scalar.activation(YQ[:, m % 2], YC[:, m], ACT.Square).then_inc(po_q, 1)
            act.wait_ge(po_v, 8)
            nc.scalar.activation(YD[:], ps[0:16, 6], ACT.Sqrt, bias=CO[0:16, 65:66],
                                 scale=1.0 / L).then_inc(po_d, 1)
            for m in range(8):
                act.wait_ge(po_y, m + 1)
                nc.scalar.activation(XH[:, m, LC:T], YT[:, m % 2], ACT.Copy).then_inc(po_hi, 1)

        def post_dve(dve):
            for m in range(9):
                if m < 8:
                    dve.wait_ge(y_in[m % 2], 32 * (m // 2 + 1))
                    nc.vector.tensor_tensor(YC[:, m], YA[:, m % 2, 0], YA[:, m % 2, 1], ALU.add
                                            ).then_inc(po_s, 1)
                if m:
                    dve.wait_ge(po_m, m)
                    nc.vector.scalar_tensor_tensor(
                        out=YC[:, m - 1], in0=ps[:, 4 + (m - 1) % 2], scalar=-1.0 / L,
                        in1=YC[:, m - 1], op0=ALU.mult, op1=ALU.add).then_inc(po_c, 1)
            dve.wait_ge(po_d, 1)
            nc.vector.reciprocal(YR[:], YD[:]).then_inc(po_d, 1)
            for m in range(8):
                b = 4 * (m % 2)
                yt, yb = YT[:, m % 2], YB[:, m % 2]
                if m >= 2:
                    dve.wait_ge(po_hi, m - 1)
                    dve.wait_ge(po_lo, m - 1)
                dve.wait_ge(po_p, m + 1)
                dve.wait_ge(v_in[m % 2], 16 * (m // 2 + 1))
                nc.vector.scalar_tensor_tensor(out=yt, in0=YC[:, m], scalar=vec("ln_g", m),
                                               in1=ps[:, b], op0=ALU.mult, op1=ALU.mult
                                               ).then_inc(po_t, 1)
                nc.vector.tensor_tensor(yb, ps[:, b + 1], YV[:, m % 2], ALU.mult
                                        ).then_inc(po_t, 1)
                dve.wait_ge(po_t, 3 * m + 2)
                nc.vector.scalar_tensor_tensor(out=yt, in0=yt, scalar=vec("ln_b", m), in1=yb,
                                               op0=ALU.add, op1=ALU.add).then_inc(po_t, 1)
                dve.wait_ge(po_t, 3 * m + 3)
                nc.vector.tensor_tensor(yt, ps[:, b + 2], yt, ALU.mult).then_inc(po_y, 1)
                if m:
                    low_part(dve, m - 1)
            low_part(dve, 7)

        def low_part(dve, m):
            dve.wait_ge(po_hi, m + 1)
            nc.vector.tensor_tensor(XL[:, m, LC:T], YT[:, m % 2], XH[:, m, LC:T].bitcast(F32),
                                    ALU.subtract).then_inc(po_lo, 1)

        block = ctx.enter_context(nc.Block())

        @block.sync
        def _(sp):
            sp.dma_start(PV[:], pv).then_inc(consts_in, 16)
            sp.dma_start(CM[:], cm).then_inc(consts_in, 16)
            ada_sync(sp, 0, 8)
            sp.dma_start(z[:], zin).then_inc(consts_in, 16)
            for t in range(2):
                sp.dma_start(WR[:, t], wall[t]).then_inc(w_in[t % 2], 16)
            ada_sync(sp, 8, 48)
            load_weights(sp)
            sp.wait_ge(acc_lat, NT)
            sp.dma_start(out, z[:, :, LC:T]).then_inc(out_done, 16)
            sp.wait_ge(out_done, 16)

        @block.gpsimd
        def _(pool):
            pool.dma_start(NSEL[:], cm0[:, C0OFF["nsel"]:C0OFF["nbc"]]).then_inc(cm0_in, 16)
            pool.dma_start(NBC[:], cm0[0:16, C0OFF["nbc"]:NC0]).then_inc(cm0_in, 16)
            ada_pool(pool, 0)
            norm_pool(pool, 0, 0)
            ada_pool(pool, 1)
            pool.dma_start(CM0[:], cm0[:, 0:C0OFF["nsel"]]).then_inc(cm0_in, 16)
            hn_pool(pool)
            attn_pool(pool)
            norm_pool(pool, 1, 8)
            for q in range(6):
                mix_pool(pool, q)
                if q == 0:
                    vk_pool(pool)
            pool.wait_ge(x_lo, 64)
            pool.dma_start(HK[:], cm1[0:16, C1OFF["hbc"]:C1OFF["hbc"] + D]
                           ).then_inc(cm1_in, 16)
            scan_pool(pool)
            post_pool(pool)
            norm_pool(pool, 3, 64)

        @block.tensor
        def _(pe):
            pe.wait_ge(consts_in, 32)
            ada_pe(pe, 0, 32)
            mod_pe(pe, 0)
            norm_pe(pe, 0, SEGS)
            ada_pe(pe, 32, 48)
            gemm_pe(pe, T_IN, N_IN, SEGS, 0, XH, XL, paced=(x_lo, 0))
            ml_gates_pe(pe)
            ml_pe(pe)
            hn_pe(pe)
            attn_pe(pe)
            gemm_pe(pe, T_OUT0, 8, SEGS, T_OUT0, XH, XL, x_wait=(at_lo, 6))
            norm_pe(pe, 1, SEGS)
            mod_pe(pe, 1)
            mlp(pe, "pe", 0, T_MLP0, SEGS, T_MLP0, (x_lo, 8))
            norm_pe(pe, 2, SEGS)
            for q, (i, t0, n, segs) in enumerate(MIXES):
                gemm_pe(pe, t0, n, segs, t0, XH, XL, paced=(x_lo, 16 + 8 * q))
                if q == 0:
                    vk_pe(pe)
            kk_pe(pe)
            scan_pe(pe)
            post_pe(pe)
            gemm_pe(pe, T_OUT1, 8, (LATS,), 0, XH, XL, x_wait=(po_lo, 8))
            norm_pe(pe, 3, (LATS,))
            mlp(pe, "pe", 1, T_MLP1, (LATS,), 0, (x_lo, 64))

        @block.scalar
        def _(act):
            silu_act(act)
            with act.Fori(0, 12) as i:
                for s in range(2):
                    ada_act(act, 0, i * 2 + s, s)
            split_hi(0, 0, 0)
            split_hi(1, 0, 1)
            norm_act(act, 0, SEGS, [(consts_in, 48)], True)
            act.wait_ge(mod_out, 32)
            step_act(act, T_IN, N_IN, in_act)
            ml_gates_act(act)
            ml_act(act)
            hn_act(act)
            attn_act(act)
            step_act(act, T_OUT0, 8, last_act(1, NZ[1]), peel=8)
            norm_act(act, 1, SEGS, NZ[1], True)
            mlp(act, "act", 0, T_MLP0, SEGS, T_MLP0, None)
            norm_act(act, 2, SEGS, NZ[2], False)
            for q, (i, t0, n, segs) in enumerate(MIXES):
                if q == 1:
                    vk_act(act)
                mix_act(act, q)
                if q == 1:
                    act.wait_ge(vt_out, 16)
                    act.wait_ge(vk_t, 8)
                step_act(act, t0, n, mix_evict(q, "act"))
            kk_act(act)
            scan_act(act)
            post_act(act)
            step_act(act, T_OUT1, 8, last_act(3, NZ[3]), peel=8)
            norm_act(act, 3, (LATS,), NZ[3], True)
            mlp(act, "act", 1, T_MLP1, (LATS,), 0, None)

        @block.vector
        def _(dve):
            silu_dve(dve)
            split_lo(0, 0, 0)
            split_lo(1, 0, 1)
            norm_dve(dve, 0, SEGS, [(consts_in, 48)], 0, True)
            dve.wait_ge(mod_out, 32)
            step_dve(dve, T_IN, N_IN, in_dve)
            ml_gates_dve(dve)
            ml_dve(dve)
            hn_dve(dve)
            attn_dve(dve)
            step_dve(dve, T_OUT0, 8, last_dve(1, res_dve(0, 2, SEGS)), peel=8)
            norm_dve(dve, 1, SEGS, NZ[1], 8, True)
            mod_dve(dve, 1)
            mlp(dve, "dve", 0, T_MLP0, SEGS, T_MLP0, None)
            norm_dve(dve, 2, SEGS, NZ[2], 16, False)
            mu = vec("mu", 0, 96).rearrange("p (i s k) -> p i s k", i=6, s=2)
            nc.vector.scalar_tensor_tensor(out=MC[:], in0=mu[:, :, 0], scalar=-1.0,
                                           in1=mu[:, :, 1], op0=ALU.mult, op1=ALU.subtract
                                           ).then_inc(mc_ready, 1)
            dve.wait_ge(mc_ready, 1)
            nc.vector.tensor_scalar(MC[:], MC[:], 1.0, None, ALU.add).then_inc(mc_ready, 1)
            for q, (i, t0, n, segs) in enumerate(MIXES):
                mix_dve(dve, q)
                if q == 1:
                    dve.wait_ge(vt_out, 16)
                    dve.wait_ge(vk_t, 8)
                step_dve(dve, t0, n, mix_evict(q, "dve"))
            kk_dve(dve)
            scan_dve(dve)
            post_dve(dve)
            dve.wait_ge(z_in, 16)
            step_dve(dve, T_OUT1, 8, last_dve(3, res_dve(1, 2, (LATS,))), peel=8)
            norm_dve(dve, 3, (LATS,), NZ[3], 64, True)
            mlp(dve, "dve", 1, T_MLP1, (LATS,), 0, None)


def _tiles(w):
    return w.reshape(KT, P, -1, P).transpose(2, 1, 0, 3)


def _cols(v):
    v = v.reshape(-1, P)
    return v.T


GATE_ROWS = np.concatenate([np.arange(4) + r for r in (0, 32, 64, 96)])
GATE_COLS = np.concatenate([np.arange(4) + g for g in (0, 8, 4, 12)])


def pack(a):
    f = np.float32
    a = {k: np.ascontiguousarray(v) for k, v in a.items()}
    zz = np.concatenate([a["ctx"][0], a["x"][0]], 0)
    zin = zz.T.reshape(KT, P, T).transpose(1, 0, 2)
    wi = a["ev_w_in"][0]
    bi = a["ev_b_in"][0]
    gw = np.zeros((D, P), f)
    gb = np.zeros((P,), f)
    gw[:, GATE_ROWS] = wi[:, 2048 + GATE_COLS]
    gb[GATE_ROWS] = bi[2048 + GATE_COLS]
    fb = np.zeros((P,), f)
    fb[[64, 65, 66, 67]] = a["ml_f_bias"][0, 0]
    fb[[96, 97, 98, 99]] = a["ml_f_bias"][0, 1]
    w_in = np.concatenate([wi[:, :2048], gw, wi[:, 2064:]], 1)
    b_in = np.concatenate([bi[:2048], gb, bi[2064:]])

    def mlp(layer):
        w1, w2 = _tiles(a["mlp_w1"][layer]), a["mlp_w2"][layer]
        return [x for g in range(4) for x in (w1[8 * g:8 * g + 8], _tiles(w2[D * g:D * g + D]))]
    g1 = np.concatenate([a["rw_g1"][0], np.zeros((D, 256 - 160), f)], 1)
    rkv = a["rw_w_rkv"][0]
    wall = np.concatenate(
        [_tiles(w_in), _tiles(a["ev_w_out"][0]), *mlp(0), _tiles(rkv[2]), _tiles(rkv[1]),
         _tiles(np.concatenate([a["rw_w1"][0, 0], a["rw_w1"][0, 1]], 1)),
         _tiles(np.concatenate([a["rw_a1"][0, 0], a["rw_a1"][0, 1]], 1)), _tiles(rkv[0]),
         _tiles(g1), _tiles(a["rw_w_out"][0]), *mlp(1)], 0)
    ada = np.concatenate([_tiles(a["ada_w"][0]), _tiles(a["ada_w"][1])], 0)
    cc = np.stack([a["c_ctx"], a["c"][0]], 0).reshape(2, KT, P).transpose(2, 1, 0).reshape(P, 16)
    pv = np.concatenate(
        [cc, _cols(a["ada_b"]), _cols(a["norm1_g"]), _cols(a["norm2_g"]), _cols(b_in),
         fb[:, None], _cols(a["ml_out_g"][0]), np.tile(a["at_q_g"][0], 2)[:, None],
         np.tile(a["at_k_g"][0], 2)[:, None], np.broadcast_to(a["at_sink"][0], (P, 8)),
         _cols(a["rw_mu"][0]), _cols(a["rw_w0"][0]), _cols(a["rw_a0"][0]), _cols(a["rw_k_k"][0]),
         _cols(a["rw_k_a"][0]), _cols(a["rw_r_k"][0]), _cols(a["rw_ln_g"][0]),
         _cols(a["rw_ln_b"][0])], 1)
    lora2 = np.stack([a["rw_w2"][0].reshape(P, D), a["rw_a2"][0].reshape(P, D)], 1)
    g2 = np.zeros((P, 2, D), f)
    g2[:, 0] = a["rw_g2"][0, :P]
    g2[:160 - P, 1] = a["rw_g2"][0, P:]
    return dict(zin=zin, wall=wall, ada=ada, pv=pv, lora2=lora2, g2w=g2, **tables())


def tables():
    f = np.float32
    i = np.arange(P)
    cm = np.concatenate([np.eye(P), np.ones((P, P)), (i[:, None] // 64 == i[None] // 64)], 1)
    perm = np.zeros((P, P))
    for m in range(P):
        if m % 32 < 16:
            perm[m + 16, m] = -1.0
        else:
            perm[m - 16, m] = 1.0
    neg = np.concatenate([np.where(i[:, None] <= i[None], 0, NEG),
                          np.where(i[:, None] >= i[None], 0, NEG)], 1)
    inv = (10000.0 ** (-np.arange(16, dtype=f) / f(16))).astype(f)
    t = np.arange(LAT)
    pos = np.where((i[:, None] % 64) < 32, (t // 64)[None], (t % 64)[None]).astype(f)
    ang = (pos * inv[i % 16][:, None]).astype(f)
    sel = np.zeros((P, 8, P))
    for d in range(2):
        for h in range(4):
            sel[32 * d + h, 4 * d + h] = 1
    reset = np.broadcast_to(np.arange(T) % P != 0, (P, T))
    nsel, nbc = np.zeros((P, 9, 16)), np.zeros((P, 9, P))
    for m in range(5):
        for e in range(2):
            nsel[64 * e:64 * e + 64, m, 2 * m + e] = 1 / 64
            nbc[2 * m + e, m, 64 * e:64 * e + 64] = 1
    for h in range(4):
        nsel[:, 5 + h, 10 + h] = 1 / P
        nbc[10 + h, 5 + h] = 1
    cm0 = np.concatenate([perm, neg, np.cos(ang), np.sin(ang), sel.reshape(P, -1), reset,
                          nsel.reshape(P, -1), nbc.reshape(P, -1)], 1)
    j, r = np.arange(64), (i % 64)[:, None]
    lvl = [[], []]
    for s in (1, 2, 4, 8, 16, 32):
        pair = r // (2 * s) == j[None] // (2 * s)
        low, high = r % (2 * s) < s, j[None] % (2 * s) >= s
        lvl[0].append(pair & low & high)
        lvl[1].append(pair & ~low & ~high)
    hsel = np.zeros((P, 8, 16))
    hbc = np.zeros((P, 8, P))
    for p in range(8):
        for e in range(2):
            hsel[64 * e:64 * e + 64, p, 2 * p + e] = 1
            hbc[2 * p + e, p, 64 * e:64 * e + 64] = 1
    j = j[None]
    cm1 = np.concatenate([r < j, r <= j, r > j, r >= j, *lvl[0], *lvl[1], r == j,
                          np.broadcast_to(np.arange(512) % 64 != 0, (P, 512)),
                          hsel.reshape(P, -1), hbc.reshape(P, -1)], 1)
    return {"cm": cm.astype(f), "cm0": cm0.astype(f), "cm1": cm1.astype(f)}


SCRATCH = [("z_dram", (P, KT, LAT)), ("vt_dram", (P, KT, LAT)), ("vk_dram", (T, D)),
           ("y_dram", (2, P, KT, LAT)), ("mod_dram", (2, 2, 6 * D))]


def kernel(**inputs):
    import concourse.bacc as _bacc
    from concourse.bass_utils import run_bass_kernel_spmd as _run

    packed = {k: np.ascontiguousarray(v, dtype=np.float32)
              for k, v in pack({k: np.asarray(v) for k, v in inputs.items()}).items()}
    nc = _bacc.Bacc("TRN2", target_bir_lowering=False, num_devices=1)
    dram = {k: nc.dram_tensor(f"{k}_dram", v.shape, F32, kind="ExternalInput").ap()
            for k, v in packed.items()}
    scratch = {k: nc.dram_tensor(k, shape, F32, kind="Internal").ap() for k, shape in SCRATCH}
    out = nc.dram_tensor("out_dram", (P, KT, LAT), F32, kind="ExternalOutput").ap()
    trunk(nc, out=out, **dram, **scratch)
    r = _run(nc, [{f"{k}_dram": v for k, v in packed.items()}], core_ids=[0])
    y = r.results[0]["out_dram"]
    return np.ascontiguousarray(y.transpose(2, 1, 0)).reshape(1, LAT, D)
```
